# Optimizing a Trainium2 kernel written in Bass

```python
import numpy as np
import jax
import jax.numpy as jnp
from jax import lax

D_MODEL = 1024
BATCH = 1
SEQ = 256
DEPTH = 2

ROPE_THETA = 10000.0
NORM_EPS = 1e-6
NEG_INF = -1e30
TINY = 1e-30
D_FF = 2816
Q_BLOCK = 128

MLA_HEADS = 8
MLA_NOPE = 64
MLA_ROPE = 32
MLA_V = 64
MLA_Q_LORA = 256
MLA_KV_LORA = 128

GLA_HEADS = 4
GLA_DK = 64
GLA_DV = 128
GLA_GATE_RANK = 16
GLA_GATE_TAU = 16.0
GLA_CHUNK = 64

NSA_HEADS = 16
NSA_KV_GROUPS = 4
NSA_HEAD_DIM = 64
NSA_CMP_LEN = 32
NSA_CMP_STRIDE = 16
NSA_CMP_HIDDEN = 128
NSA_SEL_LEN = 64
NSA_TOP_N = 16
NSA_WINDOW = 512
NSA_Q_BLOCK = 64
NSA_FORCE_SCORE = 1e4

HY_SPLITS = (MLA_Q_LORA, MLA_KV_LORA, MLA_ROPE, GLA_HEADS * GLA_DK, GLA_HEADS * GLA_DK,
             GLA_HEADS * GLA_DV, GLA_GATE_RANK, GLA_HEADS * GLA_DV)
HY_IN = sum(HY_SPLITS)
HY_OUT = MLA_HEADS * MLA_V + GLA_HEADS * GLA_DV
NSA_KV_WIDTH = NSA_KV_GROUPS * NSA_HEAD_DIM
NSA_SPLITS = (NSA_HEADS * NSA_HEAD_DIM,) + (NSA_KV_WIDTH,) * 6 + (NSA_HEADS * 3,)
NSA_IN = sum(NSA_SPLITS)
NSA_OUT = NSA_HEADS * NSA_HEAD_DIM
N_EVEN = (DEPTH + 1) // 2
N_ODD = DEPTH // 2


def split_cols(h, sizes):
    return jnp.split(h, np.cumsum(sizes)[:-1].tolist(), axis=-1)

def rms_norm(x, g):
    xf = x.astype(jnp.float32)
    y = xf * lax.rsqrt(jnp.mean(xf * xf, axis=-1, keepdims=True) + NORM_EPS)
    return (y * g.astype(jnp.float32)).astype(x.dtype)

def rope(x, pos):
    d = x.shape[-1]
    inv_freq = jnp.power(ROPE_THETA, -jnp.arange(d // 2, dtype=jnp.float32) * (2.0 / d))
    ang = pos.astype(jnp.float32)[..., None] * inv_freq
    cos = jnp.cos(ang)[:, :, None, :]
    sin = jnp.sin(ang)[:, :, None, :]
    xf = x.astype(jnp.float32)
    x1, x2 = xf[..., : d // 2], xf[..., d // 2:]
    return jnp.concatenate([x1 * cos - x2 * sin, x2 * cos + x1 * sin], axis=-1).astype(x.dtype)

def masked_softmax(s, mask):
    s = jnp.where(mask, s.astype(jnp.float32), NEG_INF)
    m = jnp.max(s, axis=-1, keepdims=True)
    p = jnp.where(mask, jnp.exp(s - m), 0.0)
    return p / jnp.maximum(jnp.sum(p, axis=-1, keepdims=True), TINY)

def swiglu(x, w_gate, w_up, w_down):
    return (jax.nn.silu(x @ w_gate) * (x @ w_up)) @ w_down

def causal_block_attention(q, k, v, scale):
    B, S, H, Dk = q.shape
    nb = S // Q_BLOCK
    q_blocks = q.reshape(B, nb, Q_BLOCK, H, Dk).transpose(1, 0, 2, 3, 4)
    key_pos = jnp.arange(S)

    def one_block(args):
        i, qb = args
        s = jnp.einsum('bqhd,bkhd->bhqk', qb, k, preferred_element_type=jnp.float32) * scale
        q_pos = i * Q_BLOCK + jnp.arange(Q_BLOCK)
        p = masked_softmax(s, key_pos[None, :] <= q_pos[:, None])
        return jnp.einsum('bhqk,bkhd->bqhd', p.astype(v.dtype), v)

    out = lax.map(one_block, (jnp.arange(nb), q_blocks))
    return out.transpose(1, 0, 2, 3, 4).reshape(B, S, H, v.shape[-1])

def mla_heads(c_q, c_kv, k_r, positions, q_norm, w_uq, kv_norm, w_ukv):
    B, S, _ = c_q.shape
    q = (rms_norm(c_q, q_norm) @ w_uq).reshape(B, S, MLA_HEADS, MLA_NOPE + MLA_ROPE)
    q_nope, q_rot = q[..., :MLA_NOPE], rope(q[..., MLA_NOPE:], positions)
    kv = (rms_norm(c_kv, kv_norm) @ w_ukv).reshape(B, S, MLA_HEADS, MLA_NOPE + MLA_V)
    k_nope, v = kv[..., :MLA_NOPE], kv[..., MLA_NOPE:]
    k_rot = rope(k_r.reshape(B, S, 1, MLA_ROPE), positions)
    q_full = jnp.concatenate([q_nope, q_rot], axis=-1)
    k_full = jnp.concatenate([k_nope, jnp.broadcast_to(k_rot, (B, S, MLA_HEADS, MLA_ROPE))], axis=-1)
    o = causal_block_attention(q_full, k_full, v, (MLA_NOPE + MLA_ROPE) ** -0.5)
    return o.reshape(B, S, MLA_HEADS * MLA_V)

def gla_heads(h_q, h_k, h_v, h_a, h_r, w_a2, b_a, out_norm):
    B, S, _ = h_q.shape
    H, DK, DV, C = GLA_HEADS, GLA_DK, GLA_DV, GLA_CHUNK
    nc = S // C
    f32 = jnp.float32
    q = h_q.reshape(B, nc, C, H, DK).astype(f32) * DK ** -0.5
    k = h_k.reshape(B, nc, C, H, DK).astype(f32)
    v = h_v.reshape(B, nc, C, H, DV).astype(f32)
    log_a = jax.nn.log_sigmoid((h_a @ w_a2 + b_a).astype(f32)) / GLA_GATE_TAU
    b = jnp.cumsum(log_a.reshape(B, nc, C, H, DK), axis=2)
    b_last = b[:, :, -1:]
    k_dec = k * jnp.exp(b_last - b)
    q_inter = q * jnp.exp(b)
    q_intra = q * jnp.exp(b - b_last)
    causal = jnp.tril(jnp.ones((C, C), dtype=bool))
    A = jnp.where(causal, jnp.einsum('bnihd,bnjhd->bnhij', q_intra, k_dec), 0.0)
    o_intra = jnp.einsum('bnhij,bnjhv->bnihv', A, v)
    kv_chunk = jnp.einsum('bnjhd,bnjhv->nbhdv', k_dec, v)
    decay_chunk = jnp.exp(b[:, :, -1]).transpose(1, 0, 2, 3)

    def step(state, inp):
        dec, kv = inp
        return state * dec[..., None] + kv, state

    _, s_prev = lax.scan(step, jnp.zeros((B, H, DK, DV), f32), (decay_chunk, kv_chunk))
    o_inter = jnp.einsum('bnihd,nbhdv->bnihv', q_inter, s_prev)
    o = rms_norm((o_intra + o_inter).reshape(B, S, H, DV), out_norm)
    o = o * jax.nn.silu(h_r.reshape(B, S, H, DV).astype(f32))
    return o.reshape(B, S, H * DV).astype(h_q.dtype)

def mla_gla_mixer(u, positions, w_in, q_norm, w_uq, kv_norm, w_ukv, w_a2, b_a, out_norm, w_out):
    c_q, c_kv, k_r, g_q, g_k, g_v, g_a, g_r = split_cols(u @ w_in, HY_SPLITS)
    o_mla = mla_heads(c_q, c_kv, k_r, positions, q_norm, w_uq, kv_norm, w_ukv)
    o_gla = gla_heads(g_q, g_k, g_v, g_a, g_r, w_a2, b_a, out_norm)
    return jnp.concatenate([o_mla, o_gla.astype(o_mla.dtype)], axis=-1) @ w_out

def nsa_mixer(u, positions, w_in, pos_k, pos_v, ck_w1, ck_w2, cv_w1, cv_w2, w_out):
    B, S, _ = u.shape
    H, G, Dh = NSA_HEADS, NSA_KV_GROUPS, NSA_HEAD_DIM
    Hg = H // G
    dt = u.dtype
    q, k_c, v_c, k_s, v_s, k_w, v_w, g = split_cols(u @ w_in, NSA_SPLITS)
    q = rope(q.reshape(B, S, H, Dh), positions)
    gates = jax.nn.sigmoid(g.reshape(B, S, H, 3))

    n_cmp = (S - NSA_CMP_LEN) // NSA_CMP_STRIDE + 1
    cmp_start = np.arange(n_cmp) * NSA_CMP_STRIDE
    cmp_end = cmp_start + NSA_CMP_LEN - 1
    cmp_idx = cmp_start[:, None] + np.arange(NSA_CMP_LEN)[None, :]

    def compress(t, pos_emb, w1, w2):
        blocks = t.reshape(B, S, G, Dh)[:, cmp_idx] + pos_emb[None, None, :, None, :]
        flat = blocks.transpose(0, 1, 3, 2, 4).reshape(B, n_cmp, G, NSA_CMP_LEN * Dh)
        return jax.nn.silu(flat @ w1) @ w2

    k_cmp = rope(compress(k_c, pos_k, ck_w1, ck_w2), positions[:, cmp_end])
    v_cmp = compress(v_c, pos_v, cv_w1, cv_w2)
    cmp_end_j = jnp.asarray(cmp_end)

    n_blk = S // NSA_SEL_LEN
    n_pad = max(n_blk, NSA_TOP_N)

    def to_blocks(t):
        tb = t.reshape(B, n_blk, NSA_SEL_LEN, G, Dh).transpose(0, 3, 1, 2, 4)
        return jnp.pad(tb, ((0, 0), (0, 0), (0, n_pad - n_blk), (0, 0), (0, 0)))

    k_sel_all = to_blocks(rope(k_s.reshape(B, S, G, Dh), positions))
    v_sel_all = to_blocks(v_s.reshape(B, S, G, Dh))
    blk_start = np.arange(n_pad) * NSA_SEL_LEN
    ov = np.minimum(cmp_start[:, None] + NSA_CMP_LEN, blk_start[None, :] + NSA_SEL_LEN) - np.maximum(cmp_start[:, None], blk_start[None, :])
    overlap = jnp.asarray(np.clip(ov, 0, None) / NSA_CMP_LEN, dtype=jnp.float32)

    pad_w = ((0, 0), (NSA_WINDOW, 0), (0, 0), (0, 0))
    k_win = jnp.pad(rope(k_w.reshape(B, S, G, Dh), positions), pad_w)
    v_win = jnp.pad(v_w.reshape(B, S, G, Dh), pad_w)

    nq = S // NSA_Q_BLOCK
    q_blocks = q.reshape(B, nq, NSA_Q_BLOCK, G, Hg, Dh).transpose(1, 0, 2, 3, 4, 5)
    g_blocks = gates.reshape(B, nq, NSA_Q_BLOCK, G, Hg, 3).transpose(1, 0, 2, 3, 4, 5)
    bi = jnp.arange(B)[:, None, None, None]
    gi = jnp.arange(G)[None, :, None, None]
    scale = Dh ** -0.5
    span = NSA_Q_BLOCK + NSA_WINDOW

    def one_block(args):
        i, qb, gb = args
        t = i * NSA_Q_BLOCK + jnp.arange(NSA_Q_BLOCK)
        s_c = jnp.einsum('bqghd,bngd->bghqn', qb, k_cmp, preferred_element_type=jnp.float32) * scale
        p_c = masked_softmax(s_c, cmp_end_j[None, :] <= t[:, None])
        o_c = jnp.einsum('bghqn,bngd->bqghd', p_c.astype(dt), v_cmp)
        imp = jnp.einsum('bghqn,nm->bgqm', p_c, overlap)
        blk = jnp.arange(n_pad)[None, :]
        cur = (t // NSA_SEL_LEN)[:, None]
        forced = (blk == 0) | (blk == cur) | (blk == cur - 1)
        score = jnp.where(blk <= cur, jnp.where(forced, NSA_FORCE_SCORE, imp), NEG_INF)
        _, sel = lax.top_k(score, NSA_TOP_N)
        k_sel = k_sel_all[bi, gi, sel].reshape(B, G, NSA_Q_BLOCK, NSA_TOP_N * NSA_SEL_LEN, Dh)
        v_sel = v_sel_all[bi, gi, sel].reshape(B, G, NSA_Q_BLOCK, NSA_TOP_N * NSA_SEL_LEN, Dh)
        kpos = (sel[..., None] * NSA_SEL_LEN + jnp.arange(NSA_SEL_LEN)).reshape(B, G, NSA_Q_BLOCK, -1)
        s_s = jnp.einsum('bqghd,bgqmd->bghqm', qb, k_sel, preferred_element_type=jnp.float32) * scale
        p_s = masked_softmax(s_s, (kpos <= t[None, None, :, None])[:, :, None])
        o_s = jnp.einsum('bghqm,bgqmd->bqghd', p_s.astype(dt), v_sel)
        start = i * NSA_Q_BLOCK
        k_wb = lax.dynamic_slice_in_dim(k_win, start, span, axis=1)
        v_wb = lax.dynamic_slice_in_dim(v_win, start, span, axis=1)
        wpos = (start - NSA_WINDOW + jnp.arange(span))[None, :]
        m_w = (wpos <= t[:, None]) & (wpos > t[:, None] - NSA_WINDOW) & (wpos >= 0)
        s_w = jnp.einsum('bqghd,bkgd->bghqk', qb, k_wb, preferred_element_type=jnp.float32) * scale
        p_w = masked_softmax(s_w, m_w)
        o_w = jnp.einsum('bghqk,bkgd->bqghd', p_w.astype(dt), v_wb)
        return gb[..., 0:1] * o_c + gb[..., 1:2] * o_s + gb[..., 2:3] * o_w

    out = lax.map(one_block, (jnp.arange(nq), q_blocks, g_blocks))
    return out.transpose(1, 0, 2, 3, 4, 5).reshape(B, S, NSA_OUT) @ w_out

def first_inputs(seed: int = 0) -> dict:
    key = jax.random.key(seed)
    ks = iter(jax.random.split(key, 40))
    f32 = jnp.float32

    def w(shape, fan_in):
        return jax.random.normal(next(ks), shape, f32) * fan_in ** -0.5

    def gain(shape):
        return 1.0 + 0.02 * jax.random.normal(next(ks), shape, f32)

    def small(shape, s):
        return s * jax.random.normal(next(ks), shape, f32)

    x = jax.random.normal(next(ks), (BATCH, SEQ, D_MODEL), f32)
    offsets = jax.random.randint(next(ks), (BATCH, 1), 0, 1024)
    positions = (offsets + jnp.arange(SEQ)[None, :]).astype(jnp.int32)
    return {
        'x': x,
        'positions': positions,
        'ffn_norm': gain((DEPTH, 2, D_MODEL)),
        'ffn_w_gate': w((DEPTH, 2, D_MODEL, D_FF), D_MODEL),
        'ffn_w_up': w((DEPTH, 2, D_MODEL, D_FF), D_MODEL),
        'ffn_w_down': w((DEPTH, 2, D_FF, D_MODEL), D_FF),
        'mix_norm': gain((DEPTH, D_MODEL)),
        'hy_w_in': w((N_EVEN, D_MODEL, HY_IN), D_MODEL),
        'mla_q_norm': gain((N_EVEN, MLA_Q_LORA)),
        'mla_w_uq': w((N_EVEN, MLA_Q_LORA, MLA_HEADS * (MLA_NOPE + MLA_ROPE)), MLA_Q_LORA),
        'mla_kv_norm': gain((N_EVEN, MLA_KV_LORA)),
        'mla_w_ukv': w((N_EVEN, MLA_KV_LORA, MLA_HEADS * (MLA_NOPE + MLA_V)), MLA_KV_LORA),
        'gla_w_a2': w((N_EVEN, GLA_GATE_RANK, GLA_HEADS * GLA_DK), GLA_GATE_RANK),
        'gla_b_a': small((N_EVEN, GLA_HEADS * GLA_DK), 0.1),
        'gla_out_norm': gain((N_EVEN, GLA_DV)),
        'hy_w_out': w((N_EVEN, HY_OUT, D_MODEL), HY_OUT),
        'nsa_w_in': w((N_ODD, D_MODEL, NSA_IN), D_MODEL),
        'nsa_pos_k': small((N_ODD, NSA_CMP_LEN, NSA_HEAD_DIM), 0.1),
        'nsa_pos_v': small((N_ODD, NSA_CMP_LEN, NSA_HEAD_DIM), 0.1),
        'nsa_ck_w1': w((N_ODD, NSA_CMP_LEN * NSA_HEAD_DIM, NSA_CMP_HIDDEN), NSA_CMP_LEN * NSA_HEAD_DIM),
        'nsa_ck_w2': w((N_ODD, NSA_CMP_HIDDEN, NSA_HEAD_DIM), NSA_CMP_HIDDEN),
        'nsa_cv_w1': w((N_ODD, NSA_CMP_LEN * NSA_HEAD_DIM, NSA_CMP_HIDDEN), NSA_CMP_LEN * NSA_HEAD_DIM),
        'nsa_cv_w2': w((N_ODD, NSA_CMP_HIDDEN, NSA_HEAD_DIM), NSA_CMP_HIDDEN),
        'nsa_w_out': w((N_ODD, NSA_OUT, D_MODEL), NSA_OUT),
        'final_norm': gain((D_MODEL,)),
    }

def first_block(x, positions, ffn_norm, ffn_w_gate, ffn_w_up, ffn_w_down, mix_norm,
              hy_w_in, mla_q_norm, mla_w_uq, mla_kv_norm, mla_w_ukv, gla_w_a2, gla_b_a,
              gla_out_norm, hy_w_out, nsa_w_in, nsa_pos_k, nsa_pos_v, nsa_ck_w1, nsa_ck_w2,
              nsa_cv_w1, nsa_cv_w2, nsa_w_out, final_norm):
    h = x
    for layer in range(DEPTH):
        j = layer // 2
        h = h + 0.5 * swiglu(rms_norm(h, ffn_norm[layer, 0]), ffn_w_gate[layer, 0], ffn_w_up[layer, 0], ffn_w_down[layer, 0])
        u = rms_norm(h, mix_norm[layer])
        if layer % 2 == 0:
            mixed = mla_gla_mixer(u, positions, hy_w_in[j], mla_q_norm[j], mla_w_uq[j], mla_kv_norm[j],
                                  mla_w_ukv[j], gla_w_a2[j], gla_b_a[j], gla_out_norm[j], hy_w_out[j])
        else:
            mixed = nsa_mixer(u, positions, nsa_w_in[j], nsa_pos_k[j], nsa_pos_v[j], nsa_ck_w1[j],
                              nsa_ck_w2[j], nsa_cv_w1[j], nsa_cv_w2[j], nsa_w_out[j])
        h = h + mixed.astype(h.dtype)
        h = h + 0.5 * swiglu(rms_norm(h, ffn_norm[layer, 1]), ffn_w_gate[layer, 1], ffn_w_up[layer, 1], ffn_w_down[layer, 1])
    return rms_norm(h, final_norm)


HEAD_DIM = 64
H_NA = 4
H_DIL = 6
H_GQ = 6
H_GKV = 2
NA_W = H_NA * HEAD_DIM
DIL_W = H_DIL * HEAD_DIM
GQ_W = H_GQ * HEAD_DIM
GKV_W = H_GKV * HEAD_DIM
D_MIX = NA_W + DIL_W + GQ_W
D_IN = 3 * NA_W + 3 * DIL_W + GQ_W + 2 * GKV_W

GRID_W = 64
NA_KH_MAX = 8
NA_KW = 16
DIL_PATTERNS = ((128, 1), (512, 4), (2048, 16))
ROPE_THETA_2 = 500000.0
ROPE_DIMS = HEAD_DIM // 4
AXIAL_THETA = 10000.0
Q_BLK = 128
CONV_W = 3
EPS = 1e-6
NEG_INF_2 = -1e30


def rms_norm_2(x, g):
    xf = x.astype(jnp.float32)
    y = xf * lax.rsqrt(jnp.mean(xf * xf, axis=-1, keepdims=True) + EPS)
    return (y * g.astype(jnp.float32)).astype(x.dtype)

def rope_cos_sin(pos, dim, theta):
    inv = theta ** (-jnp.arange(0, dim, 2, dtype=jnp.float32) / dim)
    ang = pos.astype(jnp.float32)[:, None] * inv[None, :]
    return jnp.cos(ang), jnp.sin(ang)

def rotate(x, cos, sin):
    half = x.shape[-1] // 2
    x1 = x[..., :half].astype(jnp.float32)
    x2 = x[..., half:].astype(jnp.float32)
    c = cos[None, :, None, :]
    s = sin[None, :, None, :]
    return jnp.concatenate([x1 * c - x2 * s, x2 * c + x1 * s], axis=-1).astype(x.dtype)

def partial_rotary(x, cos, sin):
    return jnp.concatenate([rotate(x[..., :ROPE_DIMS], cos, sin), x[..., ROPE_DIMS:]], axis=-1)

def axial_rotary(x, cos_r, sin_r, cos_c, sin_c):
    half = x.shape[-1] // 2
    return jnp.concatenate([rotate(x[..., :half], cos_r, sin_r), rotate(x[..., half:], cos_c, sin_c)], axis=-1)

def neighbourhood_tables(S):
    rows = S // GRID_W
    kh = min(NA_KH_MAX, rows)
    t = jnp.arange(S)
    r = t // GRID_W
    c = t % GRID_W
    r0 = jnp.clip(r - kh // 2, 0, rows - kh)
    c0 = jnp.clip(c - NA_KW // 2, 0, GRID_W - NA_KW)
    kr = r0[:, None] + jnp.arange(kh)[None, :]
    kc = c0[:, None] + jnp.arange(NA_KW)[None, :]
    idx = (kr[:, :, None] * GRID_W + kc[:, None, :]).reshape(S, kh * NA_KW)
    dr = (kr - r[:, None] + NA_KH_MAX - 1)[:, :, None]
    dc = (kc - c[:, None] + NA_KW - 1)[:, None, :]
    return idx, dr, dc

def neighbourhood_attention(q, k, v, rpb, idx, dr, dc):
    B, S, H, hd = q.shape
    nk = idx.shape[1]
    nb = S // Q_BLK
    scale = hd ** -0.5
    bias = rpb[:, dr, dc].reshape(H, S, nk).astype(jnp.float32)
    qb = q.reshape(B, nb, Q_BLK, H, hd).transpose(1, 0, 2, 3, 4)
    idxb = idx.reshape(nb, Q_BLK, nk)
    biasb = bias.reshape(H, nb, Q_BLK, nk).transpose(1, 0, 2, 3)

    def block(args):
        qi, ii, bi = args
        kg = k[:, ii]
        vg = v[:, ii]
        s = jnp.einsum('bqhd,bqkhd->bhqk', qi, kg).astype(jnp.float32) * scale + bi[None]
        p = jax.nn.softmax(s, axis=-1).astype(v.dtype)
        return jnp.einsum('bhqk,bqkhd->bqhd', p, vg)

    o = lax.map(block, (qb, idxb, biasb))
    return o.transpose(1, 0, 2, 3, 4).reshape(B, S, H * hd)

def dilated_tables(S):
    t = jnp.arange(S)
    idxs, valids = [], []
    for w, d in DIL_PATTERNS:
        n = (w // 2) // d
        pos = t[:, None] + (jnp.arange(-n, n + 1) * d)[None, :]
        valids.append((pos >= 0) & (pos < S))
        idxs.append(jnp.clip(pos, 0, S - 1))
    return tuple(idxs), tuple(valids)

def dilated_window_attention(q, k, v, idxs, valids):
    B, S, H, hd = q.shape
    nb = S // Q_BLK
    scale = hd ** -0.5
    qb = q.reshape(B, nb, Q_BLK, H, hd).transpose(1, 0, 2, 3, 4)
    idxb = tuple(i.reshape(nb, Q_BLK, -1) for i in idxs)
    valb = tuple(m.reshape(nb, Q_BLK, -1) for m in valids)

    def block(args):
        qi, ii, mm = args
        lses, outs = [], []
        for ig, mg in zip(ii, mm):
            kg = k[:, ig]
            vg = v[:, ig]
            s = jnp.einsum('bqhd,bqkhd->bhqk', qi, kg).astype(jnp.float32) * scale
            s = jnp.where(mg[None, None], s, NEG_INF_2)
            lse = jax.nn.logsumexp(s, axis=-1)
            p = jnp.exp(s - lse[..., None]).astype(v.dtype)
            outs.append(jnp.einsum('bhqk,bqkhd->bqhd', p, vg))
            lses.append(lse)
        wts = jax.nn.softmax(jnp.stack(lses), axis=0).astype(v.dtype)
        return jnp.einsum('gbhq,gbqhd->bqhd', wts, jnp.stack(outs))

    o = lax.map(block, (qb, idxb, valb))
    return o.transpose(1, 0, 2, 3, 4).reshape(B, S, H * hd)

def gqa_block_attention(q, k, v):
    B, S, Hq, hd = q.shape
    Hkv = k.shape[2]
    g = Hq // Hkv
    nb = S // Q_BLK
    scale = hd ** -0.5
    qb = q.reshape(B, nb, Q_BLK, Hkv, g, hd).transpose(1, 0, 2, 3, 4, 5)

    def block(qi):
        s = jnp.einsum('bqkgd,bskd->bkgqs', qi, k).astype(jnp.float32) * scale
        p = jax.nn.softmax(s, axis=-1).astype(v.dtype)
        return jnp.einsum('bkgqs,bskd->bqkgd', p, v)

    o = lax.map(block, qb)
    return o.transpose(1, 0, 2, 3, 4, 5).reshape(B, S, Hq * hd)

def depthwise_conv_centred(z, w, b):
    S = z.shape[1]
    pad = CONV_W // 2
    zp = jnp.pad(z, ((0, 0), (pad, pad), (0, 0)))
    out = zp[:, 0:S] * w[0] + b
    for j in range(1, CONV_W):
        out = out + zp[:, j:j + S] * w[j]
    return out

def mixer_sublayer(x, n1, w_in_l, qg, kg, rpb_l, og, w_out_l, tables):
    (na_idx, na_dr, na_dc, dil_idx, dil_val, cos1, sin1, cos_r, sin_r, cos_c, sin_c) = tables
    B, S, _ = x.shape
    h = rms_norm_2(x, n1)
    proj = h @ w_in_l
    sizes = (NA_W, NA_W, NA_W, DIL_W, DIL_W, DIL_W, GQ_W, GKV_W, GKV_W)
    cuts = [int(c) for c in np.cumsum(sizes)[:-1]]
    qa, ka, va, qd, kd, vd, qc, kc, vc = jnp.split(proj, cuts, axis=-1)

    def heads(z, n):
        return z.reshape(B, S, n, HEAD_DIM)

    qa = rms_norm_2(heads(qa, H_NA), qg[0])
    ka = rms_norm_2(heads(ka, H_NA), kg[0])
    out_a = neighbourhood_attention(qa, ka, heads(va, H_NA), rpb_l, na_idx, na_dr, na_dc)
    qd = partial_rotary(rms_norm_2(heads(qd, H_DIL), qg[1]), cos1, sin1)
    kd = partial_rotary(rms_norm_2(heads(kd, H_DIL), kg[1]), cos1, sin1)
    out_d = dilated_window_attention(qd, kd, heads(vd, H_DIL), dil_idx, dil_val)
    qc = axial_rotary(rms_norm_2(heads(qc, H_GQ), qg[2]), cos_r, sin_r, cos_c, sin_c)
    kc = axial_rotary(rms_norm_2(heads(kc, H_GKV), kg[2]), cos_r, sin_r, cos_c, sin_c)
    out_c = gqa_block_attention(qc, kc, heads(vc, H_GKV))

    mix = jnp.concatenate([
        rms_norm_2(out_a, og[:NA_W]),
        rms_norm_2(out_d, og[NA_W:NA_W + DIL_W]),
        rms_norm_2(out_c, og[NA_W + DIL_W:]),
    ], axis=-1)
    return x + mix @ w_out_l

def channel_sublayer(x, n2, w_gu, cw, cb, w_dn):
    h = rms_norm_2(x, n2)
    g, u = jnp.split(h @ w_gu, 2, axis=-1)
    g = depthwise_conv_centred(g, cw, cb)
    return x + (jax.nn.gelu(g, approximate=False) * u) @ w_dn

def second_inputs(seed: int = 0) -> dict:
    key = jax.random.key(seed)
    ks = jax.random.split(key, 13)

    def nrm(k, shape, s):
        return s * jax.random.normal(k, shape, jnp.float32)

    return {
        'x': nrm(ks[0], (BATCH, SEQ, D_MODEL), 1.0),
        'norm1_g': 1.0 + nrm(ks[1], (DEPTH, D_MODEL), 0.02),
        'w_in': nrm(ks[2], (DEPTH, D_MODEL, D_IN), D_MODEL ** -0.5),
        'q_norm_g': 1.0 + nrm(ks[3], (DEPTH, 3, HEAD_DIM), 0.02),
        'k_norm_g': 1.0 + nrm(ks[4], (DEPTH, 3, HEAD_DIM), 0.02),
        'rpb': nrm(ks[5], (DEPTH, H_NA, 2 * NA_KH_MAX - 1, 2 * NA_KW - 1), 0.1),
        'out_norm_g': 1.0 + nrm(ks[6], (DEPTH, D_MIX), 0.02),
        'w_out': nrm(ks[7], (DEPTH, D_MIX, D_MODEL), D_MIX ** -0.5),
        'norm2_g': 1.0 + nrm(ks[8], (DEPTH, D_MODEL), 0.02),
        'w_gate_up': nrm(ks[9], (DEPTH, D_MODEL, 2 * D_FF), D_MODEL ** -0.5),
        'conv_w': nrm(ks[10], (DEPTH, CONV_W, D_FF), CONV_W ** -0.5),
        'conv_b': nrm(ks[11], (DEPTH, D_FF), 0.02),
        'w_down': nrm(ks[12], (DEPTH, D_FF, D_MODEL), D_FF ** -0.5),
    }

def second_block(x, norm1_g, w_in, q_norm_g, k_norm_g, rpb, out_norm_g, w_out, norm2_g, w_gate_up, conv_w, conv_b, w_down):
    S = x.shape[1]
    t = jnp.arange(S, dtype=jnp.int32)
    cos1, sin1 = rope_cos_sin(t, ROPE_DIMS, ROPE_THETA_2)
    cos_r, sin_r = rope_cos_sin(t // GRID_W, HEAD_DIM // 2, AXIAL_THETA)
    cos_c, sin_c = rope_cos_sin(t % GRID_W, HEAD_DIM // 2, AXIAL_THETA)
    na_idx, na_dr, na_dc = neighbourhood_tables(S)
    dil_idx, dil_val = dilated_tables(S)
    tables = (na_idx, na_dr, na_dc, dil_idx, dil_val, cos1, sin1, cos_r, sin_r, cos_c, sin_c)
    for l in range(DEPTH):
        x = mixer_sublayer(x, norm1_g[l], w_in[l], q_norm_g[l], k_norm_g[l], rpb[l],
                           out_norm_g[l], w_out[l], tables)
        x = channel_sublayer(x, norm2_g[l], w_gate_up[l], conv_w[l], conv_b[l], w_down[l])
    return x


def setup_inputs(seed=0):
    out = dict(first_inputs(seed))
    for name, value in second_inputs(seed + 1).items():
        if name != "x":
            out[name + "_2"] = value
    return out


def reference(
    x, positions, ffn_norm, ffn_w_gate, ffn_w_up, ffn_w_down, mix_norm, hy_w_in, mla_q_norm,
    mla_w_uq, mla_kv_norm, mla_w_ukv, gla_w_a2, gla_b_a, gla_out_norm, hy_w_out, nsa_w_in,
    nsa_pos_k, nsa_pos_v, nsa_ck_w1, nsa_ck_w2, nsa_cv_w1, nsa_cv_w2, nsa_w_out, final_norm,
    norm1_g_2, w_in_2, q_norm_g_2, k_norm_g_2, rpb_2, out_norm_g_2, w_out_2, norm2_g_2,
    w_gate_up_2, conv_w_2, conv_b_2, w_down_2,
):
    x = first_block(
        x, positions, ffn_norm, ffn_w_gate, ffn_w_up, ffn_w_down, mix_norm, hy_w_in, mla_q_norm,
        mla_w_uq, mla_kv_norm, mla_w_ukv, gla_w_a2, gla_b_a, gla_out_norm, hy_w_out, nsa_w_in,
        nsa_pos_k, nsa_pos_v, nsa_ck_w1, nsa_ck_w2, nsa_cv_w1, nsa_cv_w2, nsa_w_out, final_norm,
    )
    return second_block(
        x, norm1_g_2, w_in_2, q_norm_g_2, k_norm_g_2, rpb_2, out_norm_g_2, w_out_2, norm2_g_2,
        w_gate_up_2, conv_w_2, conv_b_2, w_down_2,
    )


_drawn_inputs = setup_inputs


def setup_inputs(seed=0):
    import zlib

    import numpy as np

    out = dict(_drawn_inputs(seed))
    spreads = {}
    factors = {'mla_q_norm': 8.0,
     'mla_kv_norm': 5.238,
     'gla_out_norm': 5.513,
     'nsa_pos_k': 8.0,
     'q_norm_g_2': 5.713,
     'k_norm_g_2': 5.696,
     'norm2_g_2': 3.517,
     'conv_b_2': 5.088,
     'rpb_2': 4.168}
    for name, (base, spread) in spreads.items():
        noise = np.random.default_rng([zlib.crc32(name.encode()), seed]).standard_normal(out[name].shape)
        drawn = base * np.exp(spread * noise) if base else spread * noise
        out[name] = jnp.asarray(drawn.astype(out[name].dtype))
    for name, factor in factors.items():
        out[name] = (out[name] * factor).astype(out[name].dtype)
    return out
```

```python
from contextlib import ExitStack

import numpy as np

import concourse.bass as bass
from concourse import mybir

F32 = mybir.dt.float32
F32R = mybir.dt.float32r
BF16 = mybir.dt.bfloat16
I32 = mybir.dt.int32
ALU = mybir.AluOpType
ACT = mybir.ActivationFunctionType
X_AXIS = mybir.AxisListType.X

P = 128
S = 256
NT = S // P
D = 1024
KD = D // P
D_FF = 2816
STEPS = D_FF // 256
EPS = 1e-6
NEG = -1e30
TINY = 1e-30

UNIT = 2048
NRAW = 3
NSPLIT = 3

HY_CQ, HY_CKV, HY_KR, HY_GQ, HY_GK, HY_GV, HY_GA, HY_GR, HY_IN = 0, 256, 384, 416, 672, 928, 1440, 1456, 1968
MLA_H, MLA_NOPE, MLA_ROPE, MLA_QK = 8, 64, 32, 96
GLA_H, GLA_DV, GLA_C, GLA_R = 4, 128, 64, 16
NS_Q, NS_KC, NS_VC, NS_KS, NS_VS, NS_KW, NS_VW, NS_G, NS_IN = 0, 1024, 1280, 1536, 1792, 2048, 2304, 2560, 2608
NS_H, NS_GR = 16, 4
CMP_LEN, CMP_STRIDE = 32, 16
NCMP = (S - CMP_LEN) // CMP_STRIDE + 1
SEC_W = dict(qa=256, ka=256, va=256, qd=384, kd=384, vd=384, qc=384, kc=128, vc=128)
SEC_ORDER = ("qa", "ka", "qd", "kd", "qc", "kc", "va", "vd", "vc")
QA, KA, QD, KDL, QC, KC, VA, VD, VC = (sum(SEC_W[m] for m in SEC_ORDER[:i]) for i in range(9))
SEC_IN = sum(SEC_W.values())
SEC_KINDS = ((QA, 8, 0, 1), (QD, 12, 8, 4), (QC, 8, 20, 6))
GRID = 64

HY_BLOCKS = [256] * 7 + [HY_IN - 7 * 256]
NSA_BLOCKS = [256] * 10 + [NS_IN - 10 * 256]
SEC_BLOCKS = [256] * 10

FFN_UNITS = 3 * STEPS
FFN_NORM = [0, 2, 3, 5, 7, 9]
N_PAR = 10
OUT_UNITS = 4
_at, U = 0, {}
for _name, _n in [("ffn0", FFN_UNITS), ("hy_in", 8), ("uq", 1), ("ukv", 1), ("mix0", OUT_UNITS),
                  ("ffn1", FFN_UNITS), ("ffn2", FFN_UNITS), ("nsa_in", 11), ("mix1", OUT_UNITS),
                  ("ffn3", FFN_UNITS), ("sec_in0", 10), ("mix2", OUT_UNITS), ("ffn4", FFN_UNITS),
                  ("sec_in1", 10), ("mix3", OUT_UNITS), ("ffn5", FFN_UNITS)]:
    U[_name] = _at
    _at += _n
N_UNITS = _at

TURN = {n: q for q, n in enumerate(["n0", "n1", "m0", "n2", "n3", "n4", "m1", "n5",
                                    "n6", "m2", "n7", "n8", "m3", "n9"])}
JOB0 = {"mla": 0, "nsa": 8, "sec0": 40, "sec1": 56}
FT_GROUPS = {"mla": 9, "nsa": 12, "sec0": 14, "sec1": 14}
FT_A0, FT_D0 = {}, {}
_a = _d = 0
for _s, _n in FT_GROUPS.items():
    FT_A0[_s], FT_D0[_s] = _a, _d
    _a += (_n + 1) // 2
    _d += _n // 2
PROJ0 = {"hy": 0, "nsa": 8, "sec0": 19, "sec1": 29}


def rms_turn(n):
    return n + (1 if n >= 6 else 0)


_c, C = 0, {}
for _name, _n in [("ident", 128), ("flip", 128), ("block_tri", 128), ("causal", 128), ("dil", 2 * 256), ("na_mask", 64),
                  ("cmp_add", 64), ("cmp_01", 64), ("freq", 48), ("cos1", 16), ("sin1", 16),
                  ("cosax", 64), ("sinax", 64)]:
    C[_name] = (_c, _c + _n)
    _c += _n
N_CONST = _c

G_NORM, G_OUT, G_Q, G_KV, N_GAIN = 0, 80, 96, 98, 99


def shape_constants():
    c = np.zeros((P, N_CONST), np.float32)

    def put(name, a):
        lo, hi = C[name]
        c[:, lo:hi] = np.asarray(a, np.float32).reshape(P, hi - lo)

    p = np.arange(P)
    put("ident", np.eye(P))
    put("flip", p[None, :] == p[:, None] // GRID * GRID + GRID - 1 - p[:, None] % GRID)
    put("block_tri", (p[:, None] <= p[None, :]) & (p[:, None] // GLA_C == p[None, :] // GLA_C))
    put("causal", np.where(p[None, :] > p[:, None], NEG, 0.0))
    t = np.arange(S)
    times = np.zeros((S, S))
    for w, d in ((128, 1), (512, 4), (2048, 16)):
        off = t[None, :] - t[:, None]
        times += (off % d == 0) & (np.abs(off) <= (w // 2) // d * d)
    dil = np.where(times > 0, np.log(np.maximum(times, 1)), NEG)
    put("dil", dil.reshape(NT, P, S).transpose(1, 0, 2))
    col = GRID - 1 - p % GRID
    c0 = np.clip(col - 8, 0, GRID - 16)
    kc = np.arange(GRID)
    put("na_mask", np.where((kc[None] >= c0[:, None]) & (kc[None] < c0[:, None] + 16), 0.0, NEG))
    n = np.arange(32)
    ok = (n[None] < NCMP) & (n[None] * CMP_STRIDE + CMP_LEN - 1 <= t[:, None])
    put("cmp_add", np.where(ok, 0.0, NEG).reshape(NT, P, 32).transpose(1, 0, 2))
    put("cmp_01", ok.reshape(NT, P, 32).transpose(1, 0, 2))

    def inv(theta, d):
        e = -np.arange(d // 2, dtype=np.float32) * np.float32(2.0 / d)
        return np.power(np.float64(theta), e.astype(np.float64)).astype(np.float32)

    put("freq", np.broadcast_to(np.concatenate([inv(10000.0, 32), inv(10000.0, 64)]), (P, 48)))

    def tables(pos, theta, d):
        ang = (pos.astype(np.float32)[:, None] * inv(theta, d)[None]).astype(np.float64)
        return np.cos(ang), np.sin(ang)

    for k, f in (("cos", 0), ("sin", 1)):
        one = tables(t, 500000.0, 16)[f]
        put(k + "1", one.reshape(NT, P, 8).transpose(1, 0, 2))
        ax = np.stack([tables(t // GRID, 10000.0, 32)[f], tables(t % GRID, 10000.0, 32)[f]], 1)
        put(k + "ax", ax.reshape(NT, P, 2, 16).transpose(1, 0, 2, 3))
    return c


def build(nc, stream, consts, gains, conv, x, positions, pos_rows, cmp_w1, cmp_w2, final_gain, gla_gain,
          gla_a2, gla_ba, q_gain2, k_gain2, rpb2, out):
    ctx = ExitStack()
    with ctx:
        def sb(name, shape, dt=F32):
            return ctx.enter_context(nc.sbuf_tensor(name, shape, dt))

        def sem(name):
            return ctx.enter_context(nc.semaphore(name))

        bank = [ctx.enter_context(nc.psum_tensor(f"bank{i}", [P, 512], F32)) for i in range(8)]

        raw = sb("raw", [P, NRAW, UNIT])
        w_hi = sb("w_hi", [P, NSPLIT, UNIT], F32R)
        w_lo = sb("w_lo", [P, NSPLIT, UNIT], F32R)
        X = sb("X", [P, NT, D])
        xt_hi = sb("xt_hi", [P, KD, S], F32R)
        xt_lo = sb("xt_lo", [P, KD, S], F32R)
        proj = sb("proj", [P, NT, NS_IN])
        work = sb("work", [P, 2 * 2048])
        QT = sb("QT", [P, 16 * S])
        KT = sb("KT", [P, 12 * S])
        O = sb("O", [P, NT, D])
        prob = sb("prob", [P, 2048])
        h_hi = sb("h_hi", [P, 2, 512], F32R)
        h_lo = sb("h_lo", [P, 2, 512], F32R)
        cst = sb("cst", [P, N_CONST])
        gcol = sb("gcol", [P, N_GAIN])
        ccol = sb("ccol", [P, 2, 4, 22])
        ident_b = sb("ident_b", [P, P], BF16)
        causal_b = sb("causal_b", [P, P], BF16)
        head_gain = sb("head_gain", [P, 2, 6, 64])
        gla_row = sb("gla_row", [P, GLA_DV])
        a2 = sb("a2", [GLA_R + 1, 256])
        w2 = sb("w2", [P, 2, 64])
        posr = sb("posr", [P, 2, 16])
        pos_i = sb("pos_i", [P, 3], I32)
        pos_f = sb("pos_f", [P, 3])
        ang = sb("ang", [P, 3, 48])
        red = sb("red", [P, 3, 48])
        tmp48 = sb("tmp48", [P, 3, 48])
        rsin = sb("rsin", [P, 3, 48])
        rcos = sb("rcos", [P, 3, 48])
        neg_half = sb("neg_half", [P, 56])
        ss = sb("ss", [P, 56])
        ms = sb("ms", [P, 56])
        rstd = sb("rstd", [P, 56])
        negmax = sb("negmax", [P, 4, 2])
        sums = sb("sums", [P, 2, 2, 4])
        rsum = sb("rsum", [P, 2, 2, 4])
        gate = sb("gate", [P, NT, 48])
        small = sb("small", [P, 4, 32])

        def const(name):
            return cst[:, C[name][0]:C[name][1]]

        ident = const("ident")
        xn = work[:, 0:2048].rearrange("p (t d) -> p t d", t=NT)
        na_bias = work[:, 2048:4096].rearrange("p (t h s) -> p t h s", t=NT, h=4)
        act_g = QT[:, 0:1024].rearrange("p (b n) -> p b n", b=2)
        h_f = QT[:, 1024:1536]
        conv_y = QT[:, 1536:2560].rearrange("p (b n) -> p b n", b=2)
        qT = QT[:, :].rearrange("p (h s) -> p h s", s=S)
        kT = KT[:, :].rearrange("p (h s) -> p h s", s=S)

        raw_in = [sem(f"raw_in{i}") for i in range(NRAW)]
        hi_done, lo_done = sem("hi_done"), sem("lo_done")
        unit_used = sem("unit_used")
        x_in, cst_in, gain_in, par_in = sem("x_in"), sem("cst_in"), sem("gain_in"), sem("par_in")
        x_upd = sem("x_upd")
        sq_done, ms_done, rstd_done = sem("sq_done"), sem("ms_done"), sem("rstd_done")
        xn0, xn1 = sem("xn0"), sem("xn1")
        xt_ps, xth, xtl = sem("xt_ps"), sem("xth"), sem("xtl")
        actg_done, mul_done, hh_done, hl_done = sem("actg_done"), sem("mul_done"), sem("hh_done"), sem("hl_done")
        cv_mid, cv_left, cv_done = sem("cv_mid"), sem("cv_left"), sem("cv_done")
        pj_evac = sem("pj_evac")
        ft_ready_d, ft_ready_p = sem("ft_ready_d"), sem("ft_ready_p")
        ft_ps, ft_a, ft_d = sem("ft_ps"), sem("ft_a"), sem("ft_d")
        s_done, nm_done, exp_done, t_done = sem("s_done"), sem("nm_done"), sem("exp_done"), sem("t_done")
        pt_evac, pv_done, o_done = sem("pt_evac"), sem("pv_done"), sem("o_done")
        mix_ready = sem("mix_ready")
        dve_own, act_own, pool_own = sem("dve_own"), sem("act_own"), sem("pool_own")
        const_ready, rope_arg, rope_tab = sem("const_ready"), sem("rope_arg"), sem("rope_tab")
        mla_sq, mla_ms, mla_rs, mla_cn, mla_tp, mla_ch, mla_cl, mla_q, mla_kv, mla_up = (
            sem("mla_" + n) for n in ("sq", "ms", "rs", "cn", "tp", "ch", "cl", "q", "kv", "up"))
        g_tp, g_ev, g_evd, g_z, g_ln, g_la, g_b, g_bt, g_d, g_e, g_qk, g_a, g_am, g_kt, g_kd, g_kv, g_st, g_o, \
            g_ms, g_rs, g_sr = (sem("g_" + n) for n in (
                "tp", "ev", "evd", "z", "ln", "la", "b", "bt", "d", "e", "qk", "a", "am", "kt", "kd", "kv", "st",
                "o", "ms", "rs", "sr"))
        c_w, c_dup, c_tp, c_m, c_h, c_b, c_hid, c_kc, c_kr, c_kt, c_kcT, c_s, c_sc, c_e, c_p, c_pt, c_pe, c_pv, \
            c_gate = (sem("c_" + n) for n in (
                "w", "dup", "tp", "m", "h", "b", "hid", "kc", "kr", "kt", "kcT", "s", "sc", "e", "p", "pt", "pe",
                "pv", "gate"))
        b_in, b_free, na_ready = sem("b_in"), sem("b_free"), sem("na_ready")
        e_sq, e_ms, e_rt, e_rs, e_m = sem("e_sq"), sem("e_ms"), sem("e_rt"), sem("e_rs"), sem("e_m")
        f_in = sem("f_in")
        stored = sem("stored")

        block = ctx.enter_context(nc.Block())

        def ffn_unit(f, kind, s):
            u0 = U[f"ffn{f}"]
            if kind == "d":
                return u0 + (FFN_UNITS - 1 if s == STEPS - 1 else 3 * s + 4)
            g = u0 if s == 0 else u0 + 3 * s - 1
            return g if kind == "g" else g + 1

        def ffn_steps(eng, f, triple):
            triple(f, 0, None)
            triple(f, 1, None)
            with eng.Fori(0, 4) as i:
                triple(f, 2, i)
                triple(f, 3, i)
            triple(f, 10, None)

        def on(n, per, i):
            return n if i is None else i * per + n

        def tap(l, n, s, j, i):
            c = on(2 * s + j, 4, i)
            return ccol[:, l, n, c:c + 1] if i is None else ccol[:, l, n, bass.ds(c, 1)]

        heads = {}
        heads["mla"] = [dict(q=h, k=h, d=MLA_QK, causal=True,
                             v=lambda kt, h=h: work[:, 2048 + kt * 1024 + h * 128 + 64:2048 + kt * 1024 + h * 128 + 128])
                        for h in range(MLA_H)]
        heads["nsa"] = [dict(q=h, k=4 * br + h // 4, d=64, causal=True,
                             v=lambda kt, h=h, br=br: proj[:, kt, (NS_VS, NS_VW)[br] + (h // 4) * 64:
                                                           (NS_VS, NS_VW)[br] + (h // 4) * 64 + 64])
                        for br in range(2) for h in range(NS_H)]

        def sec_job(h):
            if h < 4:
                return dict(q=h, k=h, d=64, causal=False, order="flip", bias=lambda qt: na_bias[:, qt, h, :],
                            v=lambda kt: proj[:, kt, VA + h * 64:VA + h * 64 + 64])
            if h < 10:
                lo = C["dil"][0]
                return dict(q=h, k=h, d=64, causal=False, order="ident", bias=lambda qt: cst[:, lo + qt * S:lo + qt * S + S],
                            v=lambda kt: proj[:, kt, VD + (h - 4) * 64:VD + (h - 4) * 64 + 64])
            g = (h - 10) // 3
            return dict(q=h, k=10 + g, d=64, causal=False, bias=None,
                        v=lambda kt: proj[:, kt, VC + g * 64:VC + g * 64 + 64])

        heads["sec0"] = heads["sec1"] = [sec_job(4 * (3 - i // 4) + i % 4) for i in range(16)]

        def ft_groups(stage):
            if stage == "mla":
                gs = [([(lambda t, h=h: work[:, 2048 + t * 1024 + h * 128:2048 + t * 1024 + h * 128 + 64])
                        for h in (2 * g, 2 * g + 1)], 64, [kT[0:64, 2 * g:2 * g + 2, :]]) for g in range(4)]
                gs.append(([lambda t: proj[:, t, HY_KR - 64:HY_KR + 32]], 96, None))
                gs += [([(lambda t, h=h: work[:, t * 768 + h * 96:t * 768 + h * 96 + 96])
                         for h in (2 * g, 2 * g + 1)], 96, [qT[0:96, 2 * g:2 * g + 2, :]]) for g in range(4)]
                return gs
            if stage == "nsa":
                src = [NS_Q + 64 * h for h in range(16)] + [NS_KS + 64 * g for g in range(4)] + \
                      [NS_KW + 64 * g for g in range(4)]
                dst = [(qT, h) for h in range(16)] + [(kT, g) for g in range(8)]
            else:
                src, dst = [], []
                for q, k, nq, nk, q0, k0 in ((QA, KA, 4, 4, 0, 0), (QD, KDL, 6, 6, 4, 4), (QC, KC, 6, 2, 10, 10)):
                    src += [q + 64 * h for h in range(nq)] + [k + 64 * h for h in range(nk)]
                    dst += [(qT, q0 + h) for h in range(nq)] + [(kT, k0 + h) for h in range(nk)]
            return [([(lambda t, c=c: proj[:, t, c:c + 64]) for c in src[2 * g:2 * g + 2]], 64,
                     [dst[2 * g][0][0:64, dst[2 * g][1]:dst[2 * g][1] + 2, :]]) for g in range(len(src) // 2)]

        def ft_scale(stage, g):
            return 0.125 if stage == "nsa" and g < NS_H // 2 else 1.0

        def ncols(job, qt):
            return P if job["causal"] and qt == 0 else S

        def pt_blocks(job):
            return [(0, 0), (1, 0), (1, 1)] if job["causal"] else [(0, 0), (1, 0), (1, 1), (0, 1)]

        def p_of(par, qt, lo, hi):
            return prob[:, par * 512 + qt * 256 + lo:par * 512 + qt * 256 + hi]

        def pts_of(par, lo, hi):
            return prob[:, 1024 + par * 512 + lo:1024 + par * 512 + hi]

        def q_(i):
            return QT[:, i * 512:(i + 1) * 512]

        gla_q, gla_k, gla_b, gla_eb, gla_d, gla_ei, gla_ed, gla_qi = (q_(i) for i in range(8))
        gla_kd, gla_za, gla_ln, gla_la, gla_kdt = (KT[:, i * 512:(i + 1) * 512] for i in range(5))
        gla_aT = KT[:, 2560:2816]
        gla_qz, gla_am, gla_st, gla_sr = (work[:, i * 1024:(i + 1) * 1024] for i in range(4))

        def chunks(ap):
            return ap.rearrange("p (a c i) -> p a c i", a=2, c=4)

        dup = work[:, 0:2048].rearrange("p (m t g e d) -> p m t g e d", m=2, t=2, g=4, e=2)
        m_k = work[:, 2048:2048 + 1280].rearrange("p (g s) -> p g s", g=5)
        m_v = work[:, 0:1280].rearrange("p (g s) -> p g s", g=5)
        hid = [QT[:, 0:128], QT[:, 128:256]]
        sc = work[:, 2048:3072]
        pc = work[:, 3072:4096]
        pct = work[:, 0:1024]
        kc_tok, vc_tok, kcT_ = KT[:, 2048:2112], KT[:, 2112:2176], KT[:, 2176:2304]
        rope_t = KT[:, 2304:3072]

        def rotate(eng, lnk, x1, x2, cos, sin, t1, t2):
            lnk(eng.tensor_tensor(t1, x1, sin, ALU.mult))
            lnk(eng.tensor_tensor(t2, x2, sin, ALU.mult))
            lnk(eng.tensor_tensor(x1, x1, cos, ALU.mult))
            lnk(eng.tensor_tensor(x2, x2, cos, ALU.mult))
            lnk(eng.tensor_tensor(x1, x1, t2, ALU.subtract))
            lnk(eng.tensor_tensor(x2, x2, t1, ALU.add))

        def rope_heads(eng, lnk, view, off, half, cos_t, sin_t, tmp):
            n = view.shape[1]
            x1 = view[:, :, off:off + half]
            x2 = view[:, :, off + half:off + 2 * half]
            cos = cos_t.unsqueeze(1).to_broadcast([P, n, half])
            sin = sin_t.unsqueeze(1).to_broadcast([P, n, half])
            t1 = tmp[:, 0:n * half].rearrange("p (h d) -> p h d", h=n)
            t2 = tmp[:, n * half:2 * n * half].rearrange("p (h d) -> p h d", h=n)
            rotate(eng, lnk, x1, x2, cos, sin, t1, t2)

        def head_rms(tile, n):
            _, heads_n, o, _ = SEC_KINDS[n]
            return tile[:, 0:56].rearrange("p (t h) -> p t h", t=NT)[:, :, o:o + heads_n]

        def sec_heads(eng, lnk, n, t, l, tmp):
            def head_view(c, m):
                return proj[:, t, c:c + m * 64].rearrange("p (h d) -> p h d", h=m)

            c, m, o, _ = SEC_KINDS[n]
            r = rstd[:, t * 28 + o:t * 28 + o + m].unsqueeze(2).to_broadcast([P, m, 64])
            lnk(eng.tensor_tensor(head_view(c, m), head_view(c, m), r, ALU.mult))
            for c1, m1, row in (((QA, 4, 0), (KA, 4, 3)), ((QD, 6, 1), (KDL, 6, 4)), ((QC, 6, 2), (KC, 2, 5)))[n]:
                g = head_gain[:, l, row, :].unsqueeze(1).to_broadcast([P, m1, 64])
                lnk(eng.tensor_tensor(head_view(c1, m1), head_view(c1, m1), g, ALU.mult))
            if n == 1:
                one = [const(k)[:, t * 8:(t + 1) * 8] for k in ("cos1", "sin1")]
                rope_heads(eng, lnk, head_view(QD, 12), 0, 8, one[0], one[1], tmp)
            if n == 2:
                v = proj[:, t, QC:QC + 512].rearrange("p (h r d) -> p h r d", h=8, r=2)
                cos, sin = (const(k)[:, t * 32:(t + 1) * 32].rearrange("p (r d) -> p r d", r=2).unsqueeze(1)
                            .to_broadcast([P, 8, 2, 16]) for k in ("cosax", "sinax"))
                t1 = tmp[:, 0:256].rearrange("p (h r d) -> p h r d", h=8, r=2)
                t2 = tmp[:, 256:512].rearrange("p (h r d) -> p h r d", h=8, r=2)
                rotate(eng, lnk, v[:, :, :, 0:16], v[:, :, :, 16:32], cos, sin, t1, t2)

        @block.sync
        def _(sp):
            def load(u, j):
                sp.dma_start(raw[:, j, :], stream[u]).then_inc(raw_in[j], 16)

            for j in range(NRAW):
                load(j, j)
            turns = N_UNITS // NRAW
            with sp.Fori(1, turns) as i:
                for j in range(NRAW):
                    sp.wait_ge(lo_done, i * NRAW + (j - NRAW + 1))
                    load(i * NRAW + j, j)
            for u in range(turns * NRAW, N_UNITS):
                sp.wait_ge(lo_done, u - NRAW + 1)
                load(u, u % NRAW)
            sp.wait_ge(x_upd, 4 * 11)
            sp.dma_start(out[0].rearrange("(t p) d -> p t d", p=P), X[:, :, :]).then_inc(stored, 16)
            sp.wait_ge(stored, 16)

        @block.tensor
        def _(pe):
            def xt_transposes(name, src):
                for b in range(4):
                    for kk in range(2):
                        for t in range(NT):
                            k = 2 * b + kk
                            ins = pe.transpose(bank[4 + b][:, (kk * 2 + t) * P:(kk * 2 + t + 1) * P],
                                               src[:, t, k * P:(k + 1) * P], ident)
                    ins.then_inc(xt_ps, 1)

            def norm(n):
                pe.wait_ge(xn0, n + 1)
                pe.wait_ge(xn1, n + 1)
                xt_transposes(f"n{n}", xn)

            def token_major(u, name, width, out_bank, first_turn):
                pe.wait_ge(lo_done, u + 1)
                sl = u % 3
                for t in range(NT):
                    dst = out_bank[:, t * 256:t * 256 + width]
                    for k in range(KD):
                        if first_turn is not None and t == 0:
                            pe.wait_ge(xtl, 8 * first_turn + k + 1)
                        tok = slice(t * P, (t + 1) * P)
                        cols = slice(k * 256, k * 256 + width)
                        pe.matmul(dst, xt_hi[:, k, tok], w_hi[:, sl, cols], start=(k == 0), stop=False)
                        pe.matmul(dst, xt_hi[:, k, tok], w_lo[:, sl, cols], start=False, stop=False)
                        ins = pe.matmul(dst, xt_lo[:, k, tok], w_hi[:, sl, cols], start=False, stop=(k == KD - 1))
                ins.then_inc(unit_used, 1)

            def project(stage, u0, blocks, turn):
                p0 = PROJ0[stage]
                for c, width in enumerate(blocks):
                    if c >= 4:
                        pe.wait_ge(pj_evac, p0 + c - 3)
                    token_major(u0 + c, stage, width, bank[c % 4], turn if c == 0 else None)

            def mix_out(m):
                u0 = U[f"mix{m}"]
                turn = TURN[f"m{m}"]
                for c in range(OUT_UNITS):
                    u = u0 + c
                    pe.wait_ge(lo_done, u + 1)
                    sl = u % 3
                    for j in range(2):
                        k = 2 * c + j
                        pe.wait_ge(xtl, 8 * turn + k + 1)
                        for t in range(NT):
                            tok = slice(t * P, (t + 1) * P)
                            for lhs, w, in ((xt_hi, w_hi), (xt_hi, w_lo), (xt_lo, w_hi)):
                                for half in range(2):
                                    cols = slice(j * D + half * 512, j * D + half * 512 + 512)
                                    ins = pe.matmul(bank[2 * t + half][:, :], lhs[:, k, tok], w[:, sl, cols],
                                                    start=(k == 0 and lhs is xt_hi and w is w_hi),
                                                    stop=(k == KD - 1 and lhs is xt_lo))
                    ins.then_inc(unit_used, 1)

            def ffn_gu(f, kind, s, i):
                u = ffn_unit(f, kind, s)
                sl = u % NSPLIT
                pe.wait_ge(lo_done, on(u + 1, 6, i))
                dst = bank[2 * (s % 2) + (0 if kind == "g" else 1)]
                turn = TURN[f"n{FFN_NORM[f]}"]
                for j in range(2):
                    for k in range(KD):
                        if s == 0 and kind == "g" and j == 0:
                            pe.wait_ge(xtl, 8 * turn + k + 1)
                        cols = slice(k * 256 + j * P, k * 256 + (j + 1) * P)
                        o = dst[:, j * S:(j + 1) * S]
                        pe.matmul(o, w_hi[:, sl, cols], xt_hi[:, k, :], start=(k == 0), stop=False)
                        pe.matmul(o, w_hi[:, sl, cols], xt_lo[:, k, :], start=False, stop=False)
                        ins = pe.matmul(o, w_lo[:, sl, cols], xt_hi[:, k, :], start=False, stop=(k == KD - 1))
                ins.then_inc(unit_used, 1)

            def ffn_down(f, s, i):
                u = ffn_unit(f, "d", s)
                sl = u % NSPLIT
                pe.wait_ge(lo_done, on(u + 1, 6, i))
                pe.wait_ge(hl_done, on(f * STEPS + s + 1, 2, i))
                for j in range(2):
                    for t in range(NT):
                        tok = slice(j * S + t * P, j * S + (t + 1) * P)
                        for lhs, w in ((h_hi, w_hi), (h_hi, w_lo), (h_lo, w_hi)):
                            for half in range(2):
                                cols = slice(j * D + half * 512, j * D + half * 512 + 512)
                                ins = pe.matmul(bank[4 + 2 * t + half][:, :], lhs[:, s % 2, tok], w[:, sl, cols],
                                                start=(s == 0 and j == 0 and lhs is h_hi and w is w_hi),
                                                stop=(s == STEPS - 1 and j == 1 and lhs is h_lo))
                ins.then_inc(unit_used, 1)

            def triple(f, s, i):
                if s >= 2:
                    pe.wait_ge(mul_done, on(f * STEPS + s - 1, 2, i))
                ffn_gu(f, "g", s, i)
                ffn_gu(f, "u", s, i)
                if s:
                    ffn_down(f, s - 1, i)

            def ffn(f):
                ffn_steps(pe, f, triple)
                ffn_down(f, STEPS - 1, None)

            def feature_major(stage):
                a0, d0 = FT_A0[stage], FT_D0[stage]
                g0 = a0 + d0
                for g, (srcs, rows, _) in enumerate(ft_groups(stage)):
                    for n, (_, _, o, _) in enumerate(SEC_KINDS):
                        if stage[:3] == "sec" and g == o // 2:
                            pe.wait_ge(ft_ready_p, 3 + 3 * int(stage[3]) + n)
                            if n == 2:
                                pe.wait_ge(ft_ready_d, 3 + int(stage[3]))
                    if g >= 4:
                        if g % 2 == 0:
                            pe.wait_ge(ft_a, a0 + (g - 4) // 2 + 1)
                        else:
                            pe.wait_ge(ft_d, d0 + (g - 4) // 2 + 1)
                    for n, src in enumerate(srcs):
                        for t in range(NT):
                            ins = pe.transpose(bank[g % 4][0:rows, (2 * n + t) * P:(2 * n + t + 1) * P], src(t), ident)
                    ins.then_inc(ft_ps, 1)

            def attention(stage):
                jobs, j0 = heads[stage], JOB0[stage]

                def scores(i):
                    if i >= len(jobs):
                        return
                    if i >= 2:
                        pe.wait_ge(exp_done, 2 * (j0 + i - 1))
                    job, dst = jobs[i], bank[i % 2]
                    if stage[:3] == "sec" and i == 12:
                        pe.wait_ge(na_ready, int(stage[3]) + 1)
                    for qt in range(NT):
                        n = ncols(job, qt)
                        plain = not job["causal"] and job["bias"] is None
                        ins = pe.matmul(dst[:, qt * S:qt * S + n], qT[0:job["d"], job["q"], qt * P:(qt + 1) * P],
                                        kT[0:job["d"], job["k"], 0:n], start=True, stop=plain)
                        if job["causal"]:
                            ins = pe.matmul(dst[:, qt * S + qt * P:qt * S + (qt + 1) * P], ident_b[:, :],
                                            causal_b[:, :], start=False, stop=True)
                        elif not plain:
                            ins = pe.matmul(dst[:, qt * S:qt * S + n], const(job["order"]), job["bias"](qt), start=False,
                                            stop=True)
                    ins.then_inc(s_done, 1)

                def turn_p(i):
                    pe.wait_ge(exp_done, 2 * (j0 + i + 1))
                    if i >= 2:
                        pe.wait_ge(pt_evac, j0 + i - 1)
                    for n, (qt, kt) in enumerate(pt_blocks(jobs[i])):
                        ins = pe.transpose(bank[2 + i % 2][:, n * P:(n + 1) * P], p_of(i % 2, qt, kt * P, (kt + 1) * P),
                                           ident)
                    ins.then_inc(t_done, 1)

                def values(i):
                    if i < 0:
                        return
                    pe.wait_ge(pt_evac, j0 + i + 1)
                    g = i // 4
                    if i % 4 == 0 and g >= 2:
                        pe.wait_ge(o_done, j0 // 4 + g - 1)
                    job = jobs[i]
                    for qt in range(NT):
                        blocks = [(n, kt) for n, (q, kt) in enumerate(pt_blocks(job)) if q == qt]
                        for m, (n, kt) in enumerate(blocks):
                            at = qt * 256 + (i % 4) * 64
                            ins = pe.matmul(bank[4 + g % 2][:, at:at + 64], pts_of(i % 2, n * P, (n + 1) * P),
                                            job["v"](kt), start=(m == 0), stop=(m == len(blocks) - 1))
                    ins.then_inc(pv_done, 1)

                scores(0)
                for i in range(len(jobs)):
                    scores(i + 1)
                    turn_p(i)
                    values(i - 1)
                values(len(jobs) - 1)

            def wait_ft(stage):
                pe.wait_ge(ft_a, FT_A0[stage] + (FT_GROUPS[stage] + 1) // 2)
                pe.wait_ge(ft_d, FT_D0[stage] + FT_GROUPS[stage] // 2)

            def gla():
                pe.wait_ge(pj_evac, 8)
                for c, b in ((HY_GQ, 0), (HY_GK, 1)):
                    for a in range(2):
                        for t in range(NT):
                            ins = pe.transpose(bank[b][:, (a * 2 + t) * P:(a * 2 + t + 1) * P],
                                               proj[:, t, c + a * P:c + (a + 1) * P], ident)
                    ins.then_inc(g_tp, 1)
                for t in range(NT):
                    ins = pe.transpose(bank[2][0:GLA_R, t * P:(t + 1) * P], proj[:, t, HY_GA:HY_GA + GLA_R], ident)
                ins.then_inc(g_tp, 1)
                pe.wait_ge(g_ev, 2)
                for t in range(NT):
                    ins = pe.matmul(bank[3][:, t * 256:(t + 1) * 256], gla_aT[0:GLA_R + 1, t * P:(t + 1) * P], a2[:, :],
                                    start=True, stop=True)
                ins.then_inc(g_z, 1)
                pe.wait_ge(g_la, 1)
                for a in range(2):
                    for t in range(NT):
                        ins = pe.matmul(bank[2][:, (a * 2 + t) * P:(a * 2 + t + 1) * P],
                                        gla_la[:, t * 256 + a * P:t * 256 + (a + 1) * P], const("block_tri"),
                                        start=True, stop=True)
                ins.then_inc(g_b, 1)
                pe.wait_ge(g_qk, 2)
                for t in range(NT):
                    for h in range(GLA_H):
                        r = slice(64 * (h % 2), 64 * (h % 2) + 64)
                        c = (h // 2) * S + t * P
                        at = (2 * t + h // 2) * P
                        ins = pe.matmul(bank[h % 2][:, at:at + P], gla_kd[r, c:c + P], gla_qi[r, c:c + P],
                                        start=True, stop=True)
                ins.then_inc(g_a, 1)
                for t in range(NT):
                    for a in range(2):
                        ins = pe.transpose(bank[2][:, (t * 2 + a) * P:(t * 2 + a + 1) * P],
                                           gla_kd[:, a * S + t * P:a * S + (t + 1) * P], ident)
                ins.then_inc(g_kt, 1)
                pe.wait_ge(g_kd, 1)
                for c in range(3):
                    r = slice(64 * (c % 2), 64 * (c % 2) + 64)
                    t = c // 2
                    for a in range(2):
                        ins = pe.matmul(bank[3 + c][:, a * 256:(a + 1) * 256], gla_kdt[r, (t * 2 + a) * P:(t * 2 + a + 1) * P],
                                        proj[r, t, HY_GV + a * 256:HY_GV + (a + 1) * 256], start=True, stop=True)
                    ins.then_inc(g_kv, 1)
                pe.wait_ge(g_am, 1)
                pe.wait_ge(g_qk, 3)
                pe.wait_ge(g_st, 3)
                qz = gla_qz.rearrange("p (a c i) -> p a c i", a=2, c=4)
                st = gla_st.rearrange("p (a c v) -> p a c v", a=2, c=4)
                for t in range(NT):
                    for h in range(GLA_H):
                        r = slice(64 * (h % 2), 64 * (h % 2) + 64)
                        a = h // 2
                        dst = bank[t + 6 * (1 - h % 2)][:, a * P:(a + 1) * P]
                        n = 4 * (h % 2) + 2 * t + a
                        pe.matmul(dst, gla_am[:, n * P:(n + 1) * P],
                                  proj[:, t, HY_GV + h * P:HY_GV + (h + 1) * P], start=True, stop=False)
                        cs = [c for c in (2 * t, 2 * t + 1) if c > 0]
                        for c in cs:
                            ins = pe.matmul(dst, qz[r, a, c, :], st[r, a, c, :], start=False, stop=(c == cs[-1]))
                ins.then_inc(g_o, 1)

            def mla():
                pe.wait_ge(mla_cn, 4)
                for a in range(2):
                    for t in range(NT):
                        ins = pe.transpose(bank[0][:, (a * 2 + t) * P:(a * 2 + t + 1) * P],
                                           proj[:, t, HY_CQ + a * P:HY_CQ + (a + 1) * P], ident)
                ins.then_inc(mla_tp, 1)
                for t in range(NT):
                    ins = pe.transpose(bank[1][:, t * P:(t + 1) * P], proj[:, t, HY_CKV:HY_CKV + P], ident)
                ins.then_inc(mla_tp, 1)
                pe.wait_ge(mla_cl, 3)
                u = U["uq"]
                pe.wait_ge(lo_done, u + 1)
                sl = u % 3
                for t in range(NT):
                    tok = slice(t * P, (t + 1) * P)
                    for c0, n, b in ((0, 512, 4), (512, 256, 5)):
                        for k in range(2):
                            cols = slice(k * 768 + c0, k * 768 + c0 + n)
                            o = bank[b + 2 * t][:, 0:n]
                            pe.matmul(o, xt_hi[:, k, tok], w_hi[:, sl, cols], start=(k == 0), stop=False)
                            pe.matmul(o, xt_hi[:, k, tok], w_lo[:, sl, cols], start=False, stop=False)
                            ins = pe.matmul(o, xt_lo[:, k, tok], w_hi[:, sl, cols], start=False, stop=(k == 1))
                ins.then_inc(unit_used, 1)
                u = U["ukv"]
                pe.wait_ge(lo_done, u + 1)
                sl = u % 3
                for t in range(NT):
                    tok = slice(t * P, (t + 1) * P)
                    for half in range(2):
                        cols = slice(half * 512, half * 512 + 512)
                        o = bank[2 * t + half][:, :]
                        pe.matmul(o, xt_hi[:, 2, tok], w_hi[:, sl, cols], start=True, stop=False)
                        pe.matmul(o, xt_hi[:, 2, tok], w_lo[:, sl, cols], start=False, stop=False)
                        ins = pe.matmul(o, xt_lo[:, 2, tok], w_hi[:, sl, cols], start=False, stop=True)
                ins.then_inc(unit_used, 1)
                pe.wait_ge(ft_ready_d, 1)
                pe.wait_ge(ft_ready_p, 1)
                feature_major("mla")
                wait_ft("mla")
                attention("mla")

            def compress():
                pe.wait_ge(c_dup, 2)
                for m in range(2):
                    for gp in range(2):
                        for g in (2 * gp, 2 * gp + 1):
                            for t in range(NT):
                                c = ((m * 2 + t) * 4 + g) * P
                                ins = pe.transpose(bank[2 * m + gp][:, ((g % 2) * 2 + t) * P:((g % 2) * 2 + t + 1) * P],
                                                   work[:, c:c + P], ident)
                        ins.then_inc(c_tp, 1)
                pe.wait_ge(c_m, 4)
                pe.wait_ge(c_w, 32)
                for m, (mt, w1) in enumerate(((m_k, prob[:, :]), (m_v, O[:, :, :].rearrange("p t d -> p (t d)")))):
                    pe.wait_ge(c_m, 4 * (m + 1))
                    for l in range(16):
                        ins = pe.matmul(bank[4 + m][:, 0:75], w1[:, l * P:(l + 1) * P],
                                        mt[:, :, 2 * l:2 * l + 225:16], start=(l == 0), stop=(l == 15))
                    ins.then_inc(c_h, 1)
                for m in range(2):
                    pe.wait_ge(c_hid, m + 1)
                    ins = pe.matmul(bank[6][:, m * 64:(m + 1) * 64], hid[m], w2[:, m, :], start=True, stop=True)
                ins.then_inc(c_kc, 1)

            def compressed_attention():
                pe.wait_ge(c_kr, 1)
                pe.transpose(bank[6][0:64, 0:P], kc_tok, ident).then_inc(c_kt, 1)
                pe.wait_ge(c_kcT, 1)
                for t in range(NT):
                    for h in range(NS_H):
                        g, j = h // 4, h % 4
                        ins = pe.matmul(bank[6 + t][:, (j * 4 + g) * 32:(j * 4 + g + 1) * 32],
                                        qT[0:64, h, t * P:(t + 1) * P], kcT_[0:64, g * 32:(g + 1) * 32],
                                        start=True, stop=True)
                ins.then_inc(c_s, 1)
                pe.wait_ge(c_p, 1)
                for t in range(NT):
                    for j in range(4):
                        ins = pe.transpose(bank[6 + t][:, j * P:(j + 1) * P], pc[:, (t * 4 + j) * P:(t * 4 + j + 1) * P],
                                           ident)
                ins.then_inc(c_pt, 1)
                pe.wait_ge(c_pe, 1)
                for t in range(NT):
                    for h in range(NS_H):
                        g, j = h // 4, h % 4
                        r = slice(32 * g, 32 * g + 32)
                        at = (t * 4 + j) * 64
                        ins = pe.matmul(bank[4 + g][:, at:at + 64], pct[r, (t * 4 + j) * P:(t * 4 + j + 1) * P],
                                        vc_tok[r, :], start=True, stop=True, tile_position=(32 * g, 0))
                ins.then_inc(c_pv, 1)

            pe.wait_ge(const_ready, 1)
            norm(0)
            ffn(0)
            norm(1)
            project("hy", U["hy_in"], HY_BLOCKS, TURN["n1"])
            gla()
            mla()
            pe.wait_ge(mix_ready, 1)
            xt_transposes("m0", O)
            mix_out(0)
            norm(2)
            ffn(1)
            norm(3)
            ffn(2)
            norm(4)
            project("nsa", U["nsa_in"], NSA_BLOCKS, TURN["n4"])
            compress()
            pe.wait_ge(ft_ready_d, 2)
            pe.wait_ge(ft_ready_p, 2)
            feature_major("nsa")
            wait_ft("nsa")
            compressed_attention()
            pe.wait_ge(c_gate, 2)
            attention("nsa")
            pe.wait_ge(mix_ready, 2)
            xt_transposes("m1", O)
            mix_out(1)
            norm(5)
            ffn(3)
            for l in range(2):
                norm(6 + 2 * l)
                project(f"sec{l}", U[f"sec_in{l}"], SEC_BLOCKS, TURN[f"n{6 + 2 * l}"])
                pe.wait_ge(pj_evac, PROJ0[f"sec{l}"] + len(SEC_BLOCKS))
                feature_major(f"sec{l}")
                wait_ft(f"sec{l}")
                attention(f"sec{l}")
                pe.wait_ge(mix_ready, 3 + l)
                xt_transposes(f"m{2 + l}", O)
                mix_out(2 + l)
                norm(7 + 2 * l)
                ffn(4 + l)

        @block.scalar
        def _(act):
            own = [0]

            def link(ins):
                own[0] += 1
                ins.then_inc(act_own, 1)
                act.wait_ge(act_own, own[0])

            def split(u, i=None):
                if u >= N_UNITS:
                    return
                sl = u % NSPLIT
                act.wait_ge(raw_in[sl], on(16 * (u // NRAW + 1), 32, i))
                if u >= NSPLIT:
                    act.wait_ge(unit_used, on(u - NSPLIT + 1, 6, i))
                act.activation(w_hi[:, sl, :], raw[:, sl, :], ACT.Copy).then_inc(hi_done, 1)

            def norm(n, between=None):
                r = rms_turn(n)
                for t in range(NT):
                    if n == 0:
                        act.wait_ge(x_in, 16)
                    else:
                        act.wait_ge(x_upd, 4 * r - 2 + 2 * t)
                    act.activation(xn[:, t, :], X[:, t, :], ACT.Square, accum_out=ss[:, t:t + 1]).then_inc(sq_done, 1)
                if between:
                    between()
                act.wait_ge(rstd_done, r + 1)
                act.activation(xn[:, 1, :], X[:, 1, :], ACT.Copy, scale=rstd[:, 1:2]).then_inc(xn1, 1)
                evac_xt(f"n{n}", G_NORM + 8 * n)

            def evac_xt(name, g0):
                q = TURN[name]
                for k in range(KD):
                    act.wait_ge(xt_ps, 4 * q + k // 2 + 1)
                    scale = 1.0 if g0 is None else gcol[:, g0 + k:g0 + k + 1]
                    act.activation(xt_hi[:, k, :], bank[4 + k // 2][:, (k % 2) * S:(k % 2 + 1) * S], ACT.Copy,
                                   scale=scale).then_inc(xth, 1)

            def project(stage, u0, blocks, after=None):
                for c, width in enumerate(blocks):
                    split(u0 + c + NSPLIT)
                    act.wait_ge(unit_used, u0 + c + 1)
                    src = bank[c % 4][:, :].rearrange("p (t n) -> p t n", t=2)
                    act.activation(proj[:, :, c * 256:c * 256 + width], src[:, :, 0:width], ACT.Copy).then_inc(pj_evac, 1)
                    if after:
                        after(c)

            def sec_rms(l, c):
                for n, (col, m, _, last) in enumerate(SEC_KINDS):
                    if c == last:
                        act.wait_ge(pj_evac, PROJ0[f"sec{l}"] + c + 1)
                        if n:
                            act.wait_ge(e_ms, 4 * l + n)
                        for t in range(NT):
                            act.activation(work[:, t * m * 64:(t + 1) * m * 64], proj[:, t, col:col + m * 64],
                                           ACT.Square).then_inc(e_sq, 1)
                    if c == last + (1 if n < 2 else 0):
                        act.wait_ge(e_ms, 4 * l + n + 1)
                        act.activation(head_rms(rstd, n), head_rms(ms, n), ACT.Sqrt).then_inc(e_rt, 1)

            def mix_out(m):
                for c in range(OUT_UNITS):
                    u = U[f"mix{m}"] + c + NSPLIT
                    split(u)

            def triple(f, s, i):
                par = s % 2
                split(ffn_unit(f, "g", s) + NSPLIT, i)
                split(ffn_unit(f, "u", s) + NSPLIT, i)
                act.wait_ge(unit_used, on(ffn_unit(f, "u", s) + 1, 6, i))
                if s >= 2:
                    act.wait_ge(mul_done, on(f * STEPS + s - 1, 2, i))
                if f < 4:
                    act.activation(act_g[:, par, :], bank[2 * par][:, :], ACT.Silu).then_inc(actg_done, 1)
                else:
                    l = f - 4
                    for j in range(2):
                        act.activation(conv_y[:, par, j * S:(j + 1) * S], bank[2 * par][:, j * S:(j + 1) * S],
                                       ACT.Identity, scale=tap(l, 1, s, j, i), bias=tap(l, 3, s, j, i)).then_inc(cv_mid, 1)
                    act.wait_ge(cv_done, on(l * STEPS + s + 1, 2, i))
                    act.activation(act_g[:, par, :], conv_y[:, par, :], ACT.Gelu).then_inc(actg_done, 1)
                act.wait_ge(mul_done, on(f * STEPS + s + 1, 2, i))
                act.activation(h_hi[:, par, :], h_f, ACT.Copy).then_inc(hh_done, 1)
                if s:
                    split(ffn_unit(f, "d", s - 1) + NSPLIT, i)

            def ffn(f):
                ffn_steps(act, f, triple)
                split(ffn_unit(f, "d", STEPS - 1) + NSPLIT)

            def feature_major(stage):
                a0, g0 = FT_A0[stage], FT_A0[stage] + FT_D0[stage]
                for g, (srcs, rows, dst) in enumerate(ft_groups(stage)):
                    if g % 2:
                        continue
                    act.wait_ge(ft_ps, g0 + g + 1)
                    if dst is None:
                        src = bank[g % 4][64:96, 0:S]
                        for h in range(MLA_H):
                            ins = act.activation(kT[64:96, h, :], src, ACT.Copy)
                        ins.then_inc(ft_a, 1)
                    else:
                        src = bank[g % 4][0:rows, :].rearrange("p (h s) -> p h s", h=2)
                        act.activation(dst[0], src, ACT.Copy, scale=ft_scale(stage, g)).then_inc(ft_a, 1)

            def attention(stage):
                jobs, j0 = heads[stage], JOB0[stage]
                for i, job in enumerate(jobs):
                    act.wait_ge(nm_done, j0 + i + 1)
                    if i >= 2:
                        act.wait_ge(t_done, j0 + i - 1)
                    if i % 4 == 0 and i >= 8:
                        act.wait_ge(o_done, j0 // 4 + i // 4 - 1)
                    for qt in range(NT):
                        n = ncols(job, qt)
                        act.activation(p_of(i % 2, qt, 0, n), bank[i % 2][:, qt * S:qt * S + n], ACT.Exp,
                                       bias=negmax[:, i % 4, qt:qt + 1],
                                       accum_out=sums[:, (i // 4) % 2, qt, i % 4:i % 4 + 1]).then_inc(exp_done, 1)

            act.dma_start(X[:, :, :], x[0].rearrange("(t p) d -> p t d", p=P)).then_inc(x_in, 16)
            act.dma_start(cst[:, :], consts).then_inc(cst_in, 16)
            act.dma_start(gcol[:, :], gains).then_inc(gain_in, 16)
            for dst, src in ((pos_i[:, :], positions), (ccol[:, :, :, :], conv),
                             (a2[0:GLA_R, :], gla_a2[0]), (a2[GLA_R:GLA_R + 1, :], gla_ba),
                             (w2[:, 0, :], cmp_w2[0]), (w2[:, 1, :], cmp_w2[1]), (posr[:, :, :], pos_rows),
                             (gla_row[:, :], gla_gain[0].partition_broadcast(P)),
                             (head_gain[:, :, 0:3, :], q_gain2.rearrange("l r d -> (l r d)").partition_broadcast(P)
                              .rearrange("p (l r d) -> p l r d", l=2, r=3)),
                             (head_gain[:, :, 3:6, :], k_gain2.rearrange("l r d -> (l r d)").partition_broadcast(P)
                              .rearrange("p (l r d) -> p l r d", l=2, r=3))):
                act.dma_start(dst, src).then_inc(par_in, 16)
            act.wait_ge(gain_in, 16)
            norm(0, lambda: [split(u) for u in range(NSPLIT)])
            ffn(0)
            act.wait_ge(par_in, 16 * N_PAR)
            act.wait_ge(rope_arg, 1)
            act.activation(rsin[:, :, :], red[:, :, :], ACT.Sin).then_inc(rope_tab, 1)
            act.activation(rcos[:, :, :], tmp48[:, :, :], ACT.Sin).then_inc(rope_tab, 1)
            norm(1)
            project("hy", U["hy_in"], HY_BLOCKS)
            act.wait_ge(g_tp, 1)
            act.activation(gla_q, bank[0][:, :], ACT.Copy, scale=0.125).then_inc(g_ev, 1)
            act.wait_ge(g_tp, 3)
            act.wait_ge(g_evd, 1)
            act.activation(gla_aT[0:GLA_R, :], bank[2][0:GLA_R, 0:S], ACT.Copy).then_inc(g_ev, 1)
            act.wait_ge(g_z, 1)
            link(act.activation(gla_za, bank[3][:, :], ACT.Abs))
            link(act.activation(gla_za, gla_za, ACT.Exp, scale=-1.0))
            act.activation(gla_ln, gla_za, ACT.Ln, bias=1.0).then_inc(g_ln, 1)
            act.wait_ge(g_b, 1)
            act.activation(gla_b, bank[2][:, :], ACT.Copy, scale=1.0 / 16.0).then_inc(g_bt, 1)
            act.wait_ge(g_bt, 1)
            act.activation(gla_eb, gla_b, ACT.Exp).then_inc(g_e, 1)
            act.wait_ge(g_d, 1)
            act.activation(gla_ei, gla_d, ACT.Exp).then_inc(g_e, 1)
            act.activation(gla_ed, gla_d, ACT.Exp, scale=-1.0).then_inc(g_e, 1)
            act.wait_ge(g_kt, 1)
            act.activation(gla_kdt, bank[2][:, :], ACT.Copy).then_inc(g_kd, 1)
            act.activation(gla_sr.rearrange("p (t n) -> p t n", t=2), proj[:, :, HY_GR:HY_GR + 512],
                           ACT.Silu).then_inc(g_sr, 1)
            for n, (c, w) in enumerate(((HY_CQ, 256), (HY_CKV, 128))):
                for t in range(NT):
                    act.activation(prob[:, 0:w], proj[:, t, c:c + w], ACT.Square,
                                   accum_out=ss[:, 8 + 2 * n + t:9 + 2 * n + t]).then_inc(mla_sq, 1)
                    act.wait_ge(mla_sq, 2 * n + t + 1)
            for k in range(3):
                act.wait_ge(mla_tp, 1 if k < 2 else 2)
                src = bank[0][:, k * S:(k + 1) * S] if k < 2 else bank[1][:, 0:S]
                act.activation(xt_hi[:, k, :], src, ACT.Copy, scale=gcol[:, G_Q + k:G_Q + k + 1]).then_inc(mla_ch, 1)
            split(U["uq"] + NSPLIT)
            act.wait_ge(unit_used, U["uq"] + 1)
            act.wait_ge(g_o, 1)
            act.wait_ge(mla_up, 1)
            for t in range(NT):
                for c0, n, b in ((0, 512, 4), (512, 256, 5)):
                    act.activation(work[:, t * 768 + c0:t * 768 + c0 + n], bank[b + 2 * t][:, 0:n], ACT.Copy,
                                   scale=float(MLA_QK) ** -0.5).then_inc(mla_q, 1)
            split(U["ukv"] + NSPLIT)
            feature_major("mla")
            attention("mla")
            evac_xt("m0", None)
            mix_out(0)
            norm(2)
            ffn(1)
            norm(3)
            ffn(2)
            norm(4)
            project("nsa", U["nsa_in"], NSA_BLOCKS)
            act.wait_ge(pj_evac, PROJ0["nsa"] + len(NSA_BLOCKS))
            act.activation(gate[:, :, :], proj[:, :, NS_G:NS_G + 48], ACT.Sigmoid).then_inc(c_gate, 1)
            for m, b in enumerate((4, 5)):
                act.wait_ge(c_b, m + 1)
                dst = hid[m].rearrange("p (g n) -> p g n", g=4)[:, :, 0:NCMP]
                src = bank[b][:, 0:60].rearrange("p (g n) -> p g n", g=4)
                act.activation(dst, src, ACT.Silu, bias=small[:, 0, m:m + 1]).then_inc(c_hid, 1)
            feature_major("nsa")
            act.wait_ge(c_sc, 1)
            act.activation(pc, sc, ACT.Exp).then_inc(c_e, 1)
            attention("nsa")
            evac_xt("m1", None)
            mix_out(1)
            norm(5)
            ffn(3)
            for t in range(NT):
                act.wait_ge(x_upd, 4 * 6 - 2 + 2 * t)
                act.activation(xn[:, t, :], X[:, t, :], ACT.Square, accum_out=ss[:, t:t + 1]).then_inc(sq_done, 1)
            for l in range(2):
                norm(6 + 2 * l)
                project(f"sec{l}", U[f"sec_in{l}"], SEC_BLOCKS, lambda c: sec_rms(l, c))
                feature_major(f"sec{l}")
                attention(f"sec{l}")
                act.wait_ge(o_done, (JOB0[f"sec{l}"] + 16) // 4)
                for t in range(NT):
                    for n, (c, w) in enumerate(((0, 256), (256, 384), (640, 384))):
                        act.activation(work[:, t * 1024 + c:t * 1024 + c + w], O[:, t, c:c + w], ACT.Square,
                                       accum_out=ss[:, 2 * n + t:2 * n + t + 1]).then_inc(e_m, 1)
                evac_xt(f"m{2 + l}", G_OUT + 8 * l)
                mix_out(2 + l)
                norm(7 + 2 * l)
                ffn(4 + l)

        @block.vector
        def _(dve):
            own = [0]

            def link(ins):
                own[0] += 1
                ins.then_inc(dve_own, 1)
                dve.wait_ge(dve_own, own[0])

            def split(u, i=None):
                if u >= N_UNITS:
                    return
                sl = u % NSPLIT
                dve.wait_ge(hi_done, on(u + 1, 6, i))
                dve.tensor_tensor(w_lo[:, sl, :], raw[:, sl, :], w_hi[:, sl, :].bitcast(F32),
                                  ALU.subtract).then_inc(lo_done, 1)

            def mean_squares(r, lo, n, scale):
                return dve.tensor_scalar(ms[:, lo:lo + n], ss[:, lo:lo + n], scale, EPS, ALU.mult, ALU.add)

            def norm(n):
                r = rms_turn(n)
                dve.wait_ge(sq_done, 2 * (r + 1))
                mean_squares(r, 0, 2, 1.0 / D).then_inc(ms_done, 1)
                dve.wait_ge(rstd_done, r + 1)
                dve.tensor_scalar(xn[:, 0, :], X[:, 0, :], rstd[:, 0:1], None, ALU.mult).then_inc(xn0, 1)
                lo_xt(f"n{n}", G_NORM + 8 * n)

            def lo_xt(name, g0):
                q = TURN[name]
                for k in range(KD):
                    dve.wait_ge(xth, 8 * q + 2 * (k // 2) + 2)
                    src = bank[4 + k // 2][:, (k % 2) * S:(k % 2 + 1) * S]
                    hi = xt_hi[:, k, :].bitcast(F32)
                    if g0 is None:
                        ins = dve.tensor_tensor(xt_lo[:, k, :], src, hi, ALU.subtract)
                    else:
                        ins = dve.scalar_tensor_tensor(xt_lo[:, k, :], src, gcol[:, g0 + k:g0 + k + 1], hi,
                                                       ALU.mult, ALU.subtract)
                    ins.then_inc(xtl, 1)

            def project(u0, blocks, after=None):
                for c in range(len(blocks)):
                    split(u0 + c + NSPLIT)
                    if after:
                        after(c)

            def sec_rms(l, c):
                for n, (_, m, o, last) in enumerate(SEC_KINDS):
                    if c == last:
                        dve.wait_ge(e_sq, 6 * l + 2 * n + 2)
                        link(dve.tensor_reduce(head_rms(ss, n), work[:, 0:2 * m * 64].rearrange(
                            "p (t h d) -> p t h d", t=NT, d=64), X_AXIS, ALU.add))
                        dve.tensor_scalar(head_rms(ms, n), head_rms(ss, n), 1.0 / 64, EPS, ALU.mult,
                                          ALU.add).then_inc(e_ms, 1)
                    if c == last + (1 if n < 2 else 0):
                        dve.wait_ge(e_rt, 3 * l + n + 1)
                        r, q = head_rms(rstd, n), head_rms(ss, n)
                        link(dve.reciprocal(r, r))
                        link(dve.tensor_tensor(q, r, r, ALU.mult))
                        link(dve.tensor_tensor(q, q, head_rms(ms, n), ALU.mult))
                        link(dve.tensor_scalar(q, q, -0.5, 1.5, ALU.mult, ALU.add))
                        dve.tensor_tensor(r, r, q, ALU.mult).then_inc(e_rs, 1)
                        dve.wait_ge(e_rs, 4 * l + n + 1)
                if c == SEC_KINDS[2][3] + 1:
                    sec_heads(dve, link, 2, 0, l, QT[:, 2560:3072])
                    dve.sem_inc(ft_ready_d, 1)

            def update_x(scale, first_bank):
                for j in range(4):
                    t, half = j // 2, j % 2
                    dst = X[:, t, half * 512:(half + 1) * 512]
                    dve.scalar_tensor_tensor(dst, bank[first_bank + j][:, :], scale, dst, ALU.mult, ALU.add).then_inc(x_upd, 1)

            def mix_out(m):
                u0 = U[f"mix{m}"]
                for c in range(OUT_UNITS):
                    if c == OUT_UNITS - 1:
                        dve.wait_ge(unit_used, u0 + OUT_UNITS)
                        update_x(1.0, 0)
                    split(u0 + c + NSPLIT)

            def triple(f, s, i):
                par = s % 2
                split(ffn_unit(f, "g", s) + NSPLIT, i)
                split(ffn_unit(f, "u", s) + NSPLIT, i)
                if f >= 4:
                    l = f - 4
                    for j in range(2):
                        y, g = conv_y[:, par, j * S:(j + 1) * S], bank[2 * par][:, j * S:(j + 1) * S]
                        dve.wait_ge(cv_mid, on(2 * (l * STEPS + s) + 2, 4, i))
                        dve.scalar_tensor_tensor(y[:, 1:S], g[:, 0:S - 1], tap(l, 0, s, j, i), y[:, 1:S], ALU.mult,
                                                 ALU.add).then_inc(cv_left, 1)
                    for j in range(2):
                        y, g = conv_y[:, par, j * S:(j + 1) * S], bank[2 * par][:, j * S:(j + 1) * S]
                        dve.wait_ge(cv_left, on(2 * (l * STEPS + s) + j + 1, 4, i))
                        ins = dve.scalar_tensor_tensor(y[:, 0:S - 1], g[:, 1:S], tap(l, 2, s, j, i), y[:, 0:S - 1],
                                                       ALU.mult, ALU.add)
                    ins.then_inc(cv_done, 1)
                dve.wait_ge(actg_done, on(f * STEPS + s + 1, 2, i))
                dve.wait_ge(unit_used, on(ffn_unit(f, "u", s) + 1, 6, i))
                if f or s:
                    dve.wait_ge(hl_done, on(f * STEPS + s, 2, i))
                dve.tensor_tensor(h_f, act_g[:, par, :], bank[2 * par + 1][:, :], ALU.mult).then_inc(mul_done, 1)
                dve.wait_ge(hh_done, on(f * STEPS + s + 1, 2, i))
                dve.tensor_tensor(h_lo[:, par, :], h_f, h_hi[:, par, :].bitcast(F32), ALU.subtract).then_inc(hl_done, 1)
                if s:
                    split(ffn_unit(f, "d", s - 1) + NSPLIT, i)

            def ffn(f):
                ffn_steps(dve, f, triple)
                dve.wait_ge(unit_used, U[f"ffn{f}"] + FFN_UNITS)
                update_x(0.5 if f < 4 else 1.0, 4)
                split(ffn_unit(f, "d", STEPS - 1) + NSPLIT)

            def feature_major(stage):
                d0, g0 = FT_D0[stage], FT_A0[stage] + FT_D0[stage]
                for g, (srcs, rows, dst) in enumerate(ft_groups(stage)):
                    if g % 2 == 0:
                        continue
                    dve.wait_ge(ft_ps, g0 + g + 1)
                    src = bank[g % 4][0:rows, :].rearrange("p (h s) -> p h s", h=2)
                    dve.tensor_scalar(dst[0], src, ft_scale(stage, g), None, ALU.mult).then_inc(ft_d, 1)

            def attention(stage, finish):
                jobs, j0 = heads[stage], JOB0[stage]

                def maxima(i):
                    if i >= len(jobs):
                        return
                    dve.wait_ge(s_done, j0 + i + 1)
                    b, job = bank[i % 2], jobs[i]
                    if job["causal"]:
                        for qt in range(NT):
                            ins = dve.tensor_reduce(negmax[:, i % 4, qt:qt + 1], b[:, qt * S:qt * S + ncols(job, qt)],
                                                    X_AXIS, ALU.max, negate=True)
                    else:
                        ins = dve.tensor_reduce(negmax[:, i % 4, :], b[:, :].rearrange("p (q s) -> p q s", q=2),
                                                X_AXIS, ALU.max, negate=True)
                    ins.then_inc(nm_done, 1)

                def evac(i):
                    dve.wait_ge(t_done, j0 + i + 1)
                    if i >= 2:
                        dve.wait_ge(pv_done, j0 + i - 1)
                    n = P * len(pt_blocks(jobs[i]))
                    dve.tensor_copy(pts_of(i % 2, 0, n), bank[2 + i % 2][:, 0:n]).then_inc(pt_evac, 1)

                def group_out(g):
                    dve.wait_ge(pv_done, j0 + 4 * g + 4)
                    dve.wait_ge(exp_done, 2 * (j0 + 4 * g + 4))
                    gp = g % 2
                    link(dve.reciprocal(rsum[:, gp, :, :], sums[:, gp, :, :]))
                    pv = bank[4 + gp][:, :].rearrange("p (t h d) -> p t h d", t=2, h=4)
                    finish(g, gp, pv)

                maxima(0)
                for i in range(len(jobs)):
                    maxima(i + 1)
                    evac(i)
                    if i % 4 == 1 and i >= 5:
                        group_out((i - 5) // 4)
                group_out(len(jobs) // 4 - 1)

            def sec_out(g, gp, pv):
                plain_out(3 - g, gp, pv)

            def plain_out(g, gp, pv):
                dst = O[:, :, g * 256:(g + 1) * 256].rearrange("p t (h d) -> p t h d", h=4)
                r = rsum[:, gp, :, :].unsqueeze(3).to_broadcast([P, 2, 4, 64])
                dve.tensor_tensor(dst, pv, r, ALU.mult).then_inc(o_done, 1)

            def nsa_out(g, gp, pv):
                br, h0 = g // 4, (g % 4) * 4
                gt = gate[:, :, :].rearrange("p t (h b) -> p t h b", b=3)[:, :, h0:h0 + 4, 1 + br]
                link(dve.tensor_tensor(rsum[:, gp, :, :], rsum[:, gp, :, :], gt, ALU.mult))
                r = rsum[:, gp, :, :].unsqueeze(3).to_broadcast([P, 2, 4, 64])
                t_ = work[:, 0:512].rearrange("p (t h d) -> p t h d", t=2, h=4)
                link(dve.tensor_tensor(t_, pv, r, ALU.mult))
                dst = O[:, :, h0 * 64:h0 * 64 + 256].rearrange("p t (h d) -> p t h d", h=4)
                dve.tensor_tensor(dst, dst, t_, ALU.add).then_inc(o_done, 1)
                dve.wait_ge(o_done, JOB0["nsa"] // 4 + g + 1)

            dve.wait_ge(cst_in, 16)
            dve.tensor_copy(ident_b[:, :], ident)
            dve.tensor_copy(causal_b[:, :], const("causal")).then_inc(const_ready, 1)
            norm(0)
            for u in range(NSPLIT):
                split(u)
            dve.wait_ge(par_in, 16 * N_PAR)
            link(dve.tensor_scalar(head_gain[:, :, 0:3, :], head_gain[:, :, 0:3, :], 0.125, None, ALU.mult))
            link(dve.tensor_copy(pos_f[:, :], pos_i[:, :]))
            fr = const("freq")
            for j in range(3):
                link(dve.tensor_scalar(ang[:, j, :], fr, pos_f[:, j:j + 1], None, ALU.mult))
            TWO_PI = 2 * np.pi
            C1 = 6.28125
            C2 = float(np.float32(np.round((TWO_PI - C1) * 2 ** 20) / 2 ** 20))
            C3 = float(np.float32(TWO_PI - C1 - C2))
            MAGIC = 1.5 * 2 ** 23

            def reduced(dst, shift):
                k = rsin[:, :, :]
                link(dve.tensor_scalar(k, ang[:, :, :], float(1 / TWO_PI), 0.25 * shift, ALU.mult, ALU.add))
                link(dve.tensor_scalar(k, k, MAGIC, MAGIC, ALU.add, ALU.subtract))
                link(dve.scalar_tensor_tensor(dst, k, -C1, ang[:, :, :], ALU.mult, ALU.add))
                link(dve.scalar_tensor_tensor(dst, k, -C2, dst, ALU.mult, ALU.add))
                link(dve.scalar_tensor_tensor(dst, k, -C3, dst, ALU.mult, ALU.add))
                if shift:
                    link(dve.tensor_scalar(dst, dst, float(np.pi / 2), None, ALU.add))
                link(dve.tensor_scalar(dst, dst, 3.1415925, -3.1415925, ALU.min, ALU.max))

            reduced(tmp48[:, :, :], 1)
            reduced(red[:, :, :], 0)
            dve.sem_inc(rope_arg, 1)
            ffn(0)
            norm(1)
            project(U["hy_in"], HY_BLOCKS)
            dve.wait_ge(pj_evac, 8)
            dve.memset(gla_aT[0:32, :], 1.0).then_inc(g_evd, 1)
            dve.memset(gla_qz, 0.0).then_inc(g_evd, 1)
            dve.wait_ge(g_tp, 2)
            dve.tensor_copy(gla_k, bank[1][:, :]).then_inc(g_evd, 1)
            dve.wait_ge(g_ln, 1)
            dve.scalar_tensor_tensor(gla_la, bank[3][:, :], 0.0, gla_ln, ALU.min, ALU.subtract).then_inc(g_la, 1)
            dve.wait_ge(g_bt, 1)
            b4 = chunks(gla_b)
            last = b4[:, :, :, 63:64].to_broadcast([P, 2, 4, 64])
            dve.tensor_tensor(chunks(gla_d), b4, last, ALU.subtract).then_inc(g_d, 1)
            dve.wait_ge(g_e, 3)
            dve.wait_ge(g_evd, 3)
            dve.tensor_tensor(gla_qi, gla_q, gla_ei, ALU.mult).then_inc(g_qk, 1)
            dve.tensor_tensor(gla_kd, gla_k, gla_ed, ALU.mult).then_inc(g_qk, 1)
            qz = gla_qz.rearrange("p (a c i) -> p a c i", a=2, c=4)
            for half in range(2):
                dst = qz[:, :, half:4:2, half * 64:half * 64 + 64]
                ins = dve.tensor_tensor(dst, chunks(gla_q)[:, :, half:4:2, :], chunks(gla_eb)[:, :, half:4:2, :],
                                        ALU.mult)
            ins.then_inc(g_qk, 1)
            dve.wait_ge(g_a, 1)
            tri = const("block_tri").unsqueeze(1).to_broadcast([P, 4, P])
            for t in range(NT):
                ins = dve.tensor_tensor(gla_am[:, t * 512:(t + 1) * 512].rearrange("p (h i) -> p h i", h=4),
                                        bank[t][:, :].rearrange("p (h i) -> p h i", h=4), tri, ALU.mult)
            ins.then_inc(g_am, 1)
            st = gla_st.rearrange("p (a c v) -> p a c v", a=2, c=4)
            eb = chunks(gla_eb)
            for c in range(3):
                dve.wait_ge(g_kv, c + 1)
                if c:
                    dve.wait_ge(g_st, c)
                for a in range(2):
                    for hh in range(2):
                        r = slice(64 * hh, 64 * hh + 64)
                        kv = bank[3 + c][r, a * 256 + hh * P:a * 256 + (hh + 1) * P]
                        if c == 0:
                            ins = dve.tensor_copy(st[r, a, 1, :], kv)
                        else:
                            ins = dve.scalar_tensor_tensor(st[r, a, c + 1, :], st[r, a, c, :], eb[r, a, c, 63:64], kv,
                                                           ALU.mult, ALU.add)
                ins.then_inc(g_st, 1)
            dve.wait_ge(g_o, 1)
            gsq = QT[:, 0:1024]
            o_gla = gla_qz.rearrange("p (t a e v) -> p t a e v", t=2, a=2, e=2)
            for t in range(NT):
                for e, b in ((0, bank[6 + t]), (1, bank[t])):
                    link(dve.tensor_copy(o_gla[:, t, :, e, :], b[:, 0:256].rearrange("p (a v) -> p a v", a=2)))
            link(dve.tensor_tensor(gsq, gla_qz, gla_qz, ALU.mult))
            link(dve.tensor_reduce(ss[:, 16:24], gsq.rearrange("p (h d) -> p h d", d=P), X_AXIS, ALU.add))
            mean_squares(0, 16, 8, 1.0 / GLA_DV).then_inc(g_ms, 1)
            dve.wait_ge(g_rs, 1)
            o8 = gla_qz.rearrange("p (h d) -> p h d", d=P)
            link(dve.tensor_tensor(o8, o8, rstd[:, 16:24].unsqueeze(2).to_broadcast([P, 8, P]), ALU.mult))
            link(dve.tensor_tensor(o8, o8, gla_row[:, :].unsqueeze(1).to_broadcast([P, 8, P]), ALU.mult))
            dve.wait_ge(g_sr, 1)
            dve.tensor_tensor(O[:, :, 512:1024], gla_qz.rearrange("p (t n) -> p t n", t=2),
                              gla_sr.rearrange("p (t n) -> p t n", t=2), ALU.mult).then_inc(mla_up, 1)
            dve.wait_ge(mla_sq, 4)
            link(mean_squares(0, 8, 2, 1.0 / 256))
            mean_squares(0, 10, 2, 1.0 / 128).then_inc(mla_ms, 1)
            dve.wait_ge(mla_rs, 1)
            for n, (c, w) in enumerate(((HY_CQ, 256), (HY_CKV, 128))):
                for t in range(NT):
                    v = proj[:, t, c:c + w]
                    dve.tensor_scalar(v, v, rstd[:, 8 + 2 * n + t:9 + 2 * n + t], None, ALU.mult).then_inc(mla_cn, 1)
            for k in range(3):
                dve.wait_ge(mla_ch, 2 if k < 2 else 3)
                src = bank[0][:, k * S:(k + 1) * S] if k < 2 else bank[1][:, 0:S]
                dve.scalar_tensor_tensor(xt_lo[:, k, :], src, gcol[:, G_Q + k:G_Q + k + 1], xt_hi[:, k, :].bitcast(F32),
                                         ALU.mult, ALU.subtract).then_inc(mla_cl, 1)
            split(U["uq"] + NSPLIT)
            dve.wait_ge(unit_used, U["ukv"] + 1)
            for t in range(NT):
                for half in range(2):
                    link(dve.tensor_copy(work[:, 2048 + t * 1024 + half * 512:2048 + t * 1024 + half * 512 + 512],
                                         bank[2 * t + half][:, :]))
            split(U["ukv"] + NSPLIT)
            dve.wait_ge(mla_q, 4)
            dve.wait_ge(rope_tab, 2)
            for t in range(NT):
                v = work[:, t * 768:(t + 1) * 768].rearrange("p (h d) -> p h d", h=MLA_H)
                rope_heads(dve, link, v, MLA_NOPE, 16, rcos[:, t, 0:16], rsin[:, t, 0:16], prob[:, 0:1024])
            dve.sem_inc(ft_ready_d, 1)
            feature_major("mla")
            attention("mla", plain_out)
            dve.wait_ge(o_done, 2)
            dve.sem_inc(mix_ready, 1)
            lo_xt("m0", None)
            mix_out(0)
            norm(2)
            ffn(1)
            norm(3)
            ffn(2)
            norm(4)
            project(U["nsa_in"], NSA_BLOCKS)
            dve.wait_ge(c_dup, 2)
            for m, mt in enumerate((m_k, m_v)):
                if m == 1:
                    dve.wait_ge(c_tp, 4)
                link(dve.memset(mt[:, 4, :], 0.0))
                link(dve.tensor_copy(mt[:, 4, 0:32:2], posr[:, m, :]))
                for gp in range(2):
                    dve.wait_ge(c_tp, 2 * m + gp + 1)
                    src = bank[2 * m + gp][:, :].rearrange("p (g s) -> p g s", g=2)
                    dve.tensor_copy(mt[0:64, 2 * gp:2 * gp + 2, :], src[0:64, :, :]).then_inc(c_m, 1)
                    dve.tensor_copy(mt[64:128, 2 * gp:2 * gp + 2, 0:S - 1], src[64:128, :, 1:S]).then_inc(c_m, 1)
            for m in range(2):
                dve.wait_ge(c_h, m + 1)
                dve.memset(hid[m], 0.0)
                dve.tensor_copy(small[:, 0, m:m + 1], bank[4 + m][:, 60:61]).then_inc(c_b, 1)
            dve.wait_ge(c_kc, 1)
            link(dve.tensor_copy(kc_tok, bank[6][:, 0:64]))
            link(dve.tensor_copy(vc_tok, bank[6][:, 64:128]))
            rope_heads(dve, link, kc_tok.rearrange("p (h d) -> p h d", h=1), 0, 32, rcos[:, 2, 16:48],
                       rsin[:, 2, 16:48], rope_t)
            dve.sem_inc(c_kr, 1)
            for c, n in ((NS_Q, 16), (NS_KS, 4), (NS_KW, 4)):
                v = proj[:, 0, c:c + n * 64].rearrange("p (h d) -> p h d", h=n)
                rope_heads(dve, link, v, 0, 32, rcos[:, 0, 16:48], rsin[:, 0, 16:48], QT[:, 1024:2048])
            dve.sem_inc(ft_ready_d, 1)
            feature_major("nsa")
            dve.wait_ge(c_kt, 1)
            dve.tensor_copy(kcT_[0:64, :], bank[6][0:64, 0:P]).then_inc(c_kcT, 1)
            dve.wait_ge(c_s, 1)
            s4 = sc.rearrange("p (t h n) -> p t h n", t=2, n=32)
            p4 = pc.rearrange("p (t h n) -> p t h n", t=2, n=32)
            add = const("cmp_add").rearrange("p (t n) -> p t n", t=2)
            keep = const("cmp_01").rearrange("p (t n) -> p t n", t=2)
            for t in range(NT):
                link(dve.tensor_tensor(s4[:, t], bank[6 + t][:, :].rearrange("p (h n) -> p h n", n=32),
                                       add[:, t, :].unsqueeze(1).to_broadcast([P, 16, 32]), ALU.add))
            link(dve.tensor_reduce(small[:, 1, :], sc.rearrange("p (h n) -> p h n", n=32), X_AXIS, ALU.max))
            s3 = sc.rearrange("p (h n) -> p h n", n=32)
            dve.tensor_tensor(s3, s3, small[:, 1, :].unsqueeze(2).to_broadcast([P, 32, 32]), ALU.subtract)\
               .then_inc(c_sc, 1)
            dve.wait_ge(c_e, 1)
            for t in range(NT):
                link(dve.tensor_tensor(p4[:, t], p4[:, t], keep[:, t, :].unsqueeze(1).to_broadcast([P, 16, 32]),
                                       ALU.mult))
            dve.tensor_reduce(small[:, 2, :], pc.rearrange("p (h n) -> p h n", n=32), X_AXIS, ALU.add).then_inc(c_p, 1)
            dve.wait_ge(c_p, 1)
            link(dve.tensor_scalar(small[:, 2, :], small[:, 2, :], TINY, None, ALU.max))
            link(dve.reciprocal(small[:, 3, :], small[:, 2, :]))
            dve.wait_ge(c_gate, 1)
            for t in range(NT):
                coef = small[:, 1, t * 16:(t + 1) * 16].rearrange("p (g j) -> p g j", g=4)
                inv = small[:, 3, t * 16:(t + 1) * 16].rearrange("p (j g) -> p g j", j=4)
                gt = gate[:, t, :].rearrange("p (g j b) -> p g j b", g=4, b=3)[:, :, :, 0]
                link(dve.tensor_tensor(coef, inv, gt, ALU.mult))
            dve.wait_ge(c_pt, 1)
            for t in range(NT):
                ins = dve.tensor_copy(pct[:, t * 512:(t + 1) * 512], bank[6 + t][:, :])
            ins.then_inc(c_pe, 1)
            dve.wait_ge(c_pv, 1)
            for t in range(NT):
                for g in range(NS_GR):
                    h0 = t * 16 + g * 4
                    dst = O[:, t, g * 256:(g + 1) * 256].rearrange("p (h d) -> p h d", h=4)
                    src = bank[4 + g][:, t * 256:(t + 1) * 256].rearrange("p (h d) -> p h d", h=4)
                    link(dve.tensor_tensor(dst, src, small[:, 1, h0:h0 + 4].unsqueeze(2).to_broadcast([P, 4, 64]),
                                           ALU.mult))
            dve.sem_inc(c_gate, 1)
            attention("nsa", nsa_out)
            dve.sem_inc(mix_ready, 1)
            lo_xt("m1", None)
            mix_out(1)
            norm(5)
            ffn(3)
            dve.wait_ge(sq_done, 2 * 7)
            mean_squares(6, 0, 2, 1.0 / D).then_inc(ms_done, 1)
            dve.wait_ge(rstd_done, 7)
            dve.wait_ge(f_in, 16)
            frow = O[:, 0, :]
            for t in range(NT):
                dve.scalar_tensor_tensor(X[:, t, :], X[:, t, :], rstd[:, t:t + 1], frow, ALU.mult,
                                         ALU.mult).then_inc(x_upd, 2)
            for l in range(2):
                norm(6 + 2 * l)
                project(U[f"sec_in{l}"], SEC_BLOCKS, lambda c: sec_rms(l, c))
                feature_major(f"sec{l}")
                attention(f"sec{l}", sec_out)
                dve.wait_ge(e_m, 6 * (l + 1))
                for n, w in enumerate((256, 384, 384)):
                    link(dve.tensor_scalar(ms[:, 2 * n:2 * n + 2], ss[:, 2 * n:2 * n + 2], 1.0 / w, EPS, ALU.mult,
                                           ALU.add))
                dve.sem_inc(e_ms, 1)
                dve.wait_ge(e_rs, 4 * l + 4)
                for t in range(NT):
                    for n, (c, w) in enumerate(((0, 256), (256, 384), (640, 384))):
                        v = O[:, t, c:c + w]
                        link(dve.tensor_scalar(v, v, rstd[:, 2 * n + t:2 * n + t + 1], None, ALU.mult))
                dve.sem_inc(mix_ready, 1)
                lo_xt(f"m{2 + l}", G_OUT + 8 * l)
                mix_out(2 + l)
                norm(7 + 2 * l)
                ffn(4 + l)

        @block.gpsimd
        def _(pool):
            own = [0]

            def link(ins):
                own[0] += 1
                ins.then_inc(pool_own, 1)
                pool.wait_ge(pool_own, own[0])

            def inv_sqrt(lo, n):
                return pool.tensor_tensor(rstd[:, lo:lo + n], ms[:, lo:lo + n], neg_half[:, lo:lo + n], ALU.pow)

            def norm(r):
                pool.wait_ge(ms_done, r + 1)
                inv_sqrt(0, 2).then_inc(rstd_done, 1)

            def fetch_bias(l):
                for r2 in range(2):
                    for qt in range(NT):
                        for h in range(4):
                            at = rpb2[l, h, 7 - (2 * qt + r2), 15:16]
                            src = bass.AP(tensor=at.tensor, offset=at.offset - (GRID - 1), ap=[[1, 64], [31, 4], [1, 64]])
                            pool.dma_start(na_bias[64 * r2:64 * r2 + 64, qt, h, :], src).then_inc(b_in, 16)

            def mask_bias(l):
                pool.wait_ge(b_in, 256 * (l + 1))
                v = work[:, 2048:4096].rearrange("p (n c) -> p n c", c=64)
                m = const("na_mask").unsqueeze(1).to_broadcast([P, 32, 64])
                pool.tensor_tensor(v, v, m, ALU.add).then_inc(na_ready, 1)

            pool.wait_ge(cst_in, 16)
            link(pool.memset(neg_half[:, :], -0.5))
            norm(0)
            norm(1)
            pool.wait_ge(g_ms, 1)
            inv_sqrt(16, 8).then_inc(g_rs, 1)
            pool.wait_ge(pj_evac, 8)
            pool.wait_ge(rope_tab, 2)
            for t in range(NT):
                v = proj[:, t, HY_KR:HY_KR + 32].rearrange("p (h d) -> p h d", h=1)
                rope_heads(pool, link, v, 0, 16, rcos[:, t, 0:16], rsin[:, t, 0:16], small[:, 2, :])
            pool.sem_inc(ft_ready_p, 1)
            pool.wait_ge(mla_ms, 1)
            inv_sqrt(8, 4).then_inc(mla_rs, 1)
            for r in (2, 3, 4):
                norm(r)
                if r == 2:
                    for m, dst in enumerate((prob[:, :], O[:, :, :].rearrange("p t d -> p (t d)"))):
                        pool.dma_start(dst, cmp_w1[m]).then_inc(c_w, 16)
            pool.wait_ge(pj_evac, 8 + 11)
            for m, c in enumerate((NS_KC, NS_VC)):
                for t in range(NT):
                    src = proj[:, t, c:c + 256].rearrange("p (g d) -> p g d", g=4)
                    for e in range(2):
                        ins = pool.tensor_copy(dup[:, m, t, :, e, :], src)
                ins.then_inc(c_dup, 1)
            for c, n in ((NS_Q, 16), (NS_KS, 4), (NS_KW, 4)):
                v = proj[:, 1, c:c + n * 64].rearrange("p (h d) -> p h d", h=n)
                rope_heads(pool, link, v, 0, 32, rcos[:, 1, 16:48], rsin[:, 1, 16:48], QT[:, 2048:3072])
            pool.sem_inc(ft_ready_p, 1)
            norm(5)
            pool.dma_start(O[:, 0, :], final_gain.partition_broadcast(P)).then_inc(f_in, 16)
            norm(6)
            for l in range(2):
                norm(7 + 2 * l)
                fetch_bias(l)
                for n in range(3):
                    pool.wait_ge(e_rs, 4 * l + n + 1)
                    for t in ((0, 1) if n < 2 else (1,)):
                        sec_heads(pool, link, n, t, l, QT[:, 3072:4096])
                    pool.sem_inc(ft_ready_p, 1)
                mask_bias(l)
                pool.wait_ge(e_ms, 4 * l + 4)
                inv_sqrt(0, 6).then_inc(e_rs, 1)
                norm(8 + 2 * l)


def _stream(a):
    s = np.zeros((N_UNITS, P, UNIT), np.float32)

    def columns(u, w, c0, n):
        k = w.shape[0] // P
        s[u].reshape(P, k, UNIT // k)[:, :, 0:n] = w[:, c0:c0 + n].reshape(k, P, n).transpose(1, 0, 2)

    def rows(u, w, r0):
        s[u].reshape(P, 2, D)[:] = w[r0:r0 + 2 * P].reshape(2, P, D).transpose(1, 0, 2)

    def ffn(f, gate, up, down):
        u0 = U[f"ffn{f}"]
        for t in range(STEPS):
            g = u0 + max(3 * t - 1, 0)
            columns(g, gate, 256 * t, 256)
            columns(g + 1, up, 256 * t, 256)
            rows(u0 + (FFN_UNITS - 1 if t == STEPS - 1 else 3 * t + 4), down, 256 * t)

    def project(u0, w, blocks):
        for c, n in enumerate(blocks):
            columns(u0 + c, w, 256 * c, n)

    for f in range(4):
        ffn(f, *(a[n][f // 2, f % 2] for n in ("ffn_w_gate", "ffn_w_up", "ffn_w_down")))
    at = dict(zip(SEC_W, np.cumsum([0] + list(SEC_W.values()))))
    sec_cols = np.concatenate([at[m] + np.arange(SEC_W[m]) for m in SEC_ORDER])
    for l in range(2):
        gu = a["w_gate_up_2"][l]
        ffn(4 + l, gu[:, :D_FF], gu[:, D_FF:], a["w_down_2"][l])
        project(U[f"sec_in{l}"], a["w_in_2"][l][:, sec_cols], SEC_BLOCKS)
    project(U["hy_in"], a["hy_w_in"][0], HY_BLOCKS)
    project(U["nsa_in"], a["nsa_w_in"][0], NSA_BLOCKS)
    s[U["uq"]][:, 0:1536] = a["mla_w_uq"][0].reshape(2, P, 768).transpose(1, 0, 2).reshape(P, 1536)
    s[U["ukv"]][:, 0:1024] = a["mla_w_ukv"][0]
    for m, w in enumerate((a["hy_w_out"][0], a["nsa_w_out"][0], a["w_out_2"][0], a["w_out_2"][1])):
        for c in range(OUT_UNITS):
            rows(U[f"mix{m}"] + c, w, 256 * c)
    return s


def _lay_out(a):
    def cols(v):
        return np.ascontiguousarray(v.reshape(-1, P).T)

    norms = [a["ffn_norm"][0, 0], a["mix_norm"][0], a["ffn_norm"][0, 1], a["ffn_norm"][1, 0], a["mix_norm"][1],
             a["ffn_norm"][1, 1], a["norm1_g_2"][0], a["norm2_g_2"][0], a["norm1_g_2"][1], a["norm2_g_2"][1]]
    gains = np.concatenate([cols(np.stack(norms)), cols(a["out_norm_g_2"]), cols(a["mla_q_norm"]),
                            cols(a["mla_kv_norm"])], 1)
    conv = np.concatenate([a["conv_w_2"], a["conv_b_2"][:, None]], 1).reshape(2, 4, D_FF // P, P).transpose(3, 0, 1, 2)
    pos = a["positions"][0]
    places = np.zeros((P, 3), pos.dtype)
    places[:, 0], places[:, 1] = pos[:P], pos[P:]
    for g in range(NS_GR):
        places[32 * g:32 * g + NCMP, 2] = pos[CMP_LEN - 1::CMP_STRIDE][:NCMP]
    rows = np.stack([a[n][0].reshape(16, P).T for n in ("nsa_pos_k", "nsa_pos_v")], 1)
    w1 = np.stack([a[n][0].reshape(16, P, P).transpose(1, 0, 2).reshape(P, 2048) for n in ("nsa_ck_w1", "nsa_cv_w1")])
    w2 = np.stack([a["nsa_ck_w2"][0], a["nsa_cv_w2"][0]])
    return {"stream": _stream(a), "consts": shape_constants(), "gains": gains, "conv": conv, "x": a["x"],
            "positions": places, "pos_rows": rows, "cmp_w1": w1, "cmp_w2": w2, "final_gain": a["final_norm"],
            "gla_gain": a["gla_out_norm"], "gla_a2": a["gla_w_a2"], "gla_ba": a["gla_b_a"],
            "q_gain2": a["q_norm_g_2"], "k_gain2": a["k_norm_g_2"], "rpb2": a["rpb_2"]}


def kernel(**inputs):
    import concourse.bacc as _bacc
    from concourse.bass_utils import run_bass_kernel_spmd as _run

    nc = _bacc.Bacc("TRN2", target_bir_lowering=False, num_devices=1)
    arrays, args = {}, []
    for name, v in _lay_out({k: np.asarray(v) for k, v in inputs.items()}).items():
        v = np.ascontiguousarray(v)
        arrays[f"in_{name}"] = v
        args.append(nc.dram_tensor(f"in_{name}", v.shape, mybir.dt.from_np(v.dtype), kind="ExternalInput").ap())
    args.append(nc.dram_tensor("out_0", (1, S, D), F32, kind="ExternalOutput").ap())
    build(nc, *args)
    r = _run(nc, [arrays], core_ids=[0])
    return r.results[0]["out_0"]
```

```python
from contextlib import ExitStack

import numpy as np

import concourse.bass as bass
from concourse import mybir

F32 = mybir.dt.float32
F32R = mybir.dt.float32r
BF16 = mybir.dt.bfloat16
I32 = mybir.dt.int32
ALU = mybir.AluOpType
ACT = mybir.ActivationFunctionType
X_AXIS = mybir.AxisListType.X

P = 128
S = 256
NT = S // P
D = 1024
KD = D // P
D_FF = 2816
STEPS = D_FF // 256
EPS = 1e-6
NEG = -1e30
TINY = 1e-30

UNIT = 2048
S_BANKS = (0, 1, 6)
NRAW = 3
NSPLIT = 3

HY_CQ, HY_CKV, HY_KR, HY_GQ, HY_GK, HY_GV, HY_GA, HY_GR, HY_IN = 0, 256, 384, 416, 672, 928, 1440, 1456, 1968
MLA_H, MLA_NOPE, MLA_ROPE, MLA_QK = 8, 64, 32, 96
GLA_H, GLA_DV, GLA_C, GLA_R = 4, 128, 64, 16
NS_Q, NS_KC, NS_VC, NS_KS, NS_VS, NS_KW, NS_VW, NS_G, NS_IN = 0, 1024, 1280, 1536, 1792, 2048, 2304, 2560, 2608
NS_H, NS_GR = 16, 4
CMP_LEN, CMP_STRIDE = 32, 16
NCMP = (S - CMP_LEN) // CMP_STRIDE + 1
SEC_W = dict(qa=256, ka=256, va=256, qd=384, kd=384, vd=384, qc=384, kc=128, vc=128)
SEC_ORDER = ("qa", "ka", "qd", "kd", "qc", "kc", "va", "vd", "vc")
QA, KA, QD, KDL, QC, KC, VA, VD, VC = (sum(SEC_W[m] for m in SEC_ORDER[:i]) for i in range(9))
SEC_IN = sum(SEC_W.values())
SEC_KINDS = ((QA, 8, 0, 1), (QD, 12, 8, 4), (QC, 8, 20, 6))
GRID = 64

HY_BLOCKS = [256] * 7 + [HY_IN - 7 * 256]
NSA_BLOCKS = [256] * 10 + [NS_IN - 10 * 256]
SEC_BLOCKS = [256] * 10

FFN_UNITS = 3 * STEPS
FFN_NORM = [0, 2, 3, 5, 7, 9]
N_PAR = 10
OUT_UNITS = 4
_at, U = 0, {}
for _name, _n in [("ffn0", FFN_UNITS), ("hy_in", 8), ("uq", 1), ("ukv", 1), ("mix0", OUT_UNITS),
                  ("ffn1", FFN_UNITS), ("ffn2", FFN_UNITS), ("nsa_in", 11), ("mix1", OUT_UNITS),
                  ("ffn3", FFN_UNITS), ("sec_in0", 10), ("mix2", OUT_UNITS), ("ffn4", FFN_UNITS),
                  ("sec_in1", 10), ("mix3", OUT_UNITS), ("ffn5", FFN_UNITS)]:
    U[_name] = _at
    _at += _n
N_UNITS = _at

TURN = {n: q for q, n in enumerate(["n0", "n1", "m0", "n2", "n3", "n4", "m1", "n5",
                                    "n6", "m2", "n7", "n8", "m3", "n9"])}
JOB0 = {"mla": 0, "nsa": 8, "sec0": 40, "sec1": 56}
FT_GROUPS = {"mla": 9, "nsa": 12, "sec0": 14, "sec1": 14}
FT_A0, FT_D0 = {}, {}
_a = _d = 0
for _s, _n in FT_GROUPS.items():
    FT_A0[_s], FT_D0[_s] = _a, _d
    _a += (_n + 1) // 2
    _d += _n // 2
PROJ0 = {"hy": 0, "nsa": 8, "sec0": 19, "sec1": 29}


def out_tile(m, place):
    return (place + 4) % KD if m == 0 else place if m == 1 else KD - 1 - place


def rms_turn(n):
    return n + (1 if n >= 6 else 0)


_c, C = 0, {}
for _name, _n in [("ident", 128), ("flip", 128), ("block_tri", 128), ("causal", 128), ("dil", 2 * 256), ("na_mask", 64),
                  ("cmp_add", 64), ("cmp_01", 64), ("freq", 48), ("cos1", 16), ("sin1", 16),
                  ("cosax", 64), ("sinax", 64), ("ones", 128)]:
    C[_name] = (_c, _c + _n)
    _c += _n
N_CONST = _c

G_NORM, G_OUT, G_Q, G_KV, N_GAIN = 0, 80, 96, 98, 99


def shape_constants():
    c = np.zeros((P, N_CONST), np.float32)

    def put(name, a):
        lo, hi = C[name]
        c[:, lo:hi] = np.asarray(a, np.float32).reshape(P, hi - lo)

    p = np.arange(P)
    put("ident", np.eye(P))
    put("ones", np.ones((P, P)))
    put("flip", p[None, :] == p[:, None] // GRID * GRID + GRID - 1 - p[:, None] % GRID)
    put("block_tri", (p[:, None] <= p[None, :]) & (p[:, None] // GLA_C == p[None, :] // GLA_C))
    put("causal", np.where(p[None, :] > p[:, None], NEG, 0.0))
    t = np.arange(S)
    times = np.zeros((S, S))
    for w, d in ((128, 1), (512, 4), (2048, 16)):
        off = t[None, :] - t[:, None]
        times += (off % d == 0) & (np.abs(off) <= (w // 2) // d * d)
    dil = np.where(times > 0, np.log(np.maximum(times, 1)), NEG)
    put("dil", dil.reshape(NT, P, S).transpose(1, 0, 2))
    col = GRID - 1 - p % GRID
    c0 = np.clip(col - 8, 0, GRID - 16)
    kc = np.arange(GRID)
    put("na_mask", np.where((kc[None] >= c0[:, None]) & (kc[None] < c0[:, None] + 16), 0.0, NEG))
    n = np.arange(32)
    ok = (n[None] < NCMP) & (n[None] * CMP_STRIDE + CMP_LEN - 1 <= t[:, None])
    put("cmp_add", np.where(ok, 0.0, NEG).reshape(NT, P, 32).transpose(1, 0, 2))
    put("cmp_01", ok.reshape(NT, P, 32).transpose(1, 0, 2))

    def inv(theta, d):
        e = -np.arange(d // 2, dtype=np.float32) * np.float32(2.0 / d)
        return np.power(np.float64(theta), e.astype(np.float64)).astype(np.float32)

    put("freq", np.broadcast_to(np.concatenate([inv(10000.0, 32), inv(10000.0, 64)]), (P, 48)))

    def tables(pos, theta, d):
        ang = (pos.astype(np.float32)[:, None] * inv(theta, d)[None]).astype(np.float64)
        return np.cos(ang), np.sin(ang)

    for k, f in (("cos", 0), ("sin", 1)):
        one = tables(t, 500000.0, 16)[f]
        put(k + "1", one.reshape(NT, P, 8).transpose(1, 0, 2))
        ax = np.stack([tables(t // GRID, 10000.0, 32)[f], tables(t % GRID, 10000.0, 32)[f]], 1)
        put(k + "ax", ax.reshape(NT, P, 2, 16).transpose(1, 0, 2, 3))
    return c


def build(nc, stream, consts, gains, conv, x, positions, pos_rows, cmp_w1, cmp_w2, final_gain, gla_gain,
          gla_a2, gla_ba, q_gain2, k_gain2, rpb2, out):
    ctx = ExitStack()
    with ctx:
        def sb(name, shape, dt=F32):
            return ctx.enter_context(nc.sbuf_tensor(name, shape, dt))

        def sem(name):
            return ctx.enter_context(nc.semaphore(name))

        bank = [ctx.enter_context(nc.psum_tensor(f"bank{i}", [P, 512], F32)) for i in range(8)]

        raw = sb("raw", [P, NRAW, UNIT])
        w_hi = sb("w_hi", [P, NSPLIT, UNIT], F32R)
        w_lo = sb("w_lo", [P, NSPLIT, UNIT], F32R)
        X = sb("X", [P, NT, D])
        xt_hi = sb("xt_hi", [P, KD, S], F32R)
        xt_lo = sb("xt_lo", [P, KD, S], F32R)
        proj = sb("proj", [P, NT, NS_IN])
        work = sb("work", [P, 2 * 2048])
        QT = sb("QT", [P, 16 * S])
        KT = sb("KT", [P, 12 * S])
        O = sb("O", [P, NT, D])
        prob = sb("prob", [P, 2048])
        h_hi = sb("h_hi", [P, 2, 512], F32R)
        h_lo = sb("h_lo", [P, 2, 512], F32R)
        cst = sb("cst", [P, N_CONST])
        gcol = sb("gcol", [P, N_GAIN])
        ccol = sb("ccol", [P, 2, 4, 22])
        ident_b = sb("ident_b", [P, P], BF16)
        causal_b = sb("causal_b", [P, P], BF16)
        head_gain = sb("head_gain", [P, 2, 6, 64])
        gla_row = sb("gla_row", [P, GLA_DV])
        a2 = sb("a2", [GLA_R + 1, 256])
        w2 = sb("w2", [P, 2, 64])
        posr = sb("posr", [P, 2, 16])
        pos_i = sb("pos_i", [P, 3], I32)
        pos_f = sb("pos_f", [P, 3])
        ang = sb("ang", [P, 3, 48])
        red = sb("red", [P, 3, 48])
        tmp48 = sb("tmp48", [P, 3, 48])
        rsin = sb("rsin", [P, 3, 48])
        rcos = sb("rcos", [P, 3, 48])
        neg_half = sb("neg_half", [P, 56])
        ss = sb("ss", [P, 56])
        ms = sb("ms", [P, 56])
        rstd = sb("rstd", [P, 56])
        negmax = sb("negmax", [P, 4, 2])
        sums = sb("sums", [P, 4, 2])
        rsum = sb("rsum", [P, 4, 2])
        gate = sb("gate", [P, NT, 48])
        small = sb("small", [P, 4, 32])

        def const(name):
            return cst[:, C[name][0]:C[name][1]]

        ident = const("ident")
        xn = work[:, 0:2048].rearrange("p (t d) -> p t d", t=NT)
        na_bias = work[:, 2048:4096].rearrange("p (t h s) -> p t h s", t=NT, h=4)
        act_g = QT[:, 0:1024].rearrange("p (b n) -> p b n", b=2)
        h_f = QT[:, 1024:1536]
        conv_y = QT[:, 1536:2560].rearrange("p (b n) -> p b n", b=2)
        qT = QT[:, :].rearrange("p (h s) -> p h s", s=S)
        kT = KT[:, :].rearrange("p (h s) -> p h s", s=S)

        raw_in = [sem(f"raw_in{i}") for i in range(NRAW)]
        hi_done, lo_done = sem("hi_done"), sem("lo_done")
        unit_used = sem("unit_used")
        x_in, cst_in, gain_in, par_in = sem("x_in"), sem("cst_in"), sem("gain_in"), sem("par_in")
        x_upd = sem("x_upd")
        sq_done, ms_done, rstd_done = sem("sq_done"), sem("ms_done"), sem("rstd_done")
        xn0, xn1 = sem("xn0"), sem("xn1")
        xt_ps, xth, xtl = sem("xt_ps"), sem("xth"), sem("xtl")
        actg_done, mul_done, hh_done, hl_done = sem("actg_done"), sem("mul_done"), sem("hh_done"), sem("hl_done")
        cv_mid, cv_left, cv_done = sem("cv_mid"), sem("cv_left"), sem("cv_done")
        pj_evac = sem("pj_evac")
        ft_ready_d, ft_ready_p = sem("ft_ready_d"), sem("ft_ready_p")
        ft_ps, ft_a, ft_d = sem("ft_ps"), sem("ft_a"), sem("ft_d")
        s_done, nm_done, exp_done, t_done = sem("s_done"), sem("nm_done"), sem("exp_done"), sem("t_done")
        pt_evac, pv_done = sem("pt_evac"), sem("pv_done")
        p_scaled = sem("p_scaled")
        o_copied, o_sum, o_scaled = sem("o_copied"), sem("o_sum"), sem("o_scaled")
        dve_own, act_own, pool_own = sem("dve_own"), sem("act_own"), sem("pool_own")
        const_ready, rope_arg, rope_tab = sem("const_ready"), sem("rope_arg"), sem("rope_tab")
        mla_sq, mla_ms, mla_rs, mla_cn, mla_tp, mla_ch, mla_cl, mla_q, mla_kv, mla_up = (
            sem("mla_" + n) for n in ("sq", "ms", "rs", "cn", "tp", "ch", "cl", "q", "kv", "up"))
        g_tp, g_ev, g_evd, g_z, g_ln, g_la, g_b, g_bt, g_d, g_e, g_qk, g_a, g_am, g_kt, g_kd, g_kv, g_st, g_o, \
            g_ms, g_rs, g_sr, g_ot = (sem("g_" + n) for n in (
                "tp", "ev", "evd", "z", "ln", "la", "b", "bt", "d", "e", "qk", "a", "am", "kt", "kd", "kv", "st",
                "o", "ms", "rs", "sr", "ot"))
        c_w, c_dup, c_tp, c_m, c_h, c_b, c_hid, c_kc, c_kr, c_kt, c_kcT, c_s, c_sc, c_e, c_p, c_pt, c_pe, \
            c_gate = (sem("c_" + n) for n in (
                "w", "dup", "tp", "m", "h", "b", "hid", "kc", "kr", "kt", "kcT", "s", "sc", "e", "p", "pt", "pe",
                "gate"))
        b_in, b_free, na_ready = sem("b_in"), sem("b_free"), sem("na_ready")
        e_sq, e_ms, e_rt, e_rs, e_m, e_mr = (sem("e_" + n) for n in ("sq", "ms", "rt", "rs", "m", "mr"))
        f_in = sem("f_in")
        stored = sem("stored")

        block = ctx.enter_context(nc.Block())

        def ffn_unit(f, kind, s):
            u0 = U[f"ffn{f}"]
            if kind == "d":
                return u0 + (FFN_UNITS - 1 if s == STEPS - 1 else 3 * s + 4)
            g = u0 if s == 0 else u0 + 3 * s - 1
            return g if kind == "g" else g + 1

        def ffn_steps(eng, f, triple):
            triple(f, 0, None)
            triple(f, 1, None)
            with eng.Fori(0, 4) as i:
                triple(f, 2, i)
                triple(f, 3, i)
            triple(f, 10, None)

        def on(n, per, i):
            return n if i is None else i * per + n

        def tap(l, n, s, j, i):
            c = on(2 * s + j, 4, i)
            return ccol[:, l, n, c:c + 1] if i is None else ccol[:, l, n, bass.ds(c, 1)]

        heads = {}
        heads["mla"] = [dict(q=h, k=h, d=MLA_QK, causal=True,
                             v=lambda kt, h=h: work[:, 2048 + kt * 1024 + h * 128 + 64:2048 + kt * 1024 + h * 128 + 128])
                        for h in range(MLA_H)]
        heads["nsa"] = [dict(q=h, k=4 * br + h // 4, d=64, causal=True,
                             v=lambda kt, h=h, br=br: proj[:, kt, (NS_VS, NS_VW)[br] + (h // 4) * 64:
                                                           (NS_VS, NS_VW)[br] + (h // 4) * 64 + 64])
                        for h in range(NS_H) for br in range(2)]

        def sec_job(h):
            if h < 4:
                return dict(q=h, k=h, d=64, causal=False, order="flip", bias=lambda qt: na_bias[:, qt, h, :],
                            v=lambda kt: proj[:, kt, VA + h * 64:VA + h * 64 + 64])
            if h < 10:
                lo = C["dil"][0]
                return dict(q=h, k=h, d=64, causal=False, order="ident", bias=lambda qt: cst[:, lo + qt * S:lo + qt * S + S],
                            v=lambda kt: proj[:, kt, VD + (h - 4) * 64:VD + (h - 4) * 64 + 64])
            g = (h - 10) // 3
            return dict(q=h, k=10 + g, d=64, causal=False, bias=None,
                        v=lambda kt: proj[:, kt, VC + g * 64:VC + g * 64 + 64])

        heads["sec0"] = heads["sec1"] = [sec_job(2 * (7 - i // 2) + i % 2) for i in range(16)]
        JOBS_PER_PAIR = {"mla": 2, "nsa": 4, "sec0": 2, "sec1": 2}

        def pair_after(stage, i, lag):
            n = JOBS_PER_PAIR[stage]
            last = i - lag
            return last // n if last >= 0 and last % n == n - 1 else None

        def late_pairs(stage, lag):
            n, jobs = JOBS_PER_PAIR[stage], len(heads[stage])
            return [q for q in range(jobs // n) if (q + 1) * n - 1 + lag >= jobs]

        o_t = O[:, :, :].rearrange("p t (a s) -> p (t a) s", s=S)
        o_sq = work[:, 0:512].rearrange("p (b s) -> p b s", b=2)
        o_rs = work[:, 512:1280]

        def kind_of(place):
            return 0 if place < 3 else 1 if place < 6 else 2

        def ft_groups(stage):
            if stage == "mla":
                gs = [([(lambda t, h=h: work[:, 2048 + t * 1024 + h * 128:2048 + t * 1024 + h * 128 + 64])
                        for h in (2 * g, 2 * g + 1)], 64, [kT[0:64, 2 * g:2 * g + 2, :]]) for g in range(4)]
                gs.append(([lambda t: proj[:, t, HY_KR - 64:HY_KR + 32]], 96, None))
                gs += [([(lambda t, h=h: work[:, t * 768 + h * 96:t * 768 + h * 96 + 96])
                         for h in (2 * g, 2 * g + 1)], 96, [qT[0:96, 2 * g:2 * g + 2, :]]) for g in range(4)]
                return gs
            if stage == "nsa":
                src = [NS_Q + 64 * h for h in range(16)] + [NS_KS + 64 * g for g in range(4)] + \
                      [NS_KW + 64 * g for g in range(4)]
                dst = [(qT, h) for h in range(16)] + [(kT, g) for g in range(8)]
            else:
                src, dst = [], []
                for q, k, nq, nk, q0, k0 in ((QA, KA, 4, 4, 0, 0), (QD, KDL, 6, 6, 4, 4), (QC, KC, 6, 2, 10, 10)):
                    src += [q + 64 * h for h in range(nq)] + [k + 64 * h for h in range(nk)]
                    dst += [(qT, q0 + h) for h in range(nq)] + [(kT, k0 + h) for h in range(nk)]
            return [([(lambda t, c=c: proj[:, t, c:c + 64]) for c in src[2 * g:2 * g + 2]], 64,
                     [dst[2 * g][0][0:64, dst[2 * g][1]:dst[2 * g][1] + 2, :]]) for g in range(len(src) // 2)]

        def ft_scale(stage, g):
            return 0.125 if stage == "nsa" and g < NS_H // 2 else 1.0

        def ncols(job, qt):
            return P if job["causal"] and qt == 0 else S

        def pt_blocks(job):
            return [(0, 0), (1, 0), (1, 1)] if job["causal"] else [(0, 0), (1, 0), (0, 1), (1, 1)]

        def p_of(par, qt, lo, hi):
            return prob[:, par * 512 + qt * 256 + lo:par * 512 + qt * 256 + hi]

        def pts_of(par, lo, hi):
            return prob[:, 1024 + par * 512 + lo:1024 + par * 512 + hi]

        def q_(i):
            return QT[:, i * 512:(i + 1) * 512]

        gla_q, gla_k, gla_b, gla_eb, gla_d, gla_ei, gla_ed, gla_qi = (q_(i) for i in range(8))
        gla_kd, gla_za, gla_ln, gla_la, gla_kdt = (KT[:, i * 512:(i + 1) * 512] for i in range(5))
        gla_aT = KT[:, 2560:2816]
        gla_qz, gla_am, gla_st, gla_sr = (work[:, i * 1024:(i + 1) * 1024] for i in range(4))

        def chunks(ap):
            return ap.rearrange("p (a c i) -> p a c i", a=2, c=4)

        dup = work[:, 0:2048].rearrange("p (m t g e d) -> p m t g e d", m=2, t=2, g=4, e=2)
        m_k = work[:, 2048:2048 + 1280].rearrange("p (g s) -> p g s", g=5)
        m_v = work[:, 0:1280].rearrange("p (g s) -> p g s", g=5)
        hid = [QT[:, 0:128], QT[:, 128:256]]
        sc = work[:, 2048:3072]
        pc = work[:, 3072:4096]
        pct = work[:, 0:1024]
        kc_tok, vc_tok, kcT_ = KT[:, 2048:2112], KT[:, 2112:2176], KT[:, 2176:2304]
        rope_t = KT[:, 2304:2560]
        vcz = KT[:, 2560:2816].rearrange("p (g d) -> p g d", g=4)

        def rotate(eng, lnk, x1, x2, cos, sin, t1, t2):
            lnk(eng.tensor_tensor(t1, x1, sin, ALU.mult))
            lnk(eng.tensor_tensor(t2, x2, sin, ALU.mult))
            lnk(eng.tensor_tensor(x1, x1, cos, ALU.mult))
            lnk(eng.tensor_tensor(x2, x2, cos, ALU.mult))
            lnk(eng.tensor_tensor(x1, x1, t2, ALU.subtract))
            lnk(eng.tensor_tensor(x2, x2, t1, ALU.add))

        def rope_heads(eng, lnk, view, off, half, cos_t, sin_t, tmp):
            n = view.shape[1]
            x1 = view[:, :, off:off + half]
            x2 = view[:, :, off + half:off + 2 * half]
            cos = cos_t.unsqueeze(1).to_broadcast([P, n, half])
            sin = sin_t.unsqueeze(1).to_broadcast([P, n, half])
            t1 = tmp[:, 0:n * half].rearrange("p (h d) -> p h d", h=n)
            t2 = tmp[:, n * half:2 * n * half].rearrange("p (h d) -> p h d", h=n)
            rotate(eng, lnk, x1, x2, cos, sin, t1, t2)

        def head_rms(tile, n):
            _, heads_n, o, _ = SEC_KINDS[n]
            return tile[:, 0:56].rearrange("p (t h) -> p t h", t=NT)[:, :, o:o + heads_n]

        def sec_heads(eng, lnk, n, t, l, tmp):
            def head_view(c, m):
                return proj[:, t, c:c + m * 64].rearrange("p (h d) -> p h d", h=m)

            c, m, o, _ = SEC_KINDS[n]
            r = rstd[:, t * 28 + o:t * 28 + o + m].unsqueeze(2).to_broadcast([P, m, 64])
            lnk(eng.tensor_tensor(head_view(c, m), head_view(c, m), r, ALU.mult))
            for c1, m1, row in (((QA, 4, 0), (KA, 4, 3)), ((QD, 6, 1), (KDL, 6, 4)), ((QC, 6, 2), (KC, 2, 5)))[n]:
                g = head_gain[:, l, row, :].unsqueeze(1).to_broadcast([P, m1, 64])
                lnk(eng.tensor_tensor(head_view(c1, m1), head_view(c1, m1), g, ALU.mult))
            if n == 1:
                one = [const(k)[:, t * 8:(t + 1) * 8] for k in ("cos1", "sin1")]
                rope_heads(eng, lnk, head_view(QD, 12), 0, 8, one[0], one[1], tmp)
            if n == 2:
                v = proj[:, t, QC:QC + 512].rearrange("p (h r d) -> p h r d", h=8, r=2)
                cos, sin = (const(k)[:, t * 32:(t + 1) * 32].rearrange("p (r d) -> p r d", r=2).unsqueeze(1)
                            .to_broadcast([P, 8, 2, 16]) for k in ("cosax", "sinax"))
                t1 = tmp[:, 0:256].rearrange("p (h r d) -> p h r d", h=8, r=2)
                t2 = tmp[:, 256:512].rearrange("p (h r d) -> p h r d", h=8, r=2)
                rotate(eng, lnk, v[:, :, :, 0:16], v[:, :, :, 16:32], cos, sin, t1, t2)

        @block.sync
        def _(sp):
            def load(u, j):
                sp.dma_start(raw[:, j, :], stream[u]).then_inc(raw_in[j], 16)

            for j in range(NRAW):
                load(j, j)
            turns = N_UNITS // NRAW
            with sp.Fori(1, turns) as i:
                for j in range(NRAW):
                    sp.wait_ge(lo_done, i * NRAW + (j - NRAW + 1))
                    load(i * NRAW + j, j)
            for u in range(turns * NRAW, N_UNITS):
                sp.wait_ge(lo_done, u - NRAW + 1)
                load(u, u % NRAW)
            sp.wait_ge(x_upd, 4 * 11)
            sp.dma_start(out[0].rearrange("(t p) d -> p t d", p=P), X[:, :, :]).then_inc(stored, 16)
            sp.wait_ge(stored, 16)

        @block.tensor
        def _(pe):
            def xt_transposes(src):
                for b in range(4):
                    for kk in range(2):
                        for t in range(NT):
                            k = 2 * b + kk
                            ins = pe.transpose(bank[4 + b][:, (kk * 2 + t) * P:(kk * 2 + t + 1) * P],
                                               src[:, t, k * P:(k + 1) * P], ident)
                    ins.then_inc(xt_ps, 1)

            def norm(n):
                pe.wait_ge(xn0, n + 1)
                pe.wait_ge(xn1, n + 1)
                xt_transposes(xn)

            def token_major(u, name, width, out_bank, first_turn):
                pe.wait_ge(lo_done, u + 1)
                sl = u % 3
                for t in range(NT):
                    dst = out_bank[:, t * 256:t * 256 + width]
                    for k in range(KD):
                        if first_turn is not None and t == 0:
                            pe.wait_ge(xtl, 8 * first_turn + k + 1)
                        tok = slice(t * P, (t + 1) * P)
                        cols = slice(k * 256, k * 256 + width)
                        pe.matmul(dst, xt_hi[:, k, tok], w_hi[:, sl, cols], start=(k == 0), stop=False)
                        pe.matmul(dst, xt_hi[:, k, tok], w_lo[:, sl, cols], start=False, stop=False)
                        ins = pe.matmul(dst, xt_lo[:, k, tok], w_hi[:, sl, cols], start=False, stop=(k == KD - 1))
                ins.then_inc(unit_used, 1)

            def project(stage, u0, blocks, turn):
                p0 = PROJ0[stage]
                for c, width in enumerate(blocks):
                    if c >= 4:
                        pe.wait_ge(pj_evac, p0 + c - 3)
                    token_major(u0 + c, stage, width, bank[c % 4], turn if c == 0 else None)

            def mix_out(m):
                u0 = U[f"mix{m}"]
                turn = TURN[f"m{m}"]
                for c in range(OUT_UNITS):
                    u = u0 + c
                    pe.wait_ge(lo_done, u + 1)
                    sl = u % 3
                    for j in range(2):
                        k = 2 * c + j
                        pe.wait_ge(xtl, 8 * turn + k + 1)
                        for t in range(NT):
                            tok = slice(t * P, (t + 1) * P)
                            for lhs, w, in ((xt_hi, w_hi), (xt_hi, w_lo), (xt_lo, w_hi)):
                                for half in range(2):
                                    cols = slice(j * D + half * 512, j * D + half * 512 + 512)
                                    ins = pe.matmul(bank[2 * t + half][:, :], lhs[:, k, tok], w[:, sl, cols],
                                                    start=(k == 0 and lhs is xt_hi and w is w_hi),
                                                    stop=(k == KD - 1 and lhs is xt_lo))
                    ins.then_inc(unit_used, 1)

            def ffn_gu(f, kind, s, i):
                u = ffn_unit(f, kind, s)
                sl = u % NSPLIT
                pe.wait_ge(lo_done, on(u + 1, 6, i))
                dst = bank[2 * (s % 2) + (0 if kind == "g" else 1)]
                turn = TURN[f"n{FFN_NORM[f]}"]
                for j in range(2):
                    for k in range(KD):
                        if s == 0 and kind == "g" and j == 0:
                            pe.wait_ge(xtl, 8 * turn + k + 1)
                        cols = slice(k * 256 + j * P, k * 256 + (j + 1) * P)
                        o = dst[:, j * S:(j + 1) * S]
                        pe.matmul(o, w_hi[:, sl, cols], xt_hi[:, k, :], start=(k == 0), stop=False)
                        pe.matmul(o, w_hi[:, sl, cols], xt_lo[:, k, :], start=False, stop=False)
                        ins = pe.matmul(o, w_lo[:, sl, cols], xt_hi[:, k, :], start=False, stop=(k == KD - 1))
                ins.then_inc(unit_used, 1)

            def ffn_down(f, s, i):
                u = ffn_unit(f, "d", s)
                sl = u % NSPLIT
                pe.wait_ge(lo_done, on(u + 1, 6, i))
                pe.wait_ge(hl_done, on(f * STEPS + s + 1, 2, i))
                for j in range(2):
                    for t in range(NT):
                        tok = slice(j * S + t * P, j * S + (t + 1) * P)
                        for lhs, w in ((h_hi, w_hi), (h_hi, w_lo), (h_lo, w_hi)):
                            for half in range(2):
                                cols = slice(j * D + half * 512, j * D + half * 512 + 512)
                                ins = pe.matmul(bank[4 + 2 * t + half][:, :], lhs[:, s % 2, tok], w[:, sl, cols],
                                                start=(s == 0 and j == 0 and lhs is h_hi and w is w_hi),
                                                stop=(s == STEPS - 1 and j == 1 and lhs is h_lo))
                ins.then_inc(unit_used, 1)

            def triple(f, s, i):
                if s >= 2:
                    pe.wait_ge(mul_done, on(f * STEPS + s - 1, 2, i))
                ffn_gu(f, "g", s, i)
                ffn_gu(f, "u", s, i)
                if s:
                    ffn_down(f, s - 1, i)

            def ffn(f):
                ffn_steps(pe, f, triple)
                ffn_down(f, STEPS - 1, None)

            def feature_major(stage):
                a0, d0 = FT_A0[stage], FT_D0[stage]
                g0 = a0 + d0
                for g, (srcs, rows, _) in enumerate(ft_groups(stage)):
                    for n, (_, _, o, _) in enumerate(SEC_KINDS):
                        if stage[:3] == "sec" and g == o // 2:
                            pe.wait_ge(ft_ready_p, 3 + 3 * int(stage[3]) + n)
                            if n == 2:
                                pe.wait_ge(ft_ready_d, 3 + int(stage[3]))
                    if g >= 4:
                        if g % 2 == 0:
                            pe.wait_ge(ft_a, a0 + (g - 4) // 2 + 1)
                        else:
                            pe.wait_ge(ft_d, d0 + (g - 4) // 2 + 1)
                    for n, src in enumerate(srcs):
                        for t in range(NT):
                            ins = pe.transpose(bank[g % 4][0:rows, (2 * n + t) * P:(2 * n + t + 1) * P], src(t), ident)
                    ins.then_inc(ft_ps, 1)

            def attention(stage):
                jobs, j0 = heads[stage], JOB0[stage]

                def scores(i):
                    if i >= len(jobs):
                        return
                    if i >= 3:
                        pe.wait_ge(exp_done, 2 * (j0 + i - 2))
                    job, dst = jobs[i], bank[S_BANKS[i % 3]]
                    if stage[:3] == "sec" and i == 12:
                        pe.wait_ge(na_ready, int(stage[3]) + 1)
                    for qt in range(NT):
                        n = ncols(job, qt)
                        plain = not job["causal"] and job["bias"] is None
                        ins = pe.matmul(dst[:, qt * S:qt * S + n], qT[0:job["d"], job["q"], qt * P:(qt + 1) * P],
                                        kT[0:job["d"], job["k"], 0:n], start=True, stop=plain)
                        if job["causal"]:
                            ins = pe.matmul(dst[:, qt * S + qt * P:qt * S + (qt + 1) * P], ident_b[:, :],
                                            causal_b[:, :], start=False, stop=True)
                        elif not plain:
                            ins = pe.matmul(dst[:, qt * S:qt * S + n], const(job["order"]), job["bias"](qt), start=False,
                                            stop=True)
                    ins.then_inc(s_done, 1)

                def turn_p(i):
                    pe.wait_ge(p_scaled, j0 + i + 1)
                    if i >= 2:
                        pe.wait_ge(pt_evac, j0 + i - 1)
                    for n, (qt, kt) in enumerate(pt_blocks(jobs[i])):
                        ins = pe.transpose(bank[2 + i % 2][:, n * P:(n + 1) * P], p_of(i % 2, qt, kt * P, (kt + 1) * P),
                                           ident)
                    ins.then_inc(t_done, 1)

                def values(i):
                    if i < 0:
                        return
                    pe.wait_ge(pt_evac, j0 + i + 1)
                    per = JOBS_PER_PAIR[stage]
                    pair, at = i // per, i % per
                    if at == 0 and pair >= 2:
                        if stage[:3] == "sec":
                            pe.wait_ge(o_copied, 8 * int(stage[3]) + pair - 1)
                        else:
                            pe.wait_ge(xtl, 8 * TURN["m0" if stage == "mla" else "m1"] + (4 if stage == "mla" else 0)
                                       + pair - 1)
                    job, half = jobs[i], at * 2 // per
                    dst = bank[4 + pair % 2][64 * half:64 * half + 64, 0:S]
                    first = True
                    if stage == "nsa":
                        first = False
                        if at % 2 == 0:
                            g, j = job["q"] // 4, job["q"] % 4
                            pe.matmul(dst, vcz[:, g, :], pct[:, j * S:(j + 1) * S], start=True, stop=False)
                    last = stage != "nsa" or at % 2 == 1
                    pe.matmul(dst, job["v"](0), pts_of(i % 2, 0, S), start=first, stop=False)
                    if job["causal"]:
                        ins = pe.matmul(dst[:, P:S], job["v"](1), pts_of(i % 2, S, S + P), start=False, stop=last)
                    else:
                        ins = pe.matmul(dst, job["v"](1), pts_of(i % 2, S, 2 * S), start=False, stop=last)
                    ins.then_inc(pv_done, 1)

                def square_sums(place):
                    l = int(stage[3])
                    pe.wait_ge(o_copied, 8 * l + place + 1)
                    kind = kind_of(place)
                    dst = bank[7][:, kind * S:(kind + 1) * S] if kind < 2 else bank[1][:, 0:S]
                    pe.matmul(dst, const("ones"), o_sq[:, place % 2, :], start=place in (0, 3, 6),
                              stop=place in (2, 5, 7)).then_inc(o_sum, 1)

                scores(0)
                scores(1)
                for i in range(len(jobs)):
                    scores(i + 2)
                    turn_p(i)
                    values(i - 1)
                    if stage[:3] == "sec" and pair_after(stage, i, 4) is not None:
                        square_sums(pair_after(stage, i, 4))
                values(len(jobs) - 1)
                if stage[:3] == "sec":
                    for place in late_pairs(stage, 4):
                        if place == 6:
                            pe.wait_ge(exp_done, 2 * (j0 + len(jobs)))
                        square_sums(place)

            def wait_ft(stage):
                pe.wait_ge(ft_a, FT_A0[stage] + (FT_GROUPS[stage] + 1) // 2)
                pe.wait_ge(ft_d, FT_D0[stage] + FT_GROUPS[stage] // 2)

            def gla():
                pe.wait_ge(pj_evac, 8)
                for c, b in ((HY_GQ, 0), (HY_GK, 1)):
                    for a in range(2):
                        for t in range(NT):
                            ins = pe.transpose(bank[b][:, (a * 2 + t) * P:(a * 2 + t + 1) * P],
                                               proj[:, t, c + a * P:c + (a + 1) * P], ident)
                    ins.then_inc(g_tp, 1)
                for t in range(NT):
                    ins = pe.transpose(bank[2][0:GLA_R, t * P:(t + 1) * P], proj[:, t, HY_GA:HY_GA + GLA_R], ident)
                ins.then_inc(g_tp, 1)
                pe.wait_ge(g_ev, 2)
                for t in range(NT):
                    ins = pe.matmul(bank[3][:, t * 256:(t + 1) * 256], gla_aT[0:GLA_R + 1, t * P:(t + 1) * P], a2[:, :],
                                    start=True, stop=True)
                ins.then_inc(g_z, 1)
                pe.wait_ge(g_la, 1)
                for a in range(2):
                    for t in range(NT):
                        ins = pe.matmul(bank[2][:, (a * 2 + t) * P:(a * 2 + t + 1) * P],
                                        gla_la[:, t * 256 + a * P:t * 256 + (a + 1) * P], const("block_tri"),
                                        start=True, stop=True)
                ins.then_inc(g_b, 1)
                pe.wait_ge(g_qk, 2)
                for t in range(NT):
                    for h in range(GLA_H):
                        r = slice(64 * (h % 2), 64 * (h % 2) + 64)
                        c = (h // 2) * S + t * P
                        at = (2 * t + h // 2) * P
                        ins = pe.matmul(bank[h % 2][:, at:at + P], gla_kd[r, c:c + P], gla_qi[r, c:c + P],
                                        start=True, stop=True)
                ins.then_inc(g_a, 1)
                for t in range(NT):
                    for a in range(2):
                        ins = pe.transpose(bank[2][:, (t * 2 + a) * P:(t * 2 + a + 1) * P],
                                           gla_kd[:, a * S + t * P:a * S + (t + 1) * P], ident)
                ins.then_inc(g_kt, 1)
                pe.wait_ge(g_kd, 1)
                for c in range(3):
                    r = slice(64 * (c % 2), 64 * (c % 2) + 64)
                    t = c // 2
                    for a in range(2):
                        ins = pe.matmul(bank[3 + c][:, a * 256:(a + 1) * 256], gla_kdt[r, (t * 2 + a) * P:(t * 2 + a + 1) * P],
                                        proj[r, t, HY_GV + a * 256:HY_GV + (a + 1) * 256], start=True, stop=True)
                    ins.then_inc(g_kv, 1)
                pe.wait_ge(g_am, 1)
                pe.wait_ge(g_qk, 3)
                pe.wait_ge(g_st, 3)
                qz = gla_qz.rearrange("p (a c i) -> p a c i", a=2, c=4)
                st = gla_st.rearrange("p (a c v) -> p a c v", a=2, c=4)
                for t in range(NT):
                    for h in range(GLA_H):
                        r = slice(64 * (h % 2), 64 * (h % 2) + 64)
                        a = h // 2
                        dst = bank[t + 6 * (1 - h % 2)][:, a * P:(a + 1) * P]
                        n = 4 * (h % 2) + 2 * t + a
                        pe.matmul(dst, gla_am[:, n * P:(n + 1) * P],
                                  proj[:, t, HY_GV + h * P:HY_GV + (h + 1) * P], start=True, stop=False)
                        cs = [c for c in (2 * t, 2 * t + 1) if c > 0]
                        for c in cs:
                            ins = pe.matmul(dst, qz[r, a, c, :], st[r, a, c, :], start=False, stop=(c == cs[-1]))
                ins.then_inc(g_o, 1)

            def mla():
                pe.wait_ge(mla_cn, 4)
                for a in range(2):
                    for t in range(NT):
                        ins = pe.transpose(bank[0][:, (a * 2 + t) * P:(a * 2 + t + 1) * P],
                                           proj[:, t, HY_CQ + a * P:HY_CQ + (a + 1) * P], ident)
                ins.then_inc(mla_tp, 1)
                for t in range(NT):
                    ins = pe.transpose(bank[1][:, t * P:(t + 1) * P], proj[:, t, HY_CKV:HY_CKV + P], ident)
                ins.then_inc(mla_tp, 1)
                pe.wait_ge(mla_cl, 3)
                u = U["uq"]
                pe.wait_ge(lo_done, u + 1)
                sl = u % 3
                for t in range(NT):
                    tok = slice(t * P, (t + 1) * P)
                    for c0, n, b in ((0, 512, 4), (512, 256, 5)):
                        for k in range(2):
                            cols = slice(k * 768 + c0, k * 768 + c0 + n)
                            o = bank[b + 2 * t][:, 0:n]
                            pe.matmul(o, xt_hi[:, k, tok], w_hi[:, sl, cols], start=(k == 0), stop=False)
                            pe.matmul(o, xt_hi[:, k, tok], w_lo[:, sl, cols], start=False, stop=False)
                            ins = pe.matmul(o, xt_lo[:, k, tok], w_hi[:, sl, cols], start=False, stop=(k == 1))
                ins.then_inc(unit_used, 1)
                u = U["ukv"]
                pe.wait_ge(lo_done, u + 1)
                sl = u % 3
                for t in range(NT):
                    tok = slice(t * P, (t + 1) * P)
                    for half in range(2):
                        cols = slice(half * 512, half * 512 + 512)
                        o = bank[2 * t + half][:, :]
                        pe.matmul(o, xt_hi[:, 2, tok], w_hi[:, sl, cols], start=True, stop=False)
                        pe.matmul(o, xt_hi[:, 2, tok], w_lo[:, sl, cols], start=False, stop=False)
                        ins = pe.matmul(o, xt_lo[:, 2, tok], w_hi[:, sl, cols], start=False, stop=True)
                ins.then_inc(unit_used, 1)
                pe.wait_ge(mla_q, 4)
                for b in range(2):
                    for kk in range(2):
                        for t in range(NT):
                            c = 512 + (2 * b + kk) * P
                            ins = pe.transpose(bank[4 + b][:, (kk * 2 + t) * P:(kk * 2 + t + 1) * P],
                                               O[:, t, c:c + P], ident)
                    ins.then_inc(g_ot, 1)
                pe.wait_ge(ft_ready_d, 1)
                pe.wait_ge(ft_ready_p, 1)
                feature_major("mla")
                wait_ft("mla")
                pe.wait_ge(xtl, 8 * TURN["m0"] + 4)
                attention("mla")

            def compress():
                pe.wait_ge(c_dup, 2)
                for m in range(2):
                    for gp in range(2):
                        for g in (2 * gp, 2 * gp + 1):
                            for t in range(NT):
                                c = ((m * 2 + t) * 4 + g) * P
                                ins = pe.transpose(bank[2 * m + gp][:, ((g % 2) * 2 + t) * P:((g % 2) * 2 + t + 1) * P],
                                                   work[:, c:c + P], ident)
                        ins.then_inc(c_tp, 1)
                pe.wait_ge(c_m, 4)
                pe.wait_ge(c_w, 32)
                for m, (mt, w1) in enumerate(((m_k, prob[:, :]), (m_v, O[:, :, :].rearrange("p t d -> p (t d)")))):
                    pe.wait_ge(c_m, 4 * (m + 1))
                    for l in range(16):
                        ins = pe.matmul(bank[4 + m][:, 0:75], w1[:, l * P:(l + 1) * P],
                                        mt[:, :, 2 * l:2 * l + 225:16], start=(l == 0), stop=(l == 15))
                    ins.then_inc(c_h, 1)
                for m in range(2):
                    pe.wait_ge(c_hid, m + 1)
                    ins = pe.matmul(bank[6][:, m * 64:(m + 1) * 64], hid[m], w2[:, m, :], start=True, stop=True)
                ins.then_inc(c_kc, 1)

            def compressed_attention():
                pe.wait_ge(c_kr, 1)
                pe.transpose(bank[6][0:64, 0:P], kc_tok, ident).then_inc(c_kt, 1)
                pe.wait_ge(c_kcT, 1)
                for t in range(NT):
                    for h in range(NS_H):
                        g, j = h // 4, h % 4
                        ins = pe.matmul(bank[6 + t][:, (j * 4 + g) * 32:(j * 4 + g + 1) * 32],
                                        qT[0:64, h, t * P:(t + 1) * P], kcT_[0:64, g * 32:(g + 1) * 32],
                                        start=True, stop=True)
                ins.then_inc(c_s, 1)
                pe.wait_ge(c_p, 2)
                for j in range(4):
                    for t in range(NT):
                        ins = pe.transpose(bank[6 + j // 2][:, ((j % 2) * 2 + t) * P:((j % 2) * 2 + t + 1) * P],
                                           pc[:, (t * 4 + j) * P:(t * 4 + j + 1) * P], ident)
                ins.then_inc(c_pt, 1)
                pe.wait_ge(c_pe, 1)

            pe.wait_ge(const_ready, 1)
            norm(0)
            ffn(0)
            norm(1)
            project("hy", U["hy_in"], HY_BLOCKS, TURN["n1"])
            gla()
            mla()
            mix_out(0)
            norm(2)
            ffn(1)
            norm(3)
            ffn(2)
            norm(4)
            project("nsa", U["nsa_in"], NSA_BLOCKS, TURN["n4"])
            compress()
            pe.wait_ge(ft_ready_d, 2)
            pe.wait_ge(ft_ready_p, 2)
            feature_major("nsa")
            wait_ft("nsa")
            compressed_attention()
            attention("nsa")
            mix_out(1)
            norm(5)
            ffn(3)
            for l in range(2):
                norm(6 + 2 * l)
                project(f"sec{l}", U[f"sec_in{l}"], SEC_BLOCKS, TURN[f"n{6 + 2 * l}"])
                pe.wait_ge(pj_evac, PROJ0[f"sec{l}"] + len(SEC_BLOCKS))
                feature_major(f"sec{l}")
                wait_ft(f"sec{l}")
                attention(f"sec{l}")
                mix_out(2 + l)
                norm(7 + 2 * l)
                ffn(4 + l)

        @block.scalar
        def _(act):
            own = [0]

            def link(ins):
                own[0] += 1
                ins.then_inc(act_own, 1)
                act.wait_ge(act_own, own[0])

            def split(u, i=None):
                if u >= N_UNITS:
                    return
                sl = u % NSPLIT
                act.wait_ge(raw_in[sl], on(16 * (u // NRAW + 1), 32, i))
                if u >= NSPLIT:
                    act.wait_ge(unit_used, on(u - NSPLIT + 1, 6, i))
                act.activation(w_hi[:, sl, :], raw[:, sl, :], ACT.Copy).then_inc(hi_done, 1)

            def norm(n, between=None):
                r = rms_turn(n)
                for t in range(NT):
                    if n == 0:
                        act.wait_ge(x_in, 16)
                    else:
                        act.wait_ge(x_upd, 4 * r - 2 + 2 * t)
                    act.activation(xn[:, t, :], X[:, t, :], ACT.Square, accum_out=ss[:, t:t + 1]).then_inc(sq_done, 1)
                if between:
                    between()
                act.wait_ge(rstd_done, r + 1)
                act.activation(xn[:, 1, :], X[:, 1, :], ACT.Copy, scale=rstd[:, 1:2]).then_inc(xn1, 1)
                for k in range(KD):
                    act.wait_ge(xt_ps, 4 * n + k // 2 + 1)
                    g = G_NORM + 8 * n + k
                    act.activation(xt_hi[:, k, :], bank[4 + k // 2][:, (k % 2) * S:(k % 2 + 1) * S], ACT.Copy,
                                   scale=gcol[:, g:g + 1]).then_inc(xth, 1)

            def project(stage, u0, blocks, after=None):
                for c, width in enumerate(blocks):
                    split(u0 + c + NSPLIT)
                    act.wait_ge(unit_used, u0 + c + 1)
                    src = bank[c % 4][:, :].rearrange("p (t n) -> p t n", t=2)
                    act.activation(proj[:, :, c * 256:c * 256 + width], src[:, :, 0:width], ACT.Copy).then_inc(pj_evac, 1)
                    if after:
                        after(c)

            def sec_rms(l, c):
                for n, (col, m, _, last) in enumerate(SEC_KINDS):
                    if c == last:
                        act.wait_ge(pj_evac, PROJ0[f"sec{l}"] + c + 1)
                        if n:
                            act.wait_ge(e_ms, 3 * l + n)
                        for t in range(NT):
                            act.activation(work[:, t * m * 64:(t + 1) * m * 64], proj[:, t, col:col + m * 64],
                                           ACT.Square).then_inc(e_sq, 1)
                    if c == last + (1 if n < 2 else 0):
                        act.wait_ge(e_ms, 3 * l + n + 1)
                        act.activation(head_rms(rstd, n), head_rms(ms, n), ACT.Sqrt).then_inc(e_rt, 1)

            def mix_out(m):
                for c in range(OUT_UNITS):
                    u = U[f"mix{m}"] + c + NSPLIT
                    split(u)

            def triple(f, s, i):
                par = s % 2
                split(ffn_unit(f, "g", s) + NSPLIT, i)
                split(ffn_unit(f, "u", s) + NSPLIT, i)
                act.wait_ge(unit_used, on(ffn_unit(f, "u", s) + 1, 6, i))
                if s >= 2:
                    act.wait_ge(mul_done, on(f * STEPS + s - 1, 2, i))
                if f < 4:
                    act.activation(act_g[:, par, :], bank[2 * par][:, :], ACT.Silu).then_inc(actg_done, 1)
                else:
                    l = f - 4
                    for j in range(2):
                        act.activation(conv_y[:, par, j * S:(j + 1) * S], bank[2 * par][:, j * S:(j + 1) * S],
                                       ACT.Identity, scale=tap(l, 1, s, j, i), bias=tap(l, 3, s, j, i)).then_inc(cv_mid, 1)
                    act.wait_ge(cv_done, on(l * STEPS + s + 1, 2, i))
                    act.activation(act_g[:, par, :], conv_y[:, par, :], ACT.Gelu).then_inc(actg_done, 1)
                act.wait_ge(mul_done, on(f * STEPS + s + 1, 2, i))
                act.activation(h_hi[:, par, :], h_f, ACT.Copy).then_inc(hh_done, 1)
                if s:
                    split(ffn_unit(f, "d", s - 1) + NSPLIT, i)

            def ffn(f):
                ffn_steps(act, f, triple)
                split(ffn_unit(f, "d", STEPS - 1) + NSPLIT)

            def feature_major(stage):
                a0, g0 = FT_A0[stage], FT_A0[stage] + FT_D0[stage]
                for g, (srcs, rows, dst) in enumerate(ft_groups(stage)):
                    if g % 2:
                        continue
                    act.wait_ge(ft_ps, g0 + g + 1)
                    if dst is None:
                        src = bank[g % 4][64:96, 0:S]
                        for h in range(MLA_H):
                            ins = act.activation(kT[64:96, h, :], src, ACT.Copy)
                        ins.then_inc(ft_a, 1)
                    else:
                        src = bank[g % 4][0:rows, :].rearrange("p (h s) -> p h s", h=2)
                        act.activation(dst[0], src, ACT.Copy, scale=ft_scale(stage, g)).then_inc(ft_a, 1)

            def attention(stage):
                jobs, j0 = heads[stage], JOB0[stage]
                for i, job in enumerate(jobs):
                    act.wait_ge(nm_done, j0 + i + 1)
                    if i >= 2:
                        act.wait_ge(t_done, j0 + i - 1)
                    for qt in range(NT):
                        n = ncols(job, qt)
                        act.activation(p_of(i % 2, qt, 0, n), bank[S_BANKS[i % 3]][:, qt * S:qt * S + n], ACT.Exp,
                                       bias=negmax[:, i % 4, qt:qt + 1],
                                       accum_out=sums[:, i % 4, qt:qt + 1]).then_inc(exp_done, 1)
                    pair_out(stage, pair_after(stage, i, 3))
                for pair in late_pairs(stage, 3):
                    pair_out(stage, pair)

            def pair_out(stage, pair):
                if pair is None:
                    return
                act.wait_ge(pv_done, JOB0[stage] + (pair + 1) * JOBS_PER_PAIR[stage])
                src = bank[4 + pair % 2][:, 0:S]
                if stage[:3] != "sec":
                    act.activation(xt_hi[:, pair + (4 if stage == "mla" else 0), :], src, ACT.Copy).then_inc(xth, 1)
                    return
                l = int(stage[3])
                act.activation(o_t[:, pair, :], src, ACT.Copy)
                if pair >= 2:
                    act.wait_ge(o_sum, 8 * l + pair - 1)
                act.activation(o_sq[:, pair % 2, :], src, ACT.Square).then_inc(o_copied, 1)

            act.dma_start(X[:, :, :], x[0].rearrange("(t p) d -> p t d", p=P)).then_inc(x_in, 16)
            act.dma_start(cst[:, :], consts).then_inc(cst_in, 16)
            act.dma_start(gcol[:, :], gains).then_inc(gain_in, 16)
            for dst, src in ((pos_i[:, :], positions), (ccol[:, :, :, :], conv),
                             (a2[0:GLA_R, :], gla_a2[0]), (a2[GLA_R:GLA_R + 1, :], gla_ba),
                             (w2[:, 0, :], cmp_w2[0]), (w2[:, 1, :], cmp_w2[1]), (posr[:, :, :], pos_rows),
                             (gla_row[:, :], gla_gain[0].partition_broadcast(P)),
                             (head_gain[:, :, 0:3, :], q_gain2.rearrange("l r d -> (l r d)").partition_broadcast(P)
                              .rearrange("p (l r d) -> p l r d", l=2, r=3)),
                             (head_gain[:, :, 3:6, :], k_gain2.rearrange("l r d -> (l r d)").partition_broadcast(P)
                              .rearrange("p (l r d) -> p l r d", l=2, r=3))):
                act.dma_start(dst, src).then_inc(par_in, 16)
            act.wait_ge(gain_in, 16)
            norm(0, lambda: [split(u) for u in range(NSPLIT)])
            ffn(0)
            act.wait_ge(par_in, 16 * N_PAR)
            act.wait_ge(rope_arg, 1)
            act.activation(rsin[:, :, :], red[:, :, :], ACT.Sin).then_inc(rope_tab, 1)
            act.activation(rcos[:, :, :], tmp48[:, :, :], ACT.Sin).then_inc(rope_tab, 1)
            norm(1)
            project("hy", U["hy_in"], HY_BLOCKS)
            act.wait_ge(g_tp, 1)
            act.activation(gla_q, bank[0][:, :], ACT.Copy, scale=0.125).then_inc(g_ev, 1)
            act.wait_ge(g_tp, 3)
            act.wait_ge(g_evd, 1)
            act.activation(gla_aT[0:GLA_R, :], bank[2][0:GLA_R, 0:S], ACT.Copy).then_inc(g_ev, 1)
            act.wait_ge(g_z, 1)
            link(act.activation(gla_za, bank[3][:, :], ACT.Abs))
            link(act.activation(gla_za, gla_za, ACT.Exp, scale=-1.0))
            act.activation(gla_ln, gla_za, ACT.Ln, bias=1.0).then_inc(g_ln, 1)
            act.wait_ge(g_b, 1)
            act.activation(gla_b, bank[2][:, :], ACT.Copy, scale=1.0 / 16.0).then_inc(g_bt, 1)
            act.wait_ge(g_bt, 1)
            act.activation(gla_eb, gla_b, ACT.Exp).then_inc(g_e, 1)
            act.wait_ge(g_d, 1)
            act.activation(gla_ei, gla_d, ACT.Exp).then_inc(g_e, 1)
            act.activation(gla_ed, gla_d, ACT.Exp, scale=-1.0).then_inc(g_e, 1)
            act.wait_ge(g_kt, 1)
            act.activation(gla_kdt, bank[2][:, :], ACT.Copy).then_inc(g_kd, 1)
            act.activation(gla_sr.rearrange("p (t n) -> p t n", t=2), proj[:, :, HY_GR:HY_GR + 512],
                           ACT.Silu).then_inc(g_sr, 1)
            for n, (c, w) in enumerate(((HY_CQ, 256), (HY_CKV, 128))):
                for t in range(NT):
                    act.activation(prob[:, 0:w], proj[:, t, c:c + w], ACT.Square,
                                   accum_out=ss[:, 8 + 2 * n + t:9 + 2 * n + t]).then_inc(mla_sq, 1)
                    act.wait_ge(mla_sq, 2 * n + t + 1)
            for k in range(3):
                act.wait_ge(mla_tp, 1 if k < 2 else 2)
                src = bank[0][:, k * S:(k + 1) * S] if k < 2 else bank[1][:, 0:S]
                act.activation(xt_hi[:, k, :], src, ACT.Copy, scale=gcol[:, G_Q + k:G_Q + k + 1]).then_inc(mla_ch, 1)
            split(U["uq"] + NSPLIT)
            act.wait_ge(unit_used, U["uq"] + 1)
            act.wait_ge(g_o, 1)
            act.wait_ge(mla_up, 1)
            for t in range(NT):
                for c0, n, b in ((0, 512, 4), (512, 256, 5)):
                    act.activation(work[:, t * 768 + c0:t * 768 + c0 + n], bank[b + 2 * t][:, 0:n], ACT.Copy,
                                   scale=float(MLA_QK) ** -0.5).then_inc(mla_q, 1)
            split(U["ukv"] + NSPLIT)
            for k in range(4):
                act.wait_ge(g_ot, k // 2 + 1)
                act.activation(xt_hi[:, k, :], bank[4 + k // 2][:, (k % 2) * S:(k % 2 + 1) * S],
                               ACT.Copy).then_inc(xth, 1)
            feature_major("mla")
            attention("mla")
            mix_out(0)
            norm(2)
            ffn(1)
            norm(3)
            ffn(2)
            norm(4)
            project("nsa", U["nsa_in"], NSA_BLOCKS)
            act.wait_ge(pj_evac, PROJ0["nsa"] + len(NSA_BLOCKS))
            act.activation(gate[:, :, :], proj[:, :, NS_G:NS_G + 48], ACT.Sigmoid).then_inc(c_gate, 1)
            for m, b in enumerate((4, 5)):
                act.wait_ge(c_b, m + 1)
                dst = hid[m].rearrange("p (g n) -> p g n", g=4)[:, :, 0:NCMP]
                src = bank[b][:, 0:60].rearrange("p (g n) -> p g n", g=4)
                act.activation(dst, src, ACT.Silu, bias=small[:, 0, m:m + 1]).then_inc(c_hid, 1)
            feature_major("nsa")
            act.wait_ge(c_sc, 1)
            act.activation(pc, sc, ACT.Exp).then_inc(c_e, 1)
            attention("nsa")
            mix_out(1)
            norm(5)
            ffn(3)
            for t in range(NT):
                act.wait_ge(x_upd, 4 * 6 - 2 + 2 * t)
                act.activation(xn[:, t, :], X[:, t, :], ACT.Square, accum_out=ss[:, t:t + 1]).then_inc(sq_done, 1)
            for l in range(2):
                norm(6 + 2 * l)
                project(f"sec{l}", U[f"sec_in{l}"], SEC_BLOCKS, lambda c: sec_rms(l, c))
                feature_major(f"sec{l}")
                attention(f"sec{l}")
                act.wait_ge(e_m, 2 * l + 1)
                act.activation(o_rs, o_rs, ACT.Sqrt).then_inc(e_mr, 1)
                for place in range(KD):
                    act.wait_ge(o_scaled, 8 * l + place + 1)
                    act.activation(xt_hi[:, place, :], o_t[:, place, :], ACT.Copy).then_inc(xth, 1)
                mix_out(2 + l)
                norm(7 + 2 * l)
                ffn(4 + l)

        @block.vector
        def _(dve):
            own = [0]

            def link(ins):
                own[0] += 1
                ins.then_inc(dve_own, 1)
                dve.wait_ge(dve_own, own[0])

            def split(u, i=None):
                if u >= N_UNITS:
                    return
                sl = u % NSPLIT
                dve.wait_ge(hi_done, on(u + 1, 6, i))
                dve.tensor_tensor(w_lo[:, sl, :], raw[:, sl, :], w_hi[:, sl, :].bitcast(F32),
                                  ALU.subtract).then_inc(lo_done, 1)

            def mean_squares(r, lo, n, scale):
                return dve.tensor_scalar(ms[:, lo:lo + n], ss[:, lo:lo + n], scale, EPS, ALU.mult, ALU.add)

            def norm(n):
                r = rms_turn(n)
                dve.wait_ge(sq_done, 2 * (r + 1))
                mean_squares(r, 0, 2, 1.0 / D).then_inc(ms_done, 1)
                dve.wait_ge(rstd_done, r + 1)
                dve.tensor_scalar(xn[:, 0, :], X[:, 0, :], rstd[:, 0:1], None, ALU.mult).then_inc(xn0, 1)
                q, g0 = TURN[f"n{n}"], G_NORM + 8 * n
                for k in range(KD):
                    dve.wait_ge(xth, 8 * q + 2 * (k // 2) + 2)
                    src = bank[4 + k // 2][:, (k % 2) * S:(k % 2 + 1) * S]
                    hi = xt_hi[:, k, :].bitcast(F32)
                    dve.scalar_tensor_tensor(xt_lo[:, k, :], src, gcol[:, g0 + k:g0 + k + 1], hi,
                                             ALU.mult, ALU.subtract).then_inc(xtl, 1)

            def project(u0, blocks, after=None):
                for c in range(len(blocks)):
                    split(u0 + c + NSPLIT)
                    if after:
                        after(c)

            def sec_rms(l, c):
                for n, (_, m, o, last) in enumerate(SEC_KINDS):
                    if c == last:
                        dve.wait_ge(e_sq, 6 * l + 2 * n + 2)
                        link(dve.tensor_reduce(head_rms(ss, n), work[:, 0:2 * m * 64].rearrange(
                            "p (t h d) -> p t h d", t=NT, d=64), X_AXIS, ALU.add))
                        dve.tensor_scalar(head_rms(ms, n), head_rms(ss, n), 1.0 / 64, EPS, ALU.mult,
                                          ALU.add).then_inc(e_ms, 1)
                    if c == last + (1 if n < 2 else 0):
                        dve.wait_ge(e_rt, 3 * l + n + 1)
                        r, q = head_rms(rstd, n), head_rms(ss, n)
                        link(dve.reciprocal(r, r))
                        link(dve.tensor_tensor(q, r, r, ALU.mult))
                        link(dve.tensor_tensor(q, q, head_rms(ms, n), ALU.mult))
                        link(dve.tensor_scalar(q, q, -0.5, 1.5, ALU.mult, ALU.add))
                        dve.tensor_tensor(r, r, q, ALU.mult).then_inc(e_rs, 1)
                        dve.wait_ge(e_rs, 3 * l + n + 1)
                if c == SEC_KINDS[2][3] + 1:
                    sec_heads(dve, link, 2, 0, l, QT[:, 2560:3072])
                    dve.sem_inc(ft_ready_d, 1)

            def update_x(scale, first_bank):
                for j in range(4):
                    t, half = j // 2, j % 2
                    dst = X[:, t, half * 512:(half + 1) * 512]
                    dve.scalar_tensor_tensor(dst, bank[first_bank + j][:, :], scale, dst, ALU.mult, ALU.add).then_inc(x_upd, 1)

            def mix_out(m):
                u0 = U[f"mix{m}"]
                for c in range(OUT_UNITS):
                    if c == OUT_UNITS - 1:
                        dve.wait_ge(unit_used, u0 + OUT_UNITS)
                        update_x(1.0, 0)
                    split(u0 + c + NSPLIT)

            def triple(f, s, i):
                par = s % 2
                split(ffn_unit(f, "g", s) + NSPLIT, i)
                split(ffn_unit(f, "u", s) + NSPLIT, i)
                if f >= 4:
                    l = f - 4
                    for j in range(2):
                        y, g = conv_y[:, par, j * S:(j + 1) * S], bank[2 * par][:, j * S:(j + 1) * S]
                        dve.wait_ge(cv_mid, on(2 * (l * STEPS + s) + 2, 4, i))
                        dve.scalar_tensor_tensor(y[:, 1:S], g[:, 0:S - 1], tap(l, 0, s, j, i), y[:, 1:S], ALU.mult,
                                                 ALU.add).then_inc(cv_left, 1)
                    for j in range(2):
                        y, g = conv_y[:, par, j * S:(j + 1) * S], bank[2 * par][:, j * S:(j + 1) * S]
                        dve.wait_ge(cv_left, on(2 * (l * STEPS + s) + j + 1, 4, i))
                        ins = dve.scalar_tensor_tensor(y[:, 0:S - 1], g[:, 1:S], tap(l, 2, s, j, i), y[:, 0:S - 1],
                                                       ALU.mult, ALU.add)
                    ins.then_inc(cv_done, 1)
                dve.wait_ge(actg_done, on(f * STEPS + s + 1, 2, i))
                dve.wait_ge(unit_used, on(ffn_unit(f, "u", s) + 1, 6, i))
                if f or s:
                    dve.wait_ge(hl_done, on(f * STEPS + s, 2, i))
                dve.tensor_tensor(h_f, act_g[:, par, :], bank[2 * par + 1][:, :], ALU.mult).then_inc(mul_done, 1)
                dve.wait_ge(hh_done, on(f * STEPS + s + 1, 2, i))
                dve.tensor_tensor(h_lo[:, par, :], h_f, h_hi[:, par, :].bitcast(F32), ALU.subtract).then_inc(hl_done, 1)
                if s:
                    split(ffn_unit(f, "d", s - 1) + NSPLIT, i)

            def ffn(f):
                ffn_steps(dve, f, triple)
                dve.wait_ge(unit_used, U[f"ffn{f}"] + FFN_UNITS)
                update_x(0.5 if f < 4 else 1.0, 4)
                split(ffn_unit(f, "d", STEPS - 1) + NSPLIT)

            def feature_major(stage):
                d0, g0 = FT_D0[stage], FT_A0[stage] + FT_D0[stage]
                for g, (srcs, rows, dst) in enumerate(ft_groups(stage)):
                    if g % 2 == 0:
                        continue
                    dve.wait_ge(ft_ps, g0 + g + 1)
                    src = bank[g % 4][0:rows, :].rearrange("p (h s) -> p h s", h=2)
                    dve.tensor_scalar(dst[0], src, ft_scale(stage, g), None, ALU.mult).then_inc(ft_d, 1)

            def attention(stage):
                jobs, j0 = heads[stage], JOB0[stage]

                def maxima(i):
                    if i >= len(jobs):
                        return
                    dve.wait_ge(s_done, j0 + i + 1)
                    b, job = bank[S_BANKS[i % 3]], jobs[i]
                    if job["causal"]:
                        for qt in range(NT):
                            ins = dve.tensor_reduce(negmax[:, i % 4, qt:qt + 1], b[:, qt * S:qt * S + ncols(job, qt)],
                                                    X_AXIS, ALU.max, negate=True)
                    else:
                        ins = dve.tensor_reduce(negmax[:, i % 4, :], b[:, :].rearrange("p (q s) -> p q s", q=2),
                                                X_AXIS, ALU.max, negate=True)
                    ins.then_inc(nm_done, 1)

                def evac(i):
                    dve.wait_ge(t_done, j0 + i + 1)
                    if i >= 2:
                        dve.wait_ge(pv_done, j0 + i - 1)
                    n = P * len(pt_blocks(jobs[i]))
                    dve.tensor_copy(pts_of(i % 2, 0, n), bank[2 + i % 2][:, 0:n]).then_inc(pt_evac, 1)

                def lo_part(pair):
                    if pair is None or stage[:3] == "sec":
                        return
                    place = pair + (4 if stage == "mla" else 0)
                    dve.wait_ge(xth, 8 * TURN["m0" if stage == "mla" else "m1"] + place + 1)
                    dve.tensor_tensor(xt_lo[:, place, :], bank[4 + pair % 2][:, 0:S], xt_hi[:, place, :].bitcast(F32),
                                      ALU.subtract).then_inc(xtl, 1)

                def scale(i):
                    if i >= len(jobs):
                        return
                    dve.wait_ge(exp_done, 2 * (j0 + i + 1))
                    link(dve.reciprocal(rsum[:, i % 4, :], sums[:, i % 4, :]))
                    for qt in range(NT):
                        v = p_of(i % 2, qt, 0, ncols(jobs[i], qt))
                        if stage == "nsa":
                            c = 3 * jobs[i]["q"] + 1 + i % 2
                            ins = dve.tensor_scalar(v, v, rsum[:, i % 4, qt:qt + 1], gate[:, qt, c:c + 1], ALU.mult,
                                                    ALU.mult)
                        else:
                            ins = dve.tensor_scalar(v, v, rsum[:, i % 4, qt:qt + 1], None, ALU.mult)
                    ins.then_inc(p_scaled, 1)

                maxima(0)
                maxima(1)
                scale(0)
                for i in range(len(jobs)):
                    maxima(i + 2)
                    scale(i + 1)
                    evac(i)
                    lo_part(pair_after(stage, i, 2))
                for pair in late_pairs(stage, 2):
                    lo_part(pair)

            dve.wait_ge(cst_in, 16)
            dve.tensor_copy(ident_b[:, :], ident)
            dve.tensor_copy(causal_b[:, :], const("causal")).then_inc(const_ready, 1)
            norm(0)
            for u in range(NSPLIT):
                split(u)
            dve.wait_ge(par_in, 16 * N_PAR)
            link(dve.tensor_scalar(head_gain[:, :, 0:3, :], head_gain[:, :, 0:3, :], 0.125, None, ALU.mult))
            link(dve.tensor_copy(pos_f[:, :], pos_i[:, :]))
            fr = const("freq")
            for j in range(3):
                link(dve.tensor_scalar(ang[:, j, :], fr, pos_f[:, j:j + 1], None, ALU.mult))
            TWO_PI = 2 * np.pi
            C1 = 6.28125
            C2 = float(np.float32(np.round((TWO_PI - C1) * 2 ** 20) / 2 ** 20))
            C3 = float(np.float32(TWO_PI - C1 - C2))
            MAGIC = 1.5 * 2 ** 23

            def reduced(dst, shift):
                k = rsin[:, :, :]
                link(dve.tensor_scalar(k, ang[:, :, :], float(1 / TWO_PI), 0.25 * shift, ALU.mult, ALU.add))
                link(dve.tensor_scalar(k, k, MAGIC, MAGIC, ALU.add, ALU.subtract))
                link(dve.scalar_tensor_tensor(dst, k, -C1, ang[:, :, :], ALU.mult, ALU.add))
                link(dve.scalar_tensor_tensor(dst, k, -C2, dst, ALU.mult, ALU.add))
                link(dve.scalar_tensor_tensor(dst, k, -C3, dst, ALU.mult, ALU.add))
                if shift:
                    link(dve.tensor_scalar(dst, dst, float(np.pi / 2), None, ALU.add))
                link(dve.tensor_scalar(dst, dst, 3.1415925, -3.1415925, ALU.min, ALU.max))

            reduced(tmp48[:, :, :], 1)
            reduced(red[:, :, :], 0)
            dve.sem_inc(rope_arg, 1)
            ffn(0)
            norm(1)
            project(U["hy_in"], HY_BLOCKS)
            dve.wait_ge(pj_evac, 8)
            dve.memset(gla_aT[0:32, :], 1.0).then_inc(g_evd, 1)
            dve.memset(gla_qz, 0.0).then_inc(g_evd, 1)
            dve.wait_ge(g_tp, 2)
            dve.tensor_copy(gla_k, bank[1][:, :]).then_inc(g_evd, 1)
            dve.wait_ge(g_ln, 1)
            dve.scalar_tensor_tensor(gla_la, bank[3][:, :], 0.0, gla_ln, ALU.min, ALU.subtract).then_inc(g_la, 1)
            dve.wait_ge(g_bt, 1)
            b4 = chunks(gla_b)
            last = b4[:, :, :, 63:64].to_broadcast([P, 2, 4, 64])
            dve.tensor_tensor(chunks(gla_d), b4, last, ALU.subtract).then_inc(g_d, 1)
            dve.wait_ge(g_e, 3)
            dve.wait_ge(g_evd, 3)
            dve.tensor_tensor(gla_qi, gla_q, gla_ei, ALU.mult).then_inc(g_qk, 1)
            dve.tensor_tensor(gla_kd, gla_k, gla_ed, ALU.mult).then_inc(g_qk, 1)
            qz = gla_qz.rearrange("p (a c i) -> p a c i", a=2, c=4)
            for half in range(2):
                dst = qz[:, :, half:4:2, half * 64:half * 64 + 64]
                ins = dve.tensor_tensor(dst, chunks(gla_q)[:, :, half:4:2, :], chunks(gla_eb)[:, :, half:4:2, :],
                                        ALU.mult)
            ins.then_inc(g_qk, 1)
            dve.wait_ge(g_a, 1)
            tri = const("block_tri").unsqueeze(1).to_broadcast([P, 4, P])
            for t in range(NT):
                ins = dve.tensor_tensor(gla_am[:, t * 512:(t + 1) * 512].rearrange("p (h i) -> p h i", h=4),
                                        bank[t][:, :].rearrange("p (h i) -> p h i", h=4), tri, ALU.mult)
            ins.then_inc(g_am, 1)
            st = gla_st.rearrange("p (a c v) -> p a c v", a=2, c=4)
            eb = chunks(gla_eb)
            for c in range(3):
                dve.wait_ge(g_kv, c + 1)
                if c:
                    dve.wait_ge(g_st, c)
                for a in range(2):
                    for hh in range(2):
                        r = slice(64 * hh, 64 * hh + 64)
                        kv = bank[3 + c][r, a * 256 + hh * P:a * 256 + (hh + 1) * P]
                        if c == 0:
                            ins = dve.tensor_copy(st[r, a, 1, :], kv)
                        else:
                            ins = dve.scalar_tensor_tensor(st[r, a, c + 1, :], st[r, a, c, :], eb[r, a, c, 63:64], kv,
                                                           ALU.mult, ALU.add)
                ins.then_inc(g_st, 1)
            dve.wait_ge(g_o, 1)
            gsq = QT[:, 0:1024]
            o_gla = gla_qz.rearrange("p (t a e v) -> p t a e v", t=2, a=2, e=2)
            for t in range(NT):
                for e, b in ((0, bank[6 + t]), (1, bank[t])):
                    link(dve.tensor_copy(o_gla[:, t, :, e, :], b[:, 0:256].rearrange("p (a v) -> p a v", a=2)))
            link(dve.tensor_tensor(gsq, gla_qz, gla_qz, ALU.mult))
            link(dve.tensor_reduce(ss[:, 16:24], gsq.rearrange("p (h d) -> p h d", d=P), X_AXIS, ALU.add))
            mean_squares(0, 16, 8, 1.0 / GLA_DV).then_inc(g_ms, 1)
            dve.wait_ge(g_rs, 1)
            o8 = gla_qz.rearrange("p (h d) -> p h d", d=P)
            link(dve.tensor_tensor(o8, o8, rstd[:, 16:24].unsqueeze(2).to_broadcast([P, 8, P]), ALU.mult))
            link(dve.tensor_tensor(o8, o8, gla_row[:, :].unsqueeze(1).to_broadcast([P, 8, P]), ALU.mult))
            dve.wait_ge(g_sr, 1)
            dve.tensor_tensor(O[:, :, 512:1024], gla_qz.rearrange("p (t n) -> p t n", t=2),
                              gla_sr.rearrange("p (t n) -> p t n", t=2), ALU.mult).then_inc(mla_up, 1)
            dve.wait_ge(mla_sq, 4)
            link(mean_squares(0, 8, 2, 1.0 / 256))
            mean_squares(0, 10, 2, 1.0 / 128).then_inc(mla_ms, 1)
            dve.wait_ge(mla_rs, 1)
            for n, (c, w) in enumerate(((HY_CQ, 256), (HY_CKV, 128))):
                for t in range(NT):
                    v = proj[:, t, c:c + w]
                    dve.tensor_scalar(v, v, rstd[:, 8 + 2 * n + t:9 + 2 * n + t], None, ALU.mult).then_inc(mla_cn, 1)
            for k in range(3):
                dve.wait_ge(mla_ch, 2 if k < 2 else 3)
                src = bank[0][:, k * S:(k + 1) * S] if k < 2 else bank[1][:, 0:S]
                dve.scalar_tensor_tensor(xt_lo[:, k, :], src, gcol[:, G_Q + k:G_Q + k + 1], xt_hi[:, k, :].bitcast(F32),
                                         ALU.mult, ALU.subtract).then_inc(mla_cl, 1)
            split(U["uq"] + NSPLIT)
            dve.wait_ge(unit_used, U["ukv"] + 1)
            for t in range(NT):
                for half in range(2):
                    link(dve.tensor_copy(work[:, 2048 + t * 1024 + half * 512:2048 + t * 1024 + half * 512 + 512],
                                         bank[2 * t + half][:, :]))
            split(U["ukv"] + NSPLIT)
            dve.wait_ge(mla_q, 4)
            dve.wait_ge(rope_tab, 2)
            for t in range(NT):
                v = work[:, t * 768:(t + 1) * 768].rearrange("p (h d) -> p h d", h=MLA_H)
                rope_heads(dve, link, v, MLA_NOPE, 16, rcos[:, t, 0:16], rsin[:, t, 0:16], prob[:, 0:1024])
            dve.sem_inc(ft_ready_d, 1)
            for k in range(4):
                dve.wait_ge(xth, 8 * TURN["m0"] + 2 * (k // 2) + 2)
                dve.tensor_tensor(xt_lo[:, k, :], bank[4 + k // 2][:, (k % 2) * S:(k % 2 + 1) * S],
                                  xt_hi[:, k, :].bitcast(F32), ALU.subtract).then_inc(xtl, 1)
            feature_major("mla")
            attention("mla")
            mix_out(0)
            norm(2)
            ffn(1)
            norm(3)
            ffn(2)
            norm(4)
            project(U["nsa_in"], NSA_BLOCKS)
            dve.wait_ge(c_dup, 2)
            for m, mt in enumerate((m_k, m_v)):
                if m == 1:
                    dve.wait_ge(c_tp, 4)
                link(dve.memset(mt[:, 4, :], 0.0))
                link(dve.tensor_copy(mt[:, 4, 0:32:2], posr[:, m, :]))
                for gp in range(2):
                    dve.wait_ge(c_tp, 2 * m + gp + 1)
                    src = bank[2 * m + gp][:, :].rearrange("p (g s) -> p g s", g=2)
                    dve.tensor_copy(mt[0:64, 2 * gp:2 * gp + 2, :], src[0:64, :, :]).then_inc(c_m, 1)
                    dve.tensor_copy(mt[64:128, 2 * gp:2 * gp + 2, 0:S - 1], src[64:128, :, 1:S]).then_inc(c_m, 1)
            for m in range(2):
                dve.wait_ge(c_h, m + 1)
                dve.memset(hid[m], 0.0)
                dve.tensor_copy(small[:, 0, m:m + 1], bank[4 + m][:, 60:61]).then_inc(c_b, 1)
            dve.wait_ge(c_kc, 1)
            link(dve.tensor_copy(kc_tok, bank[6][:, 0:64]))
            link(dve.memset(vcz, 0.0))
            for g in range(NS_GR):
                dve.tensor_copy(vcz[32 * g:32 * g + 32, g, :], bank[6][32 * g:32 * g + 32, 64:128])
            rope_heads(dve, link, kc_tok.rearrange("p (h d) -> p h d", h=1), 0, 32, rcos[:, 2, 16:48],
                       rsin[:, 2, 16:48], rope_t)
            dve.sem_inc(c_kr, 1)
            for c, n in ((NS_Q, 16), (NS_KS, 4), (NS_KW, 4)):
                v = proj[:, 0, c:c + n * 64].rearrange("p (h d) -> p h d", h=n)
                rope_heads(dve, link, v, 0, 32, rcos[:, 0, 16:48], rsin[:, 0, 16:48], QT[:, 1024:2048])
            dve.sem_inc(ft_ready_d, 1)
            feature_major("nsa")
            dve.wait_ge(c_kt, 1)
            dve.tensor_copy(kcT_[0:64, :], bank[6][0:64, 0:P]).then_inc(c_kcT, 1)
            dve.wait_ge(c_s, 1)
            s4 = sc.rearrange("p (t h n) -> p t h n", t=2, n=32)
            p4 = pc.rearrange("p (t h n) -> p t h n", t=2, n=32)
            add = const("cmp_add").rearrange("p (t n) -> p t n", t=2)
            keep = const("cmp_01").rearrange("p (t n) -> p t n", t=2)
            for t in range(NT):
                link(dve.tensor_tensor(s4[:, t], bank[6 + t][:, :].rearrange("p (h n) -> p h n", n=32),
                                       add[:, t, :].unsqueeze(1).to_broadcast([P, 16, 32]), ALU.add))
            link(dve.tensor_reduce(small[:, 1, :], sc.rearrange("p (h n) -> p h n", n=32), X_AXIS, ALU.max))
            s3 = sc.rearrange("p (h n) -> p h n", n=32)
            dve.tensor_tensor(s3, s3, small[:, 1, :].unsqueeze(2).to_broadcast([P, 32, 32]), ALU.subtract)\
               .then_inc(c_sc, 1)
            dve.wait_ge(c_e, 1)
            for t in range(NT):
                link(dve.tensor_tensor(p4[:, t], p4[:, t], keep[:, t, :].unsqueeze(1).to_broadcast([P, 16, 32]),
                                       ALU.mult))
            dve.tensor_reduce(small[:, 2, :], pc.rearrange("p (h n) -> p h n", n=32), X_AXIS, ALU.add).then_inc(c_p, 1)
            dve.wait_ge(c_p, 1)
            link(dve.tensor_scalar(small[:, 2, :], small[:, 2, :], TINY, None, ALU.max))
            link(dve.reciprocal(small[:, 3, :], small[:, 2, :]))
            dve.wait_ge(c_gate, 1)
            for t in range(NT):
                coef = small[:, 1, t * 16:(t + 1) * 16].rearrange("p (j g) -> p j g", j=4)
                inv = small[:, 3, t * 16:(t + 1) * 16].rearrange("p (j g) -> p j g", j=4)
                gt = gate[:, t, :].rearrange("p (g j b) -> p j g b", g=4, b=3)[:, :, :, 0]
                link(dve.tensor_tensor(coef, inv, gt, ALU.mult))
            pc3 = pc.rearrange("p (h n) -> p h n", n=32)
            dve.tensor_tensor(pc3, pc3, small[:, 1, :].unsqueeze(2).to_broadcast([P, 32, 32]), ALU.mult).then_inc(c_p, 1)
            dve.wait_ge(c_pt, 1)
            for t in range(NT):
                ins = dve.tensor_copy(pct[:, t * 512:(t + 1) * 512], bank[6 + t][:, :])
            ins.then_inc(c_pe, 1)
            attention("nsa")
            mix_out(1)
            norm(5)
            ffn(3)
            dve.wait_ge(sq_done, 2 * 7)
            mean_squares(6, 0, 2, 1.0 / D).then_inc(ms_done, 1)
            dve.wait_ge(rstd_done, 7)
            dve.wait_ge(f_in, 16)
            frow = O[:, 0, :]
            for t in range(NT):
                dve.scalar_tensor_tensor(X[:, t, :], X[:, t, :], rstd[:, t:t + 1], frow, ALU.mult,
                                         ALU.mult).then_inc(x_upd, 2)
            for l in range(2):
                norm(6 + 2 * l)
                project(U[f"sec_in{l}"], SEC_BLOCKS, lambda c: sec_rms(l, c))
                feature_major(f"sec{l}")
                attention(f"sec{l}")
                dve.wait_ge(o_sum, 8 * (l + 1))
                link(dve.tensor_scalar(o_rs[:, 0:2 * S], bank[7][:, :], 1.0 / 384, EPS, ALU.mult, ALU.add))
                dve.tensor_scalar(o_rs[:, 2 * S:3 * S], bank[1][:, 0:S], 1.0 / 256, EPS, ALU.mult, ALU.add).then_inc(e_m, 1)
                dve.wait_ge(e_mr, l + 1)
                dve.reciprocal(o_rs, o_rs).then_inc(e_m, 1)
                dve.wait_ge(e_m, 2 * l + 2)

                def scale(place):
                    g = G_OUT + 8 * l + out_tile(2, place)
                    kind = kind_of(place)
                    dve.scalar_tensor_tensor(o_t[:, place, :], o_t[:, place, :], gcol[:, g:g + 1],
                                             o_rs[:, kind * S:(kind + 1) * S], ALU.mult, ALU.mult).then_inc(o_scaled, 1)

                scale(0)
                for place in range(KD):
                    if place + 1 < KD:
                        scale(place + 1)
                    dve.wait_ge(xth, 8 * TURN[f"m{2 + l}"] + place + 1)
                    dve.tensor_tensor(xt_lo[:, place, :], o_t[:, place, :], xt_hi[:, place, :].bitcast(F32),
                                      ALU.subtract).then_inc(xtl, 1)
                mix_out(2 + l)
                norm(7 + 2 * l)
                ffn(4 + l)

        @block.gpsimd
        def _(pool):
            own = [0]

            def link(ins):
                own[0] += 1
                ins.then_inc(pool_own, 1)
                pool.wait_ge(pool_own, own[0])

            def inv_sqrt(lo, n):
                return pool.tensor_tensor(rstd[:, lo:lo + n], ms[:, lo:lo + n], neg_half[:, lo:lo + n], ALU.pow)

            def norm(r):
                pool.wait_ge(ms_done, r + 1)
                inv_sqrt(0, 2).then_inc(rstd_done, 1)

            def fetch_bias(l):
                for r2 in range(2):
                    for qt in range(NT):
                        for h in range(4):
                            at = rpb2[l, h, 7 - (2 * qt + r2), 15:16]
                            src = bass.AP(tensor=at.tensor, offset=at.offset - (GRID - 1), ap=[[1, 64], [31, 4], [1, 64]])
                            pool.dma_start(na_bias[64 * r2:64 * r2 + 64, qt, h, :], src).then_inc(b_in, 16)

            def mask_bias(l):
                pool.wait_ge(b_in, 256 * (l + 1))
                v = work[:, 2048:4096].rearrange("p (n c) -> p n c", c=64)
                m = const("na_mask").unsqueeze(1).to_broadcast([P, 32, 64])
                pool.tensor_tensor(v, v, m, ALU.add).then_inc(na_ready, 1)

            pool.wait_ge(cst_in, 16)
            link(pool.memset(neg_half[:, :], -0.5))
            norm(0)
            norm(1)
            pool.wait_ge(g_ms, 1)
            inv_sqrt(16, 8).then_inc(g_rs, 1)
            pool.wait_ge(pj_evac, 8)
            pool.wait_ge(rope_tab, 2)
            for t in range(NT):
                v = proj[:, t, HY_KR:HY_KR + 32].rearrange("p (h d) -> p h d", h=1)
                rope_heads(pool, link, v, 0, 16, rcos[:, t, 0:16], rsin[:, t, 0:16], small[:, 2, :])
            pool.sem_inc(ft_ready_p, 1)
            pool.wait_ge(mla_ms, 1)
            inv_sqrt(8, 4).then_inc(mla_rs, 1)
            for r in (2, 3, 4):
                norm(r)
                if r == 2:
                    for m, dst in enumerate((prob[:, :], O[:, :, :].rearrange("p t d -> p (t d)"))):
                        pool.dma_start(dst, cmp_w1[m]).then_inc(c_w, 16)
            pool.wait_ge(pj_evac, 8 + 11)
            for m, c in enumerate((NS_KC, NS_VC)):
                for t in range(NT):
                    src = proj[:, t, c:c + 256].rearrange("p (g d) -> p g d", g=4)
                    for e in range(2):
                        ins = pool.tensor_copy(dup[:, m, t, :, e, :], src)
                ins.then_inc(c_dup, 1)
            for c, n in ((NS_Q, 16), (NS_KS, 4), (NS_KW, 4)):
                v = proj[:, 1, c:c + n * 64].rearrange("p (h d) -> p h d", h=n)
                rope_heads(pool, link, v, 0, 32, rcos[:, 1, 16:48], rsin[:, 1, 16:48], QT[:, 2048:3072])
            pool.sem_inc(ft_ready_p, 1)
            norm(5)
            pool.dma_start(O[:, 0, :], final_gain.partition_broadcast(P)).then_inc(f_in, 16)
            norm(6)
            for l in range(2):
                norm(7 + 2 * l)
                fetch_bias(l)
                for n in range(3):
                    pool.wait_ge(e_rs, 3 * l + n + 1)
                    for t in ((0, 1) if n < 2 else (1,)):
                        sec_heads(pool, link, n, t, l, QT[:, 3072:4096])
                    pool.sem_inc(ft_ready_p, 1)
                mask_bias(l)
                norm(8 + 2 * l)


def _stream(a):
    s = np.zeros((N_UNITS, P, UNIT), np.float32)

    def columns(u, w, c0, n):
        k = w.shape[0] // P
        s[u].reshape(P, k, UNIT // k)[:, :, 0:n] = w[:, c0:c0 + n].reshape(k, P, n).transpose(1, 0, 2)

    def rows(u, w, r0):
        s[u].reshape(P, 2, D)[:] = w[r0:r0 + 2 * P].reshape(2, P, D).transpose(1, 0, 2)

    def ffn(f, gate, up, down):
        u0 = U[f"ffn{f}"]
        for t in range(STEPS):
            g = u0 + max(3 * t - 1, 0)
            columns(g, gate, 256 * t, 256)
            columns(g + 1, up, 256 * t, 256)
            rows(u0 + (FFN_UNITS - 1 if t == STEPS - 1 else 3 * t + 4), down, 256 * t)

    def project(u0, w, blocks):
        for c, n in enumerate(blocks):
            columns(u0 + c, w, 256 * c, n)

    for f in range(4):
        ffn(f, *(a[n][f // 2, f % 2] for n in ("ffn_w_gate", "ffn_w_up", "ffn_w_down")))
    at = dict(zip(SEC_W, np.cumsum([0] + list(SEC_W.values()))))
    sec_cols = np.concatenate([at[m] + np.arange(SEC_W[m]) for m in SEC_ORDER])
    for l in range(2):
        gu = a["w_gate_up_2"][l]
        ffn(4 + l, gu[:, :D_FF], gu[:, D_FF:], a["w_down_2"][l])
        project(U[f"sec_in{l}"], a["w_in_2"][l][:, sec_cols], SEC_BLOCKS)
    project(U["hy_in"], a["hy_w_in"][0], HY_BLOCKS)
    project(U["nsa_in"], a["nsa_w_in"][0], NSA_BLOCKS)
    s[U["uq"]][:, 0:1536] = a["mla_w_uq"][0].reshape(2, P, 768).transpose(1, 0, 2).reshape(P, 1536)
    s[U["ukv"]][:, 0:1024] = a["mla_w_ukv"][0]
    for m, w in enumerate((a["hy_w_out"][0], a["nsa_w_out"][0], a["w_out_2"][0], a["w_out_2"][1])):
        w = np.concatenate([w[out_tile(m, k) * P:(out_tile(m, k) + 1) * P] for k in range(KD)])
        for c in range(OUT_UNITS):
            rows(U[f"mix{m}"] + c, w, 256 * c)
    return s


def _lay_out(a):
    def cols(v):
        return np.ascontiguousarray(v.reshape(-1, P).T)

    norms = [a["ffn_norm"][0, 0], a["mix_norm"][0], a["ffn_norm"][0, 1], a["ffn_norm"][1, 0], a["mix_norm"][1],
             a["ffn_norm"][1, 1], a["norm1_g_2"][0], a["norm2_g_2"][0], a["norm1_g_2"][1], a["norm2_g_2"][1]]
    gains = np.concatenate([cols(np.stack(norms)), cols(a["out_norm_g_2"]), cols(a["mla_q_norm"]),
                            cols(a["mla_kv_norm"])], 1)
    conv = np.concatenate([a["conv_w_2"], a["conv_b_2"][:, None]], 1).reshape(2, 4, D_FF // P, P).transpose(3, 0, 1, 2)
    pos = a["positions"][0]
    places = np.zeros((P, 3), pos.dtype)
    places[:, 0], places[:, 1] = pos[:P], pos[P:]
    for g in range(NS_GR):
        places[32 * g:32 * g + NCMP, 2] = pos[CMP_LEN - 1::CMP_STRIDE][:NCMP]
    rows = np.stack([a[n][0].reshape(16, P).T for n in ("nsa_pos_k", "nsa_pos_v")], 1)
    w1 = np.stack([a[n][0].reshape(16, P, P).transpose(1, 0, 2).reshape(P, 2048) for n in ("nsa_ck_w1", "nsa_cv_w1")])
    w2 = np.stack([a["nsa_ck_w2"][0], a["nsa_cv_w2"][0]])
    return {"stream": _stream(a), "consts": shape_constants(), "gains": gains, "conv": conv, "x": a["x"],
            "positions": places, "pos_rows": rows, "cmp_w1": w1, "cmp_w2": w2, "final_gain": a["final_norm"],
            "gla_gain": a["gla_out_norm"], "gla_a2": a["gla_w_a2"], "gla_ba": a["gla_b_a"],
            "q_gain2": a["q_norm_g_2"], "k_gain2": a["k_norm_g_2"], "rpb2": a["rpb_2"]}


def kernel(**inputs):
    import concourse.bacc as _bacc
    from concourse.bass_utils import run_bass_kernel_spmd as _run

    nc = _bacc.Bacc("TRN2", target_bir_lowering=False, num_devices=1)
    arrays, args = {}, []
    for name, v in _lay_out({k: np.asarray(v) for k, v in inputs.items()}).items():
        v = np.ascontiguousarray(v)
        arrays[f"in_{name}"] = v
        args.append(nc.dram_tensor(f"in_{name}", v.shape, mybir.dt.from_np(v.dtype), kind="ExternalInput").ap())
    args.append(nc.dram_tensor("out_0", (1, S, D), F32, kind="ExternalOutput").ap())
    build(nc, *args)
    r = _run(nc, [arrays], core_ids=[0])
    return r.results[0]["out_0"]
```

```python
from contextlib import ExitStack

import numpy as np

import concourse.bass as bass
from concourse import mybir

F32 = mybir.dt.float32
F32R = mybir.dt.float32r
BF16 = mybir.dt.bfloat16
I32 = mybir.dt.int32
ALU = mybir.AluOpType
ACT = mybir.ActivationFunctionType
X_AXIS = mybir.AxisListType.X

P = 128
S = 256
NT = S // P
D = 1024
KD = D // P
D_FF = 2816
STEPS = D_FF // 256
EPS = 1e-6
NEG = -1e30
TINY = 1e-30

UNIT = 2048
S_BANKS = (0, 1, 6)
NRAW = 3
NSPLIT = 3

HY_W = dict(cq=256, ckv=128, kr=32, gq=256, gk=256, gv=512, ga=16, gr=512)
HY_ORDER = ("gq", "gk", "ckv", "kr", "ga", "cq", "gv", "gr")
HY_GQ, HY_GK, HY_CKV, HY_KR, HY_GA, HY_CQ, HY_GV, HY_GR = (sum(HY_W[m] for m in HY_ORDER[:i]) for i in range(8))
HY_IN = sum(HY_W.values())
MLA_H, MLA_NOPE, MLA_ROPE, MLA_QK = 8, 64, 32, 96
GLA_H, GLA_DV, GLA_C, GLA_R = 4, 128, 64, 16
NS_W = dict(q=1024, kc=256, vc=256, ks=256, vs=256, kw=256, vw=256, g=48)
NS_ORDER = ("kc", "vc", "q", "g", "ks", "kw", "vs", "vw")
NS_KC, NS_VC, NS_Q, NS_G, NS_KS, NS_KW, NS_VS, NS_VW = (sum(NS_W[m] for m in NS_ORDER[:i]) for i in range(8))
NS_IN = sum(NS_W.values())
NS_H, NS_GR = 16, 4
CMP_LEN, CMP_STRIDE = 32, 16
NCMP = (S - CMP_LEN) // CMP_STRIDE + 1
SEC_W = dict(qa=256, ka=256, va=256, qd=384, kd=384, vd=384, qc=384, kc=128, vc=128)
SEC_ORDER = ("qa", "ka", "qd", "kd", "qc", "kc", "va", "vd", "vc")
QA, KA, QD, KDL, QC, KC, VA, VD, VC = (sum(SEC_W[m] for m in SEC_ORDER[:i]) for i in range(9))
SEC_IN = sum(SEC_W.values())
SEC_KINDS = ((QA, 8, 0, 1), (QD, 12, 8, 4), (QC, 8, 20, 6))
GRID = 64

HY_BLOCKS = [256, 256, 176] + [256] * 5
NSA_BLOCKS = [256] * 6 + [48] + [256] * 4
GLA_KV_BANKS = (4, 5, 2)
UQ_BANKS = ((0, 1), (3, 6))
G_BLOCK = 6
SEC_BLOCKS = [256] * 10

FFN_UNITS = 3 * STEPS
FFN_NORM = [0, 2, 3, 5, 7, 9]
N_PAR = 10
OUT_UNITS = 4
_at, U = 0, {}
for _name, _n in [("ffn0", FFN_UNITS), ("hy_in", 8), ("uq", 1), ("ukv", 1), ("mix0", OUT_UNITS),
                  ("ffn1", FFN_UNITS), ("ffn2", FFN_UNITS), ("nsa_in", 11), ("mix1", OUT_UNITS),
                  ("ffn3", FFN_UNITS), ("sec_in0", 10), ("mix2", OUT_UNITS), ("ffn4", FFN_UNITS),
                  ("sec_in1", 10), ("mix3", OUT_UNITS), ("ffn5", FFN_UNITS)]:
    U[_name] = _at
    _at += _n
N_UNITS = _at

TURN = {n: q for q, n in enumerate(["n0", "n1", "m0", "n2", "n3", "n4", "m1", "n5",
                                    "n6", "m2", "n7", "n8", "m3", "n9"])}
JOB0 = {"mla": 0, "nsa": 8, "sec0": 40, "sec1": 56}
FT_GROUPS = {"mla": 9, "nsa": 12, "sec0": 14, "sec1": 14}
FT_A0, FT_D0 = {}, {}
_a = _d = 0
for _s, _n in FT_GROUPS.items():
    FT_A0[_s], FT_D0[_s] = _a, _d
    _a += (_n + 1) // 2
    _d += _n // 2
PROJ0 = {"hy": 0, "nsa": 8, "sec0": 19, "sec1": 29}


def out_tile(m, place):
    return (place + 4) % KD if m == 0 else place if m == 1 else KD - 1 - place


NORM_STAGE = ["ffn0", "hy_in", "ffn1", "ffn2", "nsa_in", "ffn3", "sec_in0", "ffn4", "sec_in1", "ffn5"]


def rms_turn(n):
    return n + (1 if n >= 6 else 0)


_c, C = 0, {}
for _name, _n in [("ident", 128), ("flip", 128), ("block_tri", 128), ("causal", 128), ("dil", 2 * 256), ("na_mask", 64),
                  ("cmp_add", 64), ("cmp_01", 64), ("freq", 48), ("cos1", 16), ("sin1", 16),
                  ("cosax", 64), ("sinax", 64), ("ones", 128)]:
    C[_name] = (_c, _c + _n)
    _c += _n
N_CONST = _c

G_NORM, G_OUT, G_Q, G_KV, N_GAIN = 0, 80, 96, 98, 99


def shape_constants():
    c = np.zeros((P, N_CONST), np.float32)

    def put(name, a):
        lo, hi = C[name]
        c[:, lo:hi] = np.asarray(a, np.float32).reshape(P, hi - lo)

    p = np.arange(P)
    put("ident", np.eye(P))
    put("ones", np.ones((P, P)))
    put("flip", p[None, :] == p[:, None] // GRID * GRID + GRID - 1 - p[:, None] % GRID)
    put("block_tri", (p[:, None] <= p[None, :]) & (p[:, None] // GLA_C == p[None, :] // GLA_C))
    put("causal", np.where(p[None, :] > p[:, None], NEG, 0.0))
    t = np.arange(S)
    times = np.zeros((S, S))
    for w, d in ((128, 1), (512, 4), (2048, 16)):
        off = t[None, :] - t[:, None]
        times += (off % d == 0) & (np.abs(off) <= (w // 2) // d * d)
    dil = np.where(times > 0, np.log(np.maximum(times, 1)), NEG)
    put("dil", dil.reshape(NT, P, S).transpose(1, 0, 2))
    col = GRID - 1 - p % GRID
    c0 = np.clip(col - 8, 0, GRID - 16)
    kc = np.arange(GRID)
    put("na_mask", np.where((kc[None] >= c0[:, None]) & (kc[None] < c0[:, None] + 16), 0.0, NEG))
    n = np.arange(32)
    ok = (n[None] < NCMP) & (n[None] * CMP_STRIDE + CMP_LEN - 1 <= t[:, None])
    put("cmp_add", np.where(ok, 0.0, NEG).reshape(NT, P, 32).transpose(1, 0, 2))
    put("cmp_01", ok.reshape(NT, P, 32).transpose(1, 0, 2))

    def inv(theta, d):
        e = -np.arange(d // 2, dtype=np.float32) * np.float32(2.0 / d)
        return np.power(np.float64(theta), e.astype(np.float64)).astype(np.float32)

    put("freq", np.broadcast_to(np.concatenate([inv(10000.0, 32), inv(10000.0, 64)]), (P, 48)))

    def tables(pos, theta, d):
        ang = (pos.astype(np.float32)[:, None] * inv(theta, d)[None]).astype(np.float64)
        return np.cos(ang), np.sin(ang)

    for k, f in (("cos", 0), ("sin", 1)):
        one = tables(t, 500000.0, 16)[f]
        put(k + "1", one.reshape(NT, P, 8).transpose(1, 0, 2))
        ax = np.stack([tables(t // GRID, 10000.0, 32)[f], tables(t % GRID, 10000.0, 32)[f]], 1)
        put(k + "ax", ax.reshape(NT, P, 2, 16).transpose(1, 0, 2, 3))
    return c


def build(nc, stream, consts, gains, conv, x, positions, pos_rows, cmp_w1, cmp_w2, final_gain, gla_gain,
          gla_a2, gla_ba, q_gain2, k_gain2, rpb2, out):
    ctx = ExitStack()
    with ctx:
        def sb(name, shape, dt=F32):
            return ctx.enter_context(nc.sbuf_tensor(name, shape, dt))

        def sem(name):
            return ctx.enter_context(nc.semaphore(name))

        bank = [ctx.enter_context(nc.psum_tensor(f"bank{i}", [P, 512], F32)) for i in range(8)]

        raw = sb("raw", [P, NRAW, UNIT])
        w_hi = sb("w_hi", [P, NSPLIT, UNIT], F32R)
        w_lo = sb("w_lo", [P, NSPLIT, UNIT], F32R)
        X = sb("X", [P, NT, D])
        xt_hi = sb("xt_hi", [P, KD, S], F32R)
        xt_lo = sb("xt_lo", [P, KD, S], F32R)
        proj = sb("proj", [P, NT, NS_IN])
        work = sb("work", [P, 2 * 2048])
        QT = sb("QT", [P, 16 * S])
        KT = sb("KT", [P, 12 * S])
        O = sb("O", [P, NT, D])
        prob = sb("prob", [P, 2048])
        h_hi = sb("h_hi", [P, 2, 512], F32R)
        h_lo = sb("h_lo", [P, 2, 512], F32R)
        cst = sb("cst", [P, N_CONST])
        gcol = sb("gcol", [P, N_GAIN])
        ccol = sb("ccol", [P, 2, 4, 22])
        ident_b = sb("ident_b", [P, P], BF16)
        causal_b = sb("causal_b", [P, P], BF16)
        head_gain = sb("head_gain", [P, 2, 6, 64])
        gla_row = sb("gla_row", [P, GLA_DV])
        a2 = sb("a2", [GLA_R + 1, 256])
        w2 = sb("w2", [P, 2, 64])
        posr = sb("posr", [P, 2, 16])
        pos_i = sb("pos_i", [P, 3], I32)
        pos_f = sb("pos_f", [P, 3])
        ang = sb("ang", [P, 3, 48])
        red = sb("red", [P, 3, 48])
        tmp48 = sb("tmp48", [P, 3, 48])
        rsin = sb("rsin", [P, 3, 48])
        rcos = sb("rcos", [P, 3, 48])
        neg_half = sb("neg_half", [P, 56])
        ss = sb("ss", [P, 56])
        ms = sb("ms", [P, 56])
        rstd = sb("rstd", [P, 56])
        negmax = sb("negmax", [P, 4, 2])
        sums = sb("sums", [P, 4, 2])
        rsum = sb("rsum", [P, 4, 2])
        gate = sb("gate", [P, NT, 48])
        small = sb("small", [P, 4, 32])

        def const(name):
            return cst[:, C[name][0]:C[name][1]]

        ident = const("ident")
        xn = work[:, 0:2048].rearrange("p (t d) -> p t d", t=NT)
        na_bias = work[:, 2048:4096].rearrange("p (t h s) -> p t h s", t=NT, h=4)
        act_g = QT[:, 0:1024].rearrange("p (b n) -> p b n", b=2)
        h_f = QT[:, 1024:1536]
        conv_y = QT[:, 1536:2560].rearrange("p (b n) -> p b n", b=2)
        qT = QT[:, :].rearrange("p (h s) -> p h s", s=S)
        kT = KT[:, :].rearrange("p (h s) -> p h s", s=S)

        raw_in = [sem(f"raw_in{i}") for i in range(NRAW)]
        hi_done, lo_done = sem("hi_done"), sem("lo_done")
        unit_used = sem("unit_used")
        x_in = [sem(f"x_in{t}") for t in range(NT)]
        cst_in, gain_in, par_in = sem("cst_in"), sem("gain_in"), sem("par_in")
        x_upd = sem("x_upd")
        x_part = sem("x_part")
        sq_done, ms_done, rstd_done = sem("sq_done"), sem("ms_done"), sem("rstd_done")
        xn0, xn1 = sem("xn0"), sem("xn1")
        xt_ps, xth, xtl = sem("xt_ps"), sem("xth"), sem("xtl")
        actg_done, mul_done, hh_done, hl_done = sem("actg_done"), sem("mul_done"), sem("hh_done"), sem("hl_done")
        cv_mid, cv_left, cv_done = sem("cv_mid"), sem("cv_left"), sem("cv_done")
        pj_evac = sem("pj_evac")
        ft_ready_d, ft_ready_p = sem("ft_ready_d"), sem("ft_ready_p")
        ft_ps, ft_a, ft_d = sem("ft_ps"), sem("ft_a"), sem("ft_d")
        s_done, nm_done, exp_done, t_done = sem("s_done"), sem("nm_done"), sem("exp_done"), sem("t_done")
        pt_evac, pv_done = sem("pt_evac"), sem("pv_done")
        p_scaled = sem("p_scaled")
        o_copied, o_sum, o_scaled = sem("o_copied"), sem("o_sum"), sem("o_scaled")
        dve_own, act_own, pool_own = sem("dve_own"), sem("act_own"), sem("pool_own")
        const_ready, rope_arg, rope_tab = sem("const_ready"), sem("rope_arg"), sem("rope_tab")
        mla_sq, mla_ms, mla_rs, mla_cn, mla_tp, mla_ch, mla_cl, mla_q, mla_kv, mla_up = (
            sem("mla_" + n) for n in ("sq", "ms", "rs", "cn", "tp", "ch", "cl", "q", "kv", "up"))
        g_tp, g_ev, g_evd, g_z, g_ln, g_la, g_b, g_bt, g_d, g_e, g_qk, g_a, g_am, g_kt, g_kd, g_kv, g_st, g_o, \
            g_ms, g_rs, g_sr, g_ot, g_sq = (sem("g_" + n) for n in (
                "tp", "ev", "evd", "z", "ln", "la", "b", "bt", "d", "e", "qk", "a", "am", "kt", "kd", "kv", "st",
                "o", "ms", "rs", "sr", "ot", "sq"))
        c_w, c_dup, c_tp, c_m, c_h, c_b, c_hid, c_kc, c_kr, c_kt, c_kcT, c_s, c_sc, c_e, c_p, c_pt, c_pe, \
            c_gate, c_gt = (sem("c_" + n) for n in (
                "w", "dup", "tp", "m", "h", "b", "hid", "kc", "kr", "kt", "kcT", "s", "sc", "e", "p", "pt", "pe",
                "gate", "gt"))
        b_in, na_ready = sem("b_in"), sem("na_ready")
        e_sq, e_ms, e_rt, e_rs, e_m, e_mr = (sem("e_" + n) for n in ("sq", "ms", "rt", "rs", "m", "mr"))
        f_in = sem("f_in")
        stored = sem("stored")

        block = ctx.enter_context(nc.Block())

        def ffn_unit(f, kind, s):
            u0 = U[f"ffn{f}"]
            if kind == "d":
                return u0 + (FFN_UNITS - 1 if s == STEPS - 1 else 3 * s + 4)
            g = u0 if s == 0 else u0 + 3 * s - 1
            return g if kind == "g" else g + 1

        def ffn_steps(eng, f, triple):
            triple(f, 0, None)
            triple(f, 1, None)
            with eng.Fori(0, 4) as i:
                triple(f, 2, i)
                triple(f, 3, i)
            triple(f, 10, None)

        def on(n, per, i):
            return n if i is None else i * per + n

        def tap(l, n, s, j, i):
            c = on(2 * s + j, 4, i)
            return ccol[:, l, n, c:c + 1] if i is None else ccol[:, l, n, bass.ds(c, 1)]

        heads = {}
        heads["mla"] = [dict(q=h, k=h, d=MLA_QK, causal=True,
                             v=lambda kt, h=h: work[:, 2048 + kt * 1024 + h * 128 + 64:2048 + kt * 1024 + h * 128 + 128])
                        for h in range(MLA_H)]
        heads["nsa"] = [dict(q=h, k=4 * br + h // 4, d=64, causal=True,
                             v=lambda kt, h=h, br=br: proj[:, kt, (NS_VS, NS_VW)[br] + (h // 4) * 64:
                                                           (NS_VS, NS_VW)[br] + (h // 4) * 64 + 64])
                        for h in range(NS_H) for br in range(2)]

        def sec_job(h):
            if h < 4:
                return dict(q=h, k=h, d=64, causal=False, bias=lambda qt: na_bias[:, qt, h, :],
                            v=lambda kt: proj[:, kt, VA + h * 64:VA + h * 64 + 64])
            if h < 10:
                return dict(q=h, k=h, d=64, causal=False, bias=None, dil=True,
                            v=lambda kt: proj[:, kt, VD + (h - 4) * 64:VD + (h - 4) * 64 + 64])
            g = (h - 10) // 3
            return dict(q=h, k=10 + g, d=64, causal=False, bias=None,
                        v=lambda kt: proj[:, kt, VC + g * 64:VC + g * 64 + 64])

        heads["sec0"] = heads["sec1"] = [sec_job(2 * (7 - i // 2) + i % 2) for i in range(16)]
        JOBS_PER_PAIR = {"mla": 2, "nsa": 4, "sec0": 2, "sec1": 2}

        def pair_after(stage, i, lag):
            n = JOBS_PER_PAIR[stage]
            last = i - lag
            return last // n if last >= 0 and last % n == n - 1 else None

        def late_pairs(stage, lag):
            n, jobs = JOBS_PER_PAIR[stage], len(heads[stage])
            return [q for q in range(jobs // n) if (q + 1) * n - 1 + lag >= jobs]

        o_t = O[:, :, :].rearrange("p t (a s) -> p (t a) s", s=S)
        o_sq = work[:, 0:512].rearrange("p (b s) -> p b s", b=2)
        o_rs = work[:, 512:1280]

        def kind_of(place):
            return 0 if place < 3 else 1 if place < 6 else 2

        def ft_groups(stage):
            if stage == "mla":
                gs = [([(lambda t, h=h: work[:, 2048 + t * 1024 + h * 128:2048 + t * 1024 + h * 128 + 64])
                        for h in (2 * g, 2 * g + 1)], 64, [kT[0:64, 2 * g:2 * g + 2, :]]) for g in range(4)]
                gs.append(([lambda t: proj[:, t, HY_KR - 64:HY_KR + 32]], 96, None))
                gs += [([(lambda t, h=h: prob[:, t * 768 + h * 96:t * 768 + h * 96 + 96])
                         for h in (2 * g, 2 * g + 1)], 96, [qT[0:96, 2 * g:2 * g + 2, :]]) for g in range(4)]
                return gs
            if stage == "nsa":
                src = [NS_Q + 64 * h for h in range(16)] + [NS_KS + 64 * g for g in range(4)] + \
                      [NS_KW + 64 * g for g in range(4)]
                dst = [(qT, h) for h in range(16)] + [(kT, g) for g in range(8)]
            else:
                src, dst = [], []
                for q, k, nq, nk, q0, k0 in ((QA, KA, 4, 4, 0, 0), (QD, KDL, 6, 6, 4, 4), (QC, KC, 6, 2, 10, 10)):
                    src += [q + 64 * h for h in range(nq)] + [k + 64 * h for h in range(nk)]
                    dst += [(qT, q0 + h) for h in range(nq)] + [(kT, k0 + h) for h in range(nk)]
            return [([(lambda t, c=c: proj[:, t, c:c + 64]) for c in src[2 * g:2 * g + 2]], 64,
                     [dst[2 * g][0][0:64, dst[2 * g][1]:dst[2 * g][1] + 2, :]]) for g in range(len(src) // 2)]

        def ft_bank(stage, g):
            return g % 4 if stage != "nsa" else 4 + g % 4 if g < 8 else 4 + g % 2

        def ft_before(stage, g):
            return max((q for q in range(g) if ft_bank(stage, q) == ft_bank(stage, g)), default=None)

        def ft_scale(stage, g):
            return 0.125 if stage == "nsa" and g < NS_H // 2 else 1.0

        def ncols(job, qt):
            return P if job["causal"] and qt == 0 else S

        def pt_blocks(job):
            return [(0, 0), (1, 0), (1, 1)] if job["causal"] else [(0, 0), (1, 0), (0, 1), (1, 1)]

        def p_of(par, qt, lo, hi):
            return prob[:, par * 512 + qt * 256 + lo:par * 512 + qt * 256 + hi]

        def pts_of(par, lo, hi):
            return prob[:, 1024 + par * 512 + lo:1024 + par * 512 + hi]

        def q_(i):
            return QT[:, i * 512:(i + 1) * 512]

        gla_q, gla_k, gla_b, gla_eb, gla_d, gla_ei, gla_ed, gla_qi = (q_(i) for i in range(8))
        gla_kd, gla_za, gla_ln, gla_la, gla_kdt = (KT[:, i * 512:(i + 1) * 512] for i in range(5))
        gla_aT = KT[:, 2560:2816]
        gla_qz, gla_am, gla_st, gla_sr = (work[:, i * 1024:(i + 1) * 1024] for i in range(4))

        ct_hi, ct_lo = (h[:, :, :].rearrange("p b (a s) -> p (b a) s", s=S) for h in (h_hi, h_lo))

        def chunks(ap):
            return ap.rearrange("p (a c i) -> p a c i", a=2, c=4)

        dup = work[:, 0:2048].rearrange("p (m t g e d) -> p m t g e d", m=2, t=2, g=4, e=2)
        m_k = work[:, 2048:2048 + 1280].rearrange("p (g s) -> p g s", g=5)
        m_v = work[:, 0:1280].rearrange("p (g s) -> p g s", g=5)
        hid = [QT[:, 0:128], QT[:, 128:256]]
        rope_p = KT[:, 2816:3072]
        gate_t = QT[0:48, 256:512]
        sc = work[:, 2048:3072]
        pc = work[:, 3072:4096]
        pct = work[:, 0:1024]
        kc_tok, kcT_ = KT[:, 2048:2112], KT[:, 2176:2304]
        rope_t = KT[:, 2304:2560]
        vcz = KT[:, 2560:2816].rearrange("p (g d) -> p g d", g=4)

        def rotate(eng, lnk, x1, x2, cos, sin, t1, t2):
            lnk(eng.tensor_tensor(t1, x1, sin, ALU.mult))
            lnk(eng.tensor_tensor(t2, x2, sin, ALU.mult))
            lnk(eng.tensor_tensor(x1, x1, cos, ALU.mult))
            lnk(eng.tensor_tensor(x2, x2, cos, ALU.mult))
            lnk(eng.tensor_tensor(x1, x1, t2, ALU.subtract))
            lnk(eng.tensor_tensor(x2, x2, t1, ALU.add))

        def rope_heads(eng, lnk, view, off, half, cos_t, sin_t, tmp):
            n = view.shape[1]
            x1 = view[:, :, off:off + half]
            x2 = view[:, :, off + half:off + 2 * half]
            cos = cos_t.unsqueeze(1).to_broadcast([P, n, half])
            sin = sin_t.unsqueeze(1).to_broadcast([P, n, half])
            t1 = tmp[:, 0:n * half].rearrange("p (h d) -> p h d", h=n)
            t2 = tmp[:, n * half:2 * n * half].rearrange("p (h d) -> p h d", h=n)
            rotate(eng, lnk, x1, x2, cos, sin, t1, t2)

        def head_rms(tile, n):
            _, heads_n, o, _ = SEC_KINDS[n]
            return tile[:, 0:56].rearrange("p (t h) -> p t h", t=NT)[:, :, o:o + heads_n]

        def sec_heads(eng, lnk, n, t, l, tmp):
            def head_view(c, m):
                return proj[:, t, c:c + m * 64].rearrange("p (h d) -> p h d", h=m)

            c, m, o, _ = SEC_KINDS[n]
            r = rstd[:, t * 28 + o:t * 28 + o + m].unsqueeze(2).to_broadcast([P, m, 64])
            lnk(eng.tensor_tensor(head_view(c, m), head_view(c, m), r, ALU.mult))
            for c1, m1, row in (((QA, 4, 0), (KA, 4, 3)), ((QD, 6, 1), (KDL, 6, 4)), ((QC, 6, 2), (KC, 2, 5)))[n]:
                g = head_gain[:, l, row, :].unsqueeze(1).to_broadcast([P, m1, 64])
                lnk(eng.tensor_tensor(head_view(c1, m1), head_view(c1, m1), g, ALU.mult))
            if n == 1:
                one = [const(k)[:, t * 8:(t + 1) * 8] for k in ("cos1", "sin1")]
                rope_heads(eng, lnk, head_view(QD, 12), 0, 8, one[0], one[1], tmp)
            if n == 2:
                v = proj[:, t, QC:QC + 512].rearrange("p (h r d) -> p h r d", h=8, r=2)
                cos, sin = (const(k)[:, t * 32:(t + 1) * 32].rearrange("p (r d) -> p r d", r=2).unsqueeze(1)
                            .to_broadcast([P, 8, 2, 16]) for k in ("cosax", "sinax"))
                t1 = tmp[:, 0:256].rearrange("p (h r d) -> p h r d", h=8, r=2)
                t2 = tmp[:, 256:512].rearrange("p (h r d) -> p h r d", h=8, r=2)
                rotate(eng, lnk, v[:, :, :, 0:16], v[:, :, :, 16:32], cos, sin, t1, t2)

        @block.sync
        def _(sp):
            def load(u, j):
                sp.dma_start(raw[:, j, :], stream[u]).then_inc(raw_in[j], 16)

            for t in range(NT):
                sp.dma_start(X[:, t, :], x[0, t * P:(t + 1) * P, :]).then_inc(x_in[t], 16)
            sp.dma_start(cst[:, :], consts).then_inc(cst_in, 16)
            sp.dma_start(gcol[:, :], gains).then_inc(gain_in, 16)
            for j in range(NRAW):
                load(j, j)
            for dst, src in ((pos_i[:, :], positions), (ccol[:, :, :, :], conv),
                             (a2[0:GLA_R, :], gla_a2[0]), (a2[GLA_R:GLA_R + 1, :], gla_ba),
                             (w2[:, 0, :], cmp_w2[0]), (w2[:, 1, :], cmp_w2[1]), (posr[:, :, :], pos_rows),
                             (gla_row[:, :], gla_gain[0].partition_broadcast(P)),
                             (head_gain[:, :, 0:3, :], q_gain2.rearrange("l r d -> (l r d)").partition_broadcast(P)
                              .rearrange("p (l r d) -> p l r d", l=2, r=3)),
                             (head_gain[:, :, 3:6, :], k_gain2.rearrange("l r d -> (l r d)").partition_broadcast(P)
                              .rearrange("p (l r d) -> p l r d", l=2, r=3))):
                sp.dma_start(dst, src).then_inc(par_in, 16)
            turns = N_UNITS // NRAW
            with sp.Fori(1, turns) as i:
                for j in range(NRAW):
                    sp.wait_ge(lo_done, i * NRAW + (j - NRAW + 1))
                    load(i * NRAW + j, j)
            for u in range(turns * NRAW, N_UNITS):
                sp.wait_ge(lo_done, u - NRAW + 1)
                load(u, u % NRAW)
            sp.wait_ge(x_upd, 4 * 11)
            sp.dma_start(out[0].rearrange("(t p) d -> p t d", p=P), X[:, :, :]).then_inc(stored, 16)
            sp.wait_ge(stored, 16)

        @block.tensor
        def _(pe):
            def norm(n):
                pe.wait_ge(xn0, n + 1)
                for t in range(NT):
                    for k in range(KD):
                        if t == 1 and k % 4 == 0:
                            pe.wait_ge(xn1, 2 * n + k // 4 + 1)
                        at = ((k % 2) * 2 + t) * P
                        ins = pe.transpose(bank[4 + k // 2][:, at:at + P], xn[:, t, k * P:(k + 1) * P], ident)
                        if t == 1 and k % 2:
                            ins.then_inc(xt_ps, 1)

            def token_major(u, name, width, out_bank, first_turn):
                pe.wait_ge(lo_done, u + 1)
                sl = u % 3
                for t in range(NT):
                    dst = out_bank[:, t * 256:t * 256 + width]
                    for k in range(KD):
                        if first_turn is not None and t == 0:
                            pe.wait_ge(xtl, 8 * first_turn + k + 1)
                        tok = slice(t * P, (t + 1) * P)
                        cols = slice(k * 256, k * 256 + width)
                        pe.matmul(dst, xt_hi[:, k, tok], w_hi[:, sl, cols], start=(k == 0), stop=False)
                        pe.matmul(dst, xt_hi[:, k, tok], w_lo[:, sl, cols], start=False, stop=False)
                        ins = pe.matmul(dst, xt_lo[:, k, tok], w_hi[:, sl, cols], start=False, stop=(k == KD - 1))
                ins.then_inc(unit_used, 1)

            def gates(u, dst):
                pe.wait_ge(lo_done, u + 1)
                sl = u % NSPLIT
                for k in range(KD):
                    cols = slice(k * 256, k * 256 + 48)
                    pe.matmul(dst, w_hi[:, sl, cols], xt_hi[:, k, :], start=(k == 0), stop=False)
                    pe.matmul(dst, w_hi[:, sl, cols], xt_lo[:, k, :], start=False, stop=False)
                    ins = pe.matmul(dst, w_lo[:, sl, cols], xt_hi[:, k, :], start=False, stop=(k == KD - 1))
                ins.then_inc(unit_used, 1)

            def project(stage, u0, blocks, turn, after=None):
                p0 = PROJ0[stage]
                for c, width in enumerate(blocks):
                    if c >= 4:
                        pe.wait_ge(pj_evac, p0 + c - 3)
                    if stage == "nsa" and c == G_BLOCK:
                        gates(u0 + c, bank[c % 4][0:48, 0:S])
                        continue
                    if stage == "nsa" and c == G_BLOCK + 4:
                        pe.wait_ge(c_gate, 1)
                    token_major(u0 + c, stage, width, bank[c % 4], turn if c == 0 else None)
                    if after:
                        after(c)

            def mix_out(m):
                u0 = U[f"mix{m}"]
                turn = TURN[f"m{m}"]
                for c in range(OUT_UNITS):
                    u = u0 + c
                    pe.wait_ge(lo_done, u + 1)
                    sl = u % 3
                    last = c == OUT_UNITS - 1
                    order = [(j, t, half) for t in range(NT) for half in range(2) for j in range(2)] if last else \
                            [(j, t, half) for j in range(2) for t in range(NT) for half in range(2)]
                    for j, t, half in order:
                        k = 2 * c + j
                        if t == 0 and half == 0:
                            pe.wait_ge(xtl, 8 * turn + k + 1)
                        tok = slice(t * P, (t + 1) * P)
                        cols = slice(j * D + half * 512, j * D + half * 512 + 512)
                        for lhs, w in ((xt_hi, w_hi), (xt_hi, w_lo), (xt_lo, w_hi)):
                            ins = pe.matmul(bank[2 * t + half][:, :], lhs[:, k, tok], w[:, sl, cols],
                                            start=(k == 0 and lhs is xt_hi and w is w_hi),
                                            stop=(k == KD - 1 and lhs is xt_lo))
                        if last and j == 1 and (t, half) in ((0, 1), (1, 0)):
                            ins.then_inc(x_part, 1)
                    ins.then_inc(unit_used, 1)

            def ffn_gu(f, kind, s, i):
                u = ffn_unit(f, kind, s)
                sl = u % NSPLIT
                pe.wait_ge(lo_done, on(u + 1, 6, i))
                dst = bank[2 * (s % 2) + (0 if kind == "g" else 1)]
                turn = TURN[f"n{FFN_NORM[f]}"]
                for j in range(2):
                    for k in range(KD):
                        if s == 0 and kind == "g" and j == 0:
                            pe.wait_ge(xtl, 8 * turn + k + 1)
                        cols = slice(k * 256 + j * P, k * 256 + (j + 1) * P)
                        o = dst[:, j * S:(j + 1) * S]
                        pe.matmul(o, w_hi[:, sl, cols], xt_hi[:, k, :], start=(k == 0), stop=False)
                        pe.matmul(o, w_hi[:, sl, cols], xt_lo[:, k, :], start=False, stop=False)
                        ins = pe.matmul(o, w_lo[:, sl, cols], xt_hi[:, k, :], start=False, stop=(k == KD - 1))
                ins.then_inc(unit_used, 1)

            def ffn_down(f, s, i):
                u = ffn_unit(f, "d", s)
                sl = u % NSPLIT
                pe.wait_ge(lo_done, on(u + 1, 6, i))
                pe.wait_ge(hl_done, on(f * STEPS + s + 1, 2, i))
                last = s == STEPS - 1
                order = [(j, t, half) for t in range(NT) for half in range(2) for j in range(2)] if last else \
                        [(j, t, half) for j in range(2) for t in range(NT) for half in range(2)]
                for j, t, half in order:
                    tok = slice(j * S + t * P, j * S + (t + 1) * P)
                    cols = slice(j * D + half * 512, j * D + half * 512 + 512)
                    for lhs, w in ((h_hi, w_hi), (h_hi, w_lo), (h_lo, w_hi)):
                        ins = pe.matmul(bank[4 + 2 * t + half][:, :], lhs[:, s % 2, tok], w[:, sl, cols],
                                        start=(s == 0 and j == 0 and lhs is h_hi and w is w_hi),
                                        stop=(last and j == 1 and lhs is h_lo))
                    if last and j == 1 and (t, half) in ((0, 1), (1, 0)):
                        ins.then_inc(x_part, 1)
                ins.then_inc(unit_used, 1)

            def triple(f, s, i):
                if s >= 2:
                    pe.wait_ge(mul_done, on(f * STEPS + s - 1, 2, i))
                ffn_gu(f, "g", s, i)
                ffn_gu(f, "u", s, i)
                if s:
                    ffn_down(f, s - 1, i)

            def ffn(f):
                ffn_steps(pe, f, triple)
                ffn_down(f, STEPS - 1, None)

            def feature_major(stage, lo=0, hi=None):
                a0, d0 = FT_A0[stage], FT_D0[stage]
                for g, (srcs, rows, _) in list(enumerate(ft_groups(stage)))[lo:hi]:
                    for n, (_, _, o, _) in enumerate(SEC_KINDS):
                        if stage[:3] == "sec" and g == o // 2:
                            pe.wait_ge(ft_ready_p, 4 + 3 * int(stage[3]) + n)
                            if n == 2:
                                pe.wait_ge(ft_ready_d, 4 + int(stage[3]))
                    before = ft_before(stage, g)
                    if before is not None:
                        if before % 2 == 0:
                            pe.wait_ge(ft_a, a0 + before // 2 + 1)
                        else:
                            pe.wait_ge(ft_d, d0 + before // 2 + 1)
                    for n, src in enumerate(srcs):
                        for t in range(NT):
                            ins = pe.transpose(bank[ft_bank(stage, g)][0:rows, (2 * n + t) * P:(2 * n + t + 1) * P], src(t), ident)
                    ins.then_inc(ft_ps, 1)

            def attention(stage):
                jobs, j0 = heads[stage], JOB0[stage]

                def scores(i):
                    if i >= len(jobs):
                        return
                    if i >= 3:
                        pe.wait_ge(exp_done, 2 * (j0 + i - 2))
                    if stage == "nsa" and i == 2:
                        pe.wait_ge(c_pe, 1)
                    job, dst = jobs[i], bank[S_BANKS[i % 3]]
                    if stage[:3] == "sec" and i == 12:
                        pe.wait_ge(na_ready, int(stage[3]) + 1)
                    for qt in range(NT):
                        n = ncols(job, qt)
                        plain = not job["causal"] and job["bias"] is None
                        ins = pe.matmul(dst[:, qt * S:qt * S + n], qT[0:job["d"], job["q"], qt * P:(qt + 1) * P],
                                        kT[0:job["d"], job["k"], 0:n], start=True, stop=plain)
                        if job["causal"]:
                            ins = pe.matmul(dst[:, qt * S + qt * P:qt * S + (qt + 1) * P], ident_b[:, :],
                                            causal_b[:, :], start=False, stop=True)
                        elif not plain:
                            ins = pe.matmul(dst[:, qt * S:qt * S + n], const("flip"), job["bias"](qt), start=False,
                                            stop=True)
                    ins.then_inc(s_done, 1)

                def turn_p(i):
                    pe.wait_ge(p_scaled, j0 + i + 1)
                    if i >= 2:
                        pe.wait_ge(pt_evac, j0 + i - 1)
                    for n, (qt, kt) in enumerate(pt_blocks(jobs[i])):
                        ins = pe.transpose(bank[2 + i % 2][:, n * P:(n + 1) * P], p_of(i % 2, qt, kt * P, (kt + 1) * P),
                                           ident)
                    ins.then_inc(t_done, 1)

                def values(i):
                    if i < 0:
                        return
                    pe.wait_ge(pt_evac, j0 + i + 1)
                    per = JOBS_PER_PAIR[stage]
                    pair, at = i // per, i % per
                    if at == 0 and pair >= 2:
                        if stage[:3] == "sec":
                            pe.wait_ge(o_copied, 8 * int(stage[3]) + pair - 1)
                        else:
                            pe.wait_ge(xtl, 8 * TURN["m0" if stage == "mla" else "m1"] + (4 if stage == "mla" else 0)
                                       + pair - 1)
                    job, half = jobs[i], at * 2 // per
                    dst = bank[4 + pair % 2][64 * half:64 * half + 64, 0:S]
                    first = True
                    if stage == "nsa":
                        first = False
                        if at % 2 == 0:
                            g, j = job["q"] // 4, job["q"] % 4
                            pe.matmul(dst, vcz[:, g, :], pct[:, j * S:(j + 1) * S], start=True, stop=False)
                    last = stage != "nsa" or at % 2 == 1
                    pe.matmul(dst, job["v"](0), pts_of(i % 2, 0, S), start=first, stop=False)
                    if job["causal"]:
                        ins = pe.matmul(dst[:, P:S], job["v"](1), pts_of(i % 2, S, S + P), start=False, stop=last)
                    else:
                        ins = pe.matmul(dst, job["v"](1), pts_of(i % 2, S, 2 * S), start=False, stop=last)
                    ins.then_inc(pv_done, 1)

                def square_sums(place):
                    l = int(stage[3])
                    pe.wait_ge(o_copied, 8 * l + place + 1)
                    kind = kind_of(place)
                    if place == 3:
                        pe.wait_ge(e_m, 3 * l + 1)
                    dst = bank[7 if kind < 2 else 6][:, 0:S]
                    pe.matmul(dst, const("ones"), o_sq[:, place % 2, :], start=place in (0, 3, 6),
                              stop=place in (2, 5, 7)).then_inc(o_sum, 1)

                scores(0)
                scores(1)
                for i in range(len(jobs)):
                    scores(i + 2)
                    turn_p(i)
                    values(i - 1)
                    if stage[:3] == "sec" and pair_after(stage, i, 4) is not None:
                        square_sums(pair_after(stage, i, 4))
                values(len(jobs) - 1)
                if stage[:3] == "sec":
                    for place in late_pairs(stage, 4):
                        if place == 6:
                            pe.wait_ge(exp_done, 2 * (j0 + len(jobs)))
                        square_sums(place)

            def wait_ft(stage):
                pe.wait_ge(ft_a, FT_A0[stage] + (FT_GROUPS[stage] + 1) // 2)
                pe.wait_ge(ft_d, FT_D0[stage] + FT_GROUPS[stage] // 2)

            def hybrid_step(c):
                if c == 3:
                    pe.wait_ge(pj_evac, 3)
                    for col, b in ((HY_GQ, 4), (HY_GK, 5)):
                        for a in range(2):
                            for t in range(NT):
                                ins = pe.transpose(bank[b][:, (a * 2 + t) * P:(a * 2 + t + 1) * P],
                                                   proj[:, t, col + a * P:col + (a + 1) * P], ident)
                        ins.then_inc(g_tp, 1)
                    for t in range(NT):
                        ins = pe.transpose(bank[6][0:GLA_R, t * P:(t + 1) * P], proj[:, t, HY_GA:HY_GA + GLA_R], ident)
                    ins.then_inc(g_tp, 1)
                if c == 4:
                    pe.wait_ge(g_ev, 2)
                    for t in range(NT):
                        ins = pe.matmul(bank[7][:, t * 256:(t + 1) * 256], gla_aT[0:GLA_R + 1, t * P:(t + 1) * P],
                                        a2[:, :], start=True, stop=True)
                    ins.then_inc(g_z, 1)
                if c == 5:
                    pe.wait_ge(g_la, 1)
                    for a in range(2):
                        for t in range(NT):
                            ins = pe.matmul(bank[6][:, (a * 2 + t) * P:(a * 2 + t + 1) * P],
                                            gla_la[:, t * 256 + a * P:t * 256 + (a + 1) * P], const("block_tri"),
                                            start=True, stop=True)
                    ins.then_inc(g_b, 1)
                    pe.wait_ge(mla_cn, 4)
                    pe.wait_ge(g_evd, 3)
                    for a in range(2):
                        for t in range(NT):
                            ins = pe.transpose(bank[4][:, (a * 2 + t) * P:(a * 2 + t + 1) * P],
                                               proj[:, t, HY_CQ + a * P:HY_CQ + (a + 1) * P], ident)
                    ins.then_inc(mla_tp, 1)
                    for t in range(NT):
                        ins = pe.transpose(bank[5][:, t * P:(t + 1) * P], proj[:, t, HY_CKV:HY_CKV + P], ident)
                    ins.then_inc(mla_tp, 1)
                if c == 6:
                    pe.wait_ge(g_qk, 2)
                    pe.wait_ge(mla_cl, 3)
                    for t in range(NT):
                        for h in range(GLA_H):
                            r = slice(64 * (h % 2), 64 * (h % 2) + 64)
                            col = (h // 2) * S + t * P
                            at = (2 * t + h // 2) * P
                            ins = pe.matmul(bank[4 + h % 2][:, at:at + P], gla_kd[r, col:col + P], gla_qi[r, col:col + P],
                                            start=True, stop=True)
                    ins.then_inc(g_a, 1)
                    for t in range(NT):
                        for a in range(2):
                            ins = pe.transpose(bank[6][:, (t * 2 + a) * P:(t * 2 + a + 1) * P],
                                               gla_kd[:, a * S + t * P:a * S + (t + 1) * P], ident)
                    ins.then_inc(g_kt, 1)

            def queries_up():
                u = U["uq"]
                pe.wait_ge(lo_done, u + 1)
                sl = u % 3
                for t in range(NT):
                    tok = slice(t * P, (t + 1) * P)
                    for c0, n in ((0, 512), (512, 256)):
                        for k in range(2):
                            cols = slice(k * 768 + c0, k * 768 + c0 + n)
                            o = bank[UQ_BANKS[t][c0 // 512]][:, 0:n]
                            pe.matmul(o, ct_hi[:, k, tok], w_hi[:, sl, cols], start=(k == 0), stop=False)
                            pe.matmul(o, ct_hi[:, k, tok], w_lo[:, sl, cols], start=False, stop=False)
                            ins = pe.matmul(o, ct_lo[:, k, tok], w_hi[:, sl, cols], start=False, stop=(k == 1))
                ins.then_inc(unit_used, 1)

            def gla():
                pe.wait_ge(g_kd, 1)
                pe.wait_ge(g_am, 1)
                pe.wait_ge(pj_evac, 7)
                for c in range(3):
                    r = slice(64 * (c % 2), 64 * (c % 2) + 64)
                    t = c // 2
                    for a in range(2):
                        ins = pe.matmul(bank[GLA_KV_BANKS[c]][:, a * 256:(a + 1) * 256],
                                        gla_kdt[r, (t * 2 + a) * P:(t * 2 + a + 1) * P],
                                        proj[r, t, HY_GV + a * 256:HY_GV + (a + 1) * 256], start=True, stop=True)
                    ins.then_inc(g_kv, 1)
                pe.wait_ge(pj_evac, 8)
                queries_up()
                pe.wait_ge(g_qk, 3)
                pe.wait_ge(g_st, 3)
                qz = gla_qz.rearrange("p (a c i) -> p a c i", a=2, c=4)
                st = gla_st.rearrange("p (a c v) -> p a c v", a=2, c=4)
                for t in range(NT):
                    for h in range(GLA_H):
                        r = slice(64 * (h % 2), 64 * (h % 2) + 64)
                        a = h // 2
                        dst = bank[(7, 4)[h % 2]][:, (2 * t + a) * P:(2 * t + a + 1) * P]
                        n = 4 * (h % 2) + 2 * t + a
                        pe.matmul(dst, gla_am[:, n * P:(n + 1) * P],
                                  proj[:, t, HY_GV + h * P:HY_GV + (h + 1) * P], start=True, stop=False)
                        cs = [c for c in (2 * t, 2 * t + 1) if c > 0]
                        for c in cs:
                            ins = pe.matmul(dst, qz[r, a, c, :], st[r, a, c, :], start=False, stop=(c == cs[-1]))
                ins.then_inc(g_o, 1)

            def mla():
                pe.wait_ge(mla_q, 4)
                u = U["ukv"]
                pe.wait_ge(lo_done, u + 1)
                sl = u % 3
                for t in range(NT):
                    tok = slice(t * P, (t + 1) * P)
                    for half in range(2):
                        cols = slice(half * 512, half * 512 + 512)
                        o = bank[2 * t + half][:, :]
                        pe.matmul(o, ct_hi[:, 2, tok], w_hi[:, sl, cols], start=True, stop=False)
                        pe.matmul(o, ct_hi[:, 2, tok], w_lo[:, sl, cols], start=False, stop=False)
                        ins = pe.matmul(o, ct_lo[:, 2, tok], w_hi[:, sl, cols], start=False, stop=True)
                ins.then_inc(unit_used, 1)
                pe.wait_ge(mla_q, 4)
                pe.wait_ge(mla_up, 1)
                for b in range(2):
                    for kk in range(2):
                        for t in range(NT):
                            c = 512 + (2 * b + kk) * P
                            ins = pe.transpose(bank[4 + b][:, (kk * 2 + t) * P:(kk * 2 + t + 1) * P],
                                               O[:, t, c:c + P], ident)
                    ins.then_inc(g_ot, 1)
                pe.wait_ge(mla_kv, 4)
                pe.wait_ge(ft_ready_d, 1)
                pe.wait_ge(ft_ready_p, 1)
                feature_major("mla")
                wait_ft("mla")
                pe.wait_ge(xtl, 8 * TURN["m0"] + 4)
                attention("mla")

            def nsa_step(c):
                if c == 3:
                    pe.wait_ge(c_dup, 2)
                    for m in range(2):
                        for gp in range(2):
                            for g in (2 * gp, 2 * gp + 1):
                                for t in range(NT):
                                    at = ((m * 2 + t) * 4 + g) * P
                                    ins = pe.transpose(bank[4 + 2 * m + gp][:, ((g % 2) * 2 + t) * P:((g % 2) * 2 + t + 1) * P],
                                                       work[:, at:at + P], ident)
                            ins.then_inc(c_tp, 1)
                if c == 4:
                    pe.wait_ge(c_w, 32)
                    pe.wait_ge(c_m, 8)
                    for m, (mt, w1) in enumerate(((m_k, prob[:, :]), (m_v, O[:, :, :].rearrange("p t d -> p (t d)")))):
                        for l in range(16):
                            ins = pe.matmul(bank[4 + m][:, 0:75], w1[:, l * P:(l + 1) * P],
                                            mt[:, :, 2 * l:2 * l + 225:16], start=(l == 0), stop=(l == 15))
                        ins.then_inc(c_h, 1)
                if c == 7:
                    pe.wait_ge(pj_evac, PROJ0["nsa"] + G_BLOCK + 1)
                    for t in range(NT):
                        ins = pe.transpose(bank[G_BLOCK % 4][:, S + t * 48:S + (t + 1) * 48], gate_t[:, t * P:(t + 1) * P],
                                           ident[0:48, 0:48])
                    ins.then_inc(c_gt, 1)
                if c == 5:
                    for m in range(2):
                        pe.wait_ge(c_hid, m + 1)
                        ins = pe.matmul(bank[6][:, m * 64:(m + 1) * 64], hid[m], w2[:, m, :], start=True, stop=True)
                    ins.then_inc(c_kc, 1)
                if c == 7:
                    pe.wait_ge(c_kr, 1)
                    pe.transpose(bank[6][0:64, 0:P], kc_tok, ident).then_inc(c_kt, 1)
                    pe.wait_ge(c_kcT, 1)
                    pe.wait_ge(ft_ready_d, 2)
                    pe.wait_ge(ft_ready_p, 2)
                    feature_major("nsa", 0, 8)
                if c == 8:
                    pe.wait_ge(ft_a, FT_A0["nsa"] + 4)
                    pe.wait_ge(ft_d, FT_D0["nsa"] + 4)
                    for t in range(NT):
                        for h in range(NS_H):
                            g, j = h // 4, h % 4
                            ins = pe.matmul(bank[6 + t][:, (j * 4 + g) * 32:(j * 4 + g + 1) * 32],
                                            qT[0:64, h, t * P:(t + 1) * P], kcT_[0:64, g * 32:(g + 1) * 32],
                                            start=True, stop=True)
                    ins.then_inc(c_s, 1)
                if c == 9:
                    pe.wait_ge(ft_ready_d, 3)
                    pe.wait_ge(ft_ready_p, 3)
                    feature_major("nsa", 8)
                if c == 10:
                    pe.wait_ge(c_p, 2)
                    for j in range(4):
                        for t in range(NT):
                            ins = pe.transpose(bank[6 + j // 2][:, ((j % 2) * 2 + t) * P:((j % 2) * 2 + t + 1) * P],
                                               pc[:, (t * 4 + j) * P:(t * 4 + j + 1) * P], ident)
                    ins.then_inc(c_pt, 1)

            pe.wait_ge(const_ready, 1)
            norm(0)
            ffn(0)
            norm(1)
            project("hy", U["hy_in"], HY_BLOCKS, TURN["n1"], hybrid_step)
            gla()
            mla()
            mix_out(0)
            norm(2)
            ffn(1)
            norm(3)
            ffn(2)
            norm(4)
            project("nsa", U["nsa_in"], NSA_BLOCKS, TURN["n4"], nsa_step)
            pe.wait_ge(pj_evac, PROJ0["nsa"] + len(NSA_BLOCKS))
            wait_ft("nsa")
            attention("nsa")
            mix_out(1)
            norm(5)
            ffn(3)
            for l in range(2):
                norm(6 + 2 * l)
                project(f"sec{l}", U[f"sec_in{l}"], SEC_BLOCKS, TURN[f"n{6 + 2 * l}"])
                pe.wait_ge(pj_evac, PROJ0[f"sec{l}"] + len(SEC_BLOCKS))
                feature_major(f"sec{l}")
                wait_ft(f"sec{l}")
                attention(f"sec{l}")
                mix_out(2 + l)
                norm(7 + 2 * l)
                ffn(4 + l)

        @block.scalar
        def _(act):
            own = [0]

            def link(ins):
                own[0] += 1
                ins.then_inc(act_own, 1)
                act.wait_ge(act_own, own[0])

            def split(u, i=None):
                if u >= N_UNITS:
                    return
                sl = u % NSPLIT
                act.wait_ge(raw_in[sl], on(16 * (u // NRAW + 1), 32, i))
                if u >= NSPLIT:
                    act.wait_ge(unit_used, on(u - NSPLIT + 1, 6, i))
                act.activation(w_hi[:, sl, :], raw[:, sl, :], ACT.Copy).then_inc(hi_done, 1)

            def squares(r):
                for q in range(4):
                    t, half = q // 2, slice(q % 2 * 512, q % 2 * 512 + 512)
                    if r:
                        act.wait_ge(x_upd, 4 * r - 3 + q)
                    else:
                        act.wait_ge(x_in[t], 16)
                    act.activation(xn[:, t, half], X[:, t, half], ACT.Square, accum_out=ss[:, q:q + 1]).then_inc(sq_done, 1)

            def norm(n, between=None):
                r = rms_turn(n)
                squares(r)
                if between:
                    between()
                for k in range(KD):
                    act.wait_ge(xt_ps, 4 * n + k // 2 + 1)
                    g = G_NORM + 8 * n + k
                    act.activation(xt_hi[:, k, :], bank[4 + k // 2][:, (k % 2) * S:(k % 2 + 1) * S], ACT.Copy,
                                   scale=gcol[:, g:g + 1]).then_inc(xth, 1)
                if n:
                    for ahead in (2, 1):
                        split(U[NORM_STAGE[n]] + NSPLIT - ahead)

            def project(stage, u0, blocks, after=None, before=None):
                for c, width in enumerate(blocks):
                    if before:
                        before(c)
                    split(u0 + c + NSPLIT)
                    act.wait_ge(unit_used, u0 + c + 1)
                    if stage == "nsa" and c == G_BLOCK:
                        act.activation(gate_t, bank[c % 4][0:48, 0:S], ACT.Copy).then_inc(pj_evac, 1)
                        continue
                    src = bank[c % 4][:, :].rearrange("p (t n) -> p t n", t=2)
                    at = sum(blocks[:c])
                    act.activation(proj[:, :, at:at + width], src[:, :, 0:width], ACT.Copy).then_inc(pj_evac, 1)
                    if after:
                        after(c)

            def sec_rms(l, c):
                for n, (col, m, _, last) in enumerate(SEC_KINDS):
                    if c == last:
                        act.wait_ge(pj_evac, PROJ0[f"sec{l}"] + c + 1)
                        if n:
                            act.wait_ge(e_ms, 3 * l + n)
                        for t in range(NT):
                            act.activation(work[:, t * m * 64:(t + 1) * m * 64], proj[:, t, col:col + m * 64],
                                           ACT.Square).then_inc(e_sq, 1)
                    if c == last + (1 if n < 2 else 0):
                        act.wait_ge(e_ms, 3 * l + n + 1)
                        act.activation(head_rms(rstd, n), head_rms(ms, n), ACT.Sqrt).then_inc(e_rt, 1)

            def mix_out(m):
                for c in range(OUT_UNITS - 2):
                    split(U[f"mix{m}"] + c + NSPLIT)

            def triple(f, s, i):
                par = s % 2
                split(ffn_unit(f, "g", s) + NSPLIT, i)
                last = s == STEPS - 1
                if not last:
                    split(ffn_unit(f, "u", s) + NSPLIT, i)
                act.wait_ge(unit_used, on(ffn_unit(f, "u", s) + 1, 6, i))
                if s >= 2:
                    act.wait_ge(mul_done, on(f * STEPS + s - 1, 2, i))
                if f < 4:
                    act.activation(act_g[:, par, :], bank[2 * par][:, :], ACT.Silu).then_inc(actg_done, 1)
                else:
                    l = f - 4
                    for j in range(2):
                        act.activation(conv_y[:, par, j * S:(j + 1) * S], bank[2 * par][:, j * S:(j + 1) * S],
                                       ACT.Identity, scale=tap(l, 1, s, j, i), bias=tap(l, 3, s, j, i)).then_inc(cv_mid, 1)
                    act.wait_ge(cv_done, on(l * STEPS + s + 1, 2, i))
                    act.activation(act_g[:, par, :], conv_y[:, par, :], ACT.Gelu).then_inc(actg_done, 1)
                act.wait_ge(mul_done, on(f * STEPS + s + 1, 2, i))
                act.activation(h_hi[:, par, :], h_f, ACT.Copy).then_inc(hh_done, 1)
                if last:
                    split(ffn_unit(f, "u", s) + NSPLIT)
                if s and not last:
                    split(ffn_unit(f, "d", s - 1) + NSPLIT, i)

            def ffn(f):
                ffn_steps(act, f, triple)

            def feature_major(stage, lo=0, hi=None):
                g0 = FT_A0[stage] + FT_D0[stage]
                for g, (srcs, rows, dst) in list(enumerate(ft_groups(stage)))[lo:hi]:
                    if g % 2:
                        continue
                    act.wait_ge(ft_ps, g0 + g + 1)
                    if dst is None:
                        src = bank[ft_bank(stage, g)][64:96, 0:S]
                        for h in range(MLA_H):
                            ins = act.activation(kT[64:96, h, :], src, ACT.Copy)
                        ins.then_inc(ft_a, 1)
                    else:
                        src = bank[ft_bank(stage, g)][0:rows, :].rearrange("p (h s) -> p h s", h=2)
                        act.activation(dst[0], src, ACT.Copy, scale=ft_scale(stage, g)).then_inc(ft_a, 1)

            def attention(stage):
                jobs, j0 = heads[stage], JOB0[stage]
                def evac(i):
                    act.wait_ge(t_done, j0 + i + 1)
                    if i >= 2:
                        act.wait_ge(pv_done, j0 + i - 1)
                    n = P * len(pt_blocks(jobs[i]))
                    act.activation(pts_of(i % 2, 0, n), bank[2 + i % 2][:, 0:n], ACT.Copy).then_inc(pt_evac, 1)

                for i, job in enumerate(jobs):
                    if i >= 2:
                        evac(i - 2)
                    act.wait_ge(nm_done, j0 + i + 1)
                    if i >= 2:
                        act.wait_ge(t_done, j0 + i - 1)
                    for qt in range(NT):
                        n = ncols(job, qt)
                        act.activation(p_of(i % 2, qt, 0, n), bank[S_BANKS[i % 3]][:, qt * S:qt * S + n], ACT.Exp,
                                       bias=negmax[:, i % 4, qt:qt + 1],
                                       accum_out=sums[:, i % 4, qt:qt + 1]).then_inc(exp_done, 1)
                    pair_out(stage, pair_after(stage, i, 3))
                evac(len(jobs) - 2)
                evac(len(jobs) - 1)
                for pair in late_pairs(stage, 3):
                    pair_out(stage, pair)

            def hybrid_step(c):
                if c == 3:
                    act.wait_ge(g_tp, 1)
                    act.activation(gla_q, bank[4][:, :], ACT.Copy, scale=0.125).then_inc(g_ev, 1)
                    act.wait_ge(g_tp, 3)
                    act.wait_ge(g_evd, 1)
                    act.activation(gla_aT[0:GLA_R, :], bank[6][0:GLA_R, 0:S], ACT.Copy).then_inc(g_ev, 1)
                    act.wait_ge(pj_evac, 4)
                    for n, (col, w) in enumerate(((HY_CQ, 256), (HY_CKV, 128))):
                        for t in range(NT):
                            act.activation(prob[:, 0:w], proj[:, t, col:col + w], ACT.Square,
                                           accum_out=ss[:, 8 + 2 * n + t:9 + 2 * n + t]).then_inc(mla_sq, 1)
                            act.wait_ge(mla_sq, 2 * n + t + 1)
                if c == 4:
                    act.wait_ge(g_z, 1)
                    link(act.activation(gla_za, bank[7][:, :], ACT.Abs))
                    link(act.activation(gla_za, gla_za, ACT.Exp, scale=-1.0))
                    act.activation(gla_ln, gla_za, ACT.Ln, bias=1.0).then_inc(g_ln, 1)
                if c == 5:
                    act.wait_ge(g_b, 1)
                    act.activation(gla_b, bank[6][:, :], ACT.Copy, scale=1.0 / 16.0).then_inc(g_bt, 1)
                    for k in range(3):
                        act.wait_ge(mla_tp, 1 if k < 2 else 2)
                        src = bank[4][:, k * S:(k + 1) * S] if k < 2 else bank[5][:, 0:S]
                        act.activation(ct_hi[:, k, :], src, ACT.Copy, scale=gcol[:, G_Q + k:G_Q + k + 1]).then_inc(mla_ch, 1)
                    act.wait_ge(g_bt, 1)
                    act.activation(gla_eb, gla_b, ACT.Exp).then_inc(g_e, 1)
                    act.wait_ge(g_d, 1)
                    act.activation(gla_ei, gla_d, ACT.Exp).then_inc(g_e, 1)
                    act.activation(gla_ed, gla_d, ACT.Exp, scale=-1.0).then_inc(g_e, 1)
                if c == 6:
                    act.wait_ge(g_kt, 1)
                    act.activation(gla_kdt, bank[6][:, :], ACT.Copy).then_inc(g_kd, 1)

            def nsa_step(c):
                if c == 5:
                    for m, b in enumerate((4, 5)):
                        act.wait_ge(c_b, m + 1)
                        dst = hid[m].rearrange("p (g n) -> p g n", g=4)[:, :, 0:NCMP]
                        src = bank[b][:, 0:60].rearrange("p (g n) -> p g n", g=4)
                        act.activation(dst, src, ACT.Silu, bias=small[:, 0, m:m + 1]).then_inc(c_hid, 1)
                if c == 7:
                    act.wait_ge(c_gt, 1)
                    act.activation(gate[:, :, :], bank[G_BLOCK % 4][:, S:S + 96].rearrange("p (t n) -> p t n", t=NT),
                                   ACT.Sigmoid).then_inc(c_gate, 1)
                    feature_major("nsa", 0, 8)
                if c == 9:
                    feature_major("nsa", 8)

            def nsa_exp(c):
                if c == 9:
                    act.wait_ge(c_sc, 1)
                    act.activation(pc, sc, ACT.Exp).then_inc(c_e, 1)

            def pair_out(stage, pair):
                if pair is None:
                    return
                act.wait_ge(pv_done, JOB0[stage] + (pair + 1) * JOBS_PER_PAIR[stage])
                src = bank[4 + pair % 2][:, 0:S]
                if stage[:3] != "sec":
                    act.activation(xt_hi[:, pair + (4 if stage == "mla" else 0), :], src, ACT.Copy).then_inc(xth, 1)
                    return
                l = int(stage[3])
                act.activation(o_t[:, pair, :], src, ACT.Copy)
                if pair >= 2:
                    act.wait_ge(o_sum, 8 * l + pair - 1)
                act.activation(o_sq[:, pair % 2, :], src, ACT.Square).then_inc(o_copied, 1)

            norm(0, lambda: (split(0), act.wait_ge(gain_in, 16)))
            for u in range(1, NSPLIT):
                split(u)
            ffn(0)
            act.wait_ge(par_in, 16 * N_PAR)
            act.wait_ge(rope_arg, 1)
            act.activation(rsin[:, :, :], red[:, :, :], ACT.Sin).then_inc(rope_tab, 1)
            act.activation(rcos[:, :, :], tmp48[:, :, :], ACT.Sin).then_inc(rope_tab, 1)
            norm(1)
            project("hy", U["hy_in"], HY_BLOCKS, hybrid_step)
            act.wait_ge(pj_evac, 8)
            act.wait_ge(g_kd, 1)
            act.activation(gla_sr.rearrange("p (t n) -> p t n", t=2), proj[:, :, HY_GR:HY_GR + 512],
                           ACT.Silu).then_inc(g_sr, 1)
            act.wait_ge(unit_used, U["uq"] + 1)
            for t in range(NT):
                for c0, n in ((0, 512), (512, 256)):
                    act.activation(prob[:, t * 768 + c0:t * 768 + c0 + n], bank[UQ_BANKS[t][c0 // 512]][:, 0:n], ACT.Copy,
                                   scale=float(MLA_QK) ** -0.5).then_inc(mla_q, 1)
            act.wait_ge(g_o, 1)
            for t in range(NT):
                for h in range(GLA_H):
                    src = bank[(7, 4)[h % 2]][:, (2 * t + h // 2) * P:(2 * t + h // 2 + 1) * P]
                    act.activation(QT[:, 0:P], src, ACT.Square, accum_out=ss[:, 16 + t * 4 + h:17 + t * 4 + h]).then_inc(g_sq, 1)
                    act.wait_ge(g_sq, 4 * t + h + 1)
            split(U["uq"] + NSPLIT)
            split(U["ukv"] + NSPLIT)
            act.wait_ge(unit_used, U["ukv"] + 1)
            act.wait_ge(mla_up, 1)
            for t in range(NT):
                for half in range(2):
                    act.activation(work[:, 2048 + t * 1024 + half * 512:2048 + t * 1024 + half * 512 + 512],
                                   bank[2 * t + half][:, :], ACT.Copy).then_inc(mla_kv, 1)
            for k in range(4):
                act.wait_ge(g_ot, k // 2 + 1)
                act.activation(xt_hi[:, k, :], bank[4 + k // 2][:, (k % 2) * S:(k % 2 + 1) * S],
                               ACT.Copy).then_inc(xth, 1)
            feature_major("mla")
            attention("mla")
            mix_out(0)
            norm(2)
            ffn(1)
            norm(3)
            ffn(2)
            norm(4)
            project("nsa", U["nsa_in"], NSA_BLOCKS, nsa_step, nsa_exp)
            attention("nsa")
            mix_out(1)
            norm(5)
            ffn(3)
            squares(6)
            for l in range(2):
                norm(6 + 2 * l)
                project(f"sec{l}", U[f"sec_in{l}"], SEC_BLOCKS, lambda c: sec_rms(l, c))
                feature_major(f"sec{l}")
                attention(f"sec{l}")
                for place in range(KD):
                    if place in (0, 4):
                        cols = slice(0, 2 * S) if place == 0 else slice(2 * S, 3 * S)
                        act.wait_ge(e_m, 3 * l + (2 if place == 0 else 3))
                        act.activation(o_rs[:, cols], o_rs[:, cols], ACT.Sqrt).then_inc(e_mr, 1)
                    act.wait_ge(o_scaled, 8 * l + place + 1)
                    act.activation(xt_hi[:, place, :], o_t[:, place, :], ACT.Copy).then_inc(xth, 1)
                mix_out(2 + l)
                norm(7 + 2 * l)
                ffn(4 + l)

        @block.vector
        def _(dve):
            own = [0]

            def link(ins):
                own[0] += 1
                ins.then_inc(dve_own, 1)
                dve.wait_ge(dve_own, own[0])

            def split(u, i=None):
                if u >= N_UNITS:
                    return
                sl = u % NSPLIT
                dve.wait_ge(hi_done, on(u + 1, 6, i))
                dve.tensor_tensor(w_lo[:, sl, :], raw[:, sl, :], w_hi[:, sl, :].bitcast(F32),
                                  ALU.subtract).then_inc(lo_done, 1)

            def mean_squares(lo, n, scale):
                return dve.tensor_scalar(ms[:, lo:lo + n], ss[:, lo:lo + n], scale, EPS, ALU.mult, ALU.add)

            def mean(r, t):
                dve.wait_ge(sq_done, 4 * r + 2 * t + 1)
                link(dve.tensor_scalar(ms[:, t:t + 1], ss[:, 2 * t:2 * t + 1], 1.0 / D, EPS, ALU.mult, ALU.add))
                dve.wait_ge(sq_done, 4 * r + 2 * t + 2)
                dve.scalar_tensor_tensor(ms[:, t:t + 1], ss[:, 2 * t + 1:2 * t + 2], 1.0 / D, ms[:, t:t + 1], ALU.mult,
                                         ALU.add).then_inc(ms_done, 1)

            def norm(n, between=None):
                r = rms_turn(n)
                if n in (0, 6):
                    mean(r, 0)
                dve.wait_ge(rstd_done, 2 * r + 1)
                dve.tensor_scalar(xn[:, 0, :], X[:, 0, :], rstd[:, 0:1], None, ALU.mult).then_inc(xn0, 1)
                mean(r, 1)
                dve.wait_ge(rstd_done, 2 * r + 2)
                for half in (slice(0, 512), slice(512, D)):
                    dve.tensor_scalar(xn[:, 1, half], X[:, 1, half], rstd[:, 1:2], None, ALU.mult).then_inc(xn1, 1)
                if between:
                    between()
                q, g0 = TURN[f"n{n}"], G_NORM + 8 * n
                for k in range(KD):
                    dve.wait_ge(xth, 8 * q + 2 * (k // 2) + 2)
                    src = bank[4 + k // 2][:, (k % 2) * S:(k % 2 + 1) * S]
                    hi = xt_hi[:, k, :].bitcast(F32)
                    dve.scalar_tensor_tensor(xt_lo[:, k, :], src, gcol[:, g0 + k:g0 + k + 1], hi,
                                             ALU.mult, ALU.subtract).then_inc(xtl, 1)
                if n:
                    for ahead in (2, 1):
                        split(U[NORM_STAGE[n]] + NSPLIT - ahead)

            def project(u0, blocks, after=None, before=None):
                for c in range(len(blocks)):
                    if before:
                        before(c)
                    split(u0 + c + NSPLIT)
                    if after:
                        after(c)

            def sec_rms(l, c):
                for n, (_, m, o, last) in enumerate(SEC_KINDS):
                    if c == last:
                        dve.wait_ge(e_sq, 6 * l + 2 * n + 2)
                        link(dve.tensor_reduce(head_rms(ss, n), work[:, 0:2 * m * 64].rearrange(
                            "p (t h d) -> p t h d", t=NT, d=64), X_AXIS, ALU.add))
                        dve.tensor_scalar(head_rms(ms, n), head_rms(ss, n), 1.0 / 64, EPS, ALU.mult,
                                          ALU.add).then_inc(e_ms, 1)
                    if c == last + (1 if n < 2 else 0):
                        dve.wait_ge(e_rt, 3 * l + n + 1)
                        r, q = head_rms(rstd, n), head_rms(ss, n)
                        link(dve.reciprocal(r, r))
                        link(dve.tensor_tensor(q, r, r, ALU.mult))
                        link(dve.tensor_tensor(q, q, head_rms(ms, n), ALU.mult))
                        link(dve.tensor_scalar(q, q, -0.5, 1.5, ALU.mult, ALU.add))
                        dve.tensor_tensor(r, r, q, ALU.mult).then_inc(e_rs, 1)
                        dve.wait_ge(e_rs, 3 * l + n + 1)
                if c == SEC_KINDS[2][3] + 1:
                    sec_heads(dve, link, 2, 0, l, QT[:, 2560:3072])
                    dve.sem_inc(ft_ready_d, 1)

            def update_x(scale, first_bank, turn, last_unit):
                for j in range(4):
                    t, half = j // 2, j % 2
                    if j in (0, 2):
                        if j == 2 and turn < 9:
                            mean(turn + (1 if turn < 6 else 2), 0)
                        dve.wait_ge(x_part, 2 * turn + 1 + j // 2)
                    if j == 3:
                        dve.wait_ge(unit_used, last_unit + 1)
                    dst = X[:, t, half * 512:(half + 1) * 512]
                    dve.scalar_tensor_tensor(dst, bank[first_bank + j][:, :], scale, dst, ALU.mult, ALU.add).then_inc(x_upd, 1)

            def mix_out(m):
                u0 = U[f"mix{m}"]
                for c in range(OUT_UNITS - 2):
                    split(u0 + c + NSPLIT)
                update_x(1.0, 0, (1, 4, 6, 8)[m], u0 + OUT_UNITS - 1)

            def triple(f, s, i):
                par = s % 2
                split(ffn_unit(f, "g", s) + NSPLIT, i)
                last = s == STEPS - 1
                if not last:
                    split(ffn_unit(f, "u", s) + NSPLIT, i)
                if f >= 4:
                    l = f - 4
                    for j in range(2):
                        y, g = conv_y[:, par, j * S:(j + 1) * S], bank[2 * par][:, j * S:(j + 1) * S]
                        dve.wait_ge(cv_mid, on(2 * (l * STEPS + s) + 2, 4, i))
                        dve.scalar_tensor_tensor(y[:, 1:S], g[:, 0:S - 1], tap(l, 0, s, j, i), y[:, 1:S], ALU.mult,
                                                 ALU.add).then_inc(cv_left, 1)
                    for j in range(2):
                        y, g = conv_y[:, par, j * S:(j + 1) * S], bank[2 * par][:, j * S:(j + 1) * S]
                        dve.wait_ge(cv_left, on(2 * (l * STEPS + s) + j + 1, 4, i))
                        ins = dve.scalar_tensor_tensor(y[:, 0:S - 1], g[:, 1:S], tap(l, 2, s, j, i), y[:, 0:S - 1],
                                                       ALU.mult, ALU.add)
                    ins.then_inc(cv_done, 1)
                dve.wait_ge(actg_done, on(f * STEPS + s + 1, 2, i))
                dve.wait_ge(unit_used, on(ffn_unit(f, "u", s) + 1, 6, i))
                if f or s:
                    dve.wait_ge(hl_done, on(f * STEPS + s, 2, i))
                dve.tensor_tensor(h_f, act_g[:, par, :], bank[2 * par + 1][:, :], ALU.mult).then_inc(mul_done, 1)
                dve.wait_ge(hh_done, on(f * STEPS + s + 1, 2, i))
                dve.tensor_tensor(h_lo[:, par, :], h_f, h_hi[:, par, :].bitcast(F32), ALU.subtract).then_inc(hl_done, 1)
                if last:
                    split(ffn_unit(f, "u", s) + NSPLIT)
                if s and not last:
                    split(ffn_unit(f, "d", s - 1) + NSPLIT, i)

            def ffn(f):
                ffn_steps(dve, f, triple)
                update_x(0.5 if f < 4 else 1.0, 4, (0, 2, 3, 5, 7, 9)[f], ffn_unit(f, "d", STEPS - 1))

            def feature_major(stage, lo=0, hi=None):
                g0 = FT_A0[stage] + FT_D0[stage]
                for g, (srcs, rows, dst) in list(enumerate(ft_groups(stage)))[lo:hi]:
                    if g % 2 == 0:
                        continue
                    dve.wait_ge(ft_ps, g0 + g + 1)
                    src = bank[ft_bank(stage, g)][0:rows, :].rearrange("p (h s) -> p h s", h=2)
                    dve.tensor_scalar(dst[0], src, ft_scale(stage, g), None, ALU.mult).then_inc(ft_d, 1)

            def attention(stage):
                jobs, j0 = heads[stage], JOB0[stage]

                def maxima(i):
                    if i >= len(jobs):
                        return
                    dve.wait_ge(s_done, j0 + i + 1)
                    b, job = bank[S_BANKS[i % 3]], jobs[i]
                    if "dil" in job:
                        link(dve.tensor_tensor(b[:, :], b[:, :], const("dil"), ALU.add))
                    if job["causal"]:
                        for qt in range(NT):
                            ins = dve.tensor_reduce(negmax[:, i % 4, qt:qt + 1], b[:, qt * S:qt * S + ncols(job, qt)],
                                                    X_AXIS, ALU.max, negate=True)
                    else:
                        ins = dve.tensor_reduce(negmax[:, i % 4, :], b[:, :].rearrange("p (q s) -> p q s", q=2),
                                                X_AXIS, ALU.max, negate=True)
                    ins.then_inc(nm_done, 1)

                def lo_part(pair):
                    if pair is None or stage[:3] == "sec":
                        return
                    place = pair + (4 if stage == "mla" else 0)
                    dve.wait_ge(xth, 8 * TURN["m0" if stage == "mla" else "m1"] + place + 1)
                    dve.tensor_tensor(xt_lo[:, place, :], bank[4 + pair % 2][:, 0:S], xt_hi[:, place, :].bitcast(F32),
                                      ALU.subtract).then_inc(xtl, 1)

                def scale(i):
                    if i >= len(jobs):
                        return
                    dve.wait_ge(exp_done, 2 * (j0 + i + 1))
                    link(dve.reciprocal(rsum[:, i % 4, :], sums[:, i % 4, :]))
                    for qt in range(NT):
                        v = p_of(i % 2, qt, 0, ncols(jobs[i], qt))
                        if stage == "nsa":
                            c = 3 * jobs[i]["q"] + 1 + i % 2
                            ins = dve.tensor_scalar(v, v, rsum[:, i % 4, qt:qt + 1], gate[:, qt, c:c + 1], ALU.mult,
                                                    ALU.mult)
                        else:
                            ins = dve.tensor_scalar(v, v, rsum[:, i % 4, qt:qt + 1], None, ALU.mult)
                    ins.then_inc(p_scaled, 1)

                maxima(0)
                maxima(1)
                scale(0)
                for i in range(len(jobs)):
                    maxima(i + 2)
                    scale(i + 1)
                    lo_part(pair_after(stage, i, 2))
                    if stage[:3] == "sec" and i == 10:
                        kind_mean(int(stage[3]), 0)
                for pair in late_pairs(stage, 2):
                    lo_part(pair)

            def hybrid_step(c):
                if c == 2:
                    dve.wait_ge(pj_evac, 1)
                    dve.memset(gla_aT[0:32, :], 1.0).then_inc(g_evd, 1)
                    dve.memset(gla_qz, 0.0).then_inc(g_evd, 1)
                if c == 3:
                    dve.wait_ge(g_tp, 2)
                    dve.tensor_copy(gla_k, bank[5][:, :]).then_inc(g_evd, 1)
                if c == 4:
                    dve.wait_ge(mla_sq, 4)
                    link(mean_squares(8, 2, 1.0 / 256))
                    mean_squares(10, 2, 1.0 / 128).then_inc(mla_ms, 1)
                if c == 5:
                    dve.wait_ge(mla_rs, 1)
                    for n, (col, w) in enumerate(((HY_CQ, 256), (HY_CKV, 128))):
                        for t in range(NT):
                            v = proj[:, t, col:col + w]
                            dve.tensor_scalar(v, v, rstd[:, 8 + 2 * n + t:9 + 2 * n + t], None, ALU.mult).then_inc(mla_cn, 1)
                    dve.wait_ge(g_ln, 1)
                    dve.scalar_tensor_tensor(gla_la, bank[7][:, :], 0.0, gla_ln, ALU.min, ALU.subtract).then_inc(g_la, 1)
                if c == 6:
                    for k in range(3):
                        dve.wait_ge(mla_ch, 2 if k < 2 else 3)
                        src = bank[4][:, k * S:(k + 1) * S] if k < 2 else bank[5][:, 0:S]
                        dve.scalar_tensor_tensor(ct_lo[:, k, :], src, gcol[:, G_Q + k:G_Q + k + 1],
                                                 ct_hi[:, k, :].bitcast(F32), ALU.mult, ALU.subtract).then_inc(mla_cl, 1)
                    dve.wait_ge(g_bt, 1)
                    b4 = chunks(gla_b)
                    last = b4[:, :, :, 63:64].to_broadcast([P, 2, 4, 64])
                    dve.tensor_tensor(chunks(gla_d), b4, last, ALU.subtract).then_inc(g_d, 1)
                    dve.wait_ge(g_e, 3)
                    dve.tensor_tensor(gla_qi, gla_q, gla_ei, ALU.mult).then_inc(g_qk, 1)
                    dve.tensor_tensor(gla_kd, gla_k, gla_ed, ALU.mult).then_inc(g_qk, 1)
                    qz = gla_qz.rearrange("p (a c i) -> p a c i", a=2, c=4)
                    for half in range(2):
                        dst = qz[:, :, half:4:2, half * 64:half * 64 + 64]
                        ins = dve.tensor_tensor(dst, chunks(gla_q)[:, :, half:4:2, :], chunks(gla_eb)[:, :, half:4:2, :],
                                                ALU.mult)
                    ins.then_inc(g_qk, 1)
                if c == 7:
                    dve.wait_ge(g_a, 1)
                    tri = const("block_tri").unsqueeze(1).to_broadcast([P, 4, P])
                    for e in range(2):
                        ins = dve.tensor_tensor(gla_am[:, e * 512:(e + 1) * 512].rearrange("p (h i) -> p h i", h=4),
                                                bank[4 + e][:, :].rearrange("p (h i) -> p h i", h=4), tri, ALU.mult)
                    ins.then_inc(g_am, 1)

            def kind_mean(l, kind):
                dve.wait_ge(o_sum, 8 * l + (3, 6, 8)[kind])
                dst = o_rs[:, kind * S:(kind + 1) * S]
                link(dve.tensor_scalar(dst, bank[7 if kind < 2 else 6][:, 0:S], 1.0 / (384, 384, 256)[kind], EPS,
                                       ALU.mult, ALU.add))
                dve.reciprocal(dst, dst).then_inc(e_m, 1)

            def nsa_step(c):
                p0 = PROJ0["nsa"]
                if c == 1:
                    dve.wait_ge(pj_evac, p0 + 1)
                    for t in range(NT):
                        src = proj[:, t, NS_KC:NS_KC + 256].rearrange("p (g d) -> p g d", g=4)
                        for e in range(2):
                            ins = dve.tensor_copy(dup[:, 0, t, :, e, :], src)
                    ins.then_inc(c_dup, 1)
                if c == 3:
                    for m, mt in enumerate((m_k, m_v)):
                        if m == 1:
                            dve.wait_ge(c_tp, 4)
                        link(dve.memset(mt[:, 4, :], 0.0))
                        link(dve.tensor_copy(mt[:, 4, 0:32:2], posr[:, m, :]))
                        for gp in range(2):
                            dve.wait_ge(c_tp, 2 * m + gp + 1)
                            src = bank[4 + 2 * m + gp][:, :].rearrange("p (g s) -> p g s", g=2)
                            dve.tensor_copy(mt[0:64, 2 * gp:2 * gp + 2, :], src[0:64, :, :]).then_inc(c_m, 1)
                            dve.tensor_copy(mt[64:128, 2 * gp:2 * gp + 2, 0:S - 1], src[64:128, :, 1:S]).then_inc(c_m, 1)
                if c == 5:
                    for m in range(2):
                        dve.wait_ge(c_h, m + 1)
                        dve.memset(hid[m], 0.0)
                        dve.tensor_copy(small[:, 0, m:m + 1], bank[4 + m][:, 60:61]).then_inc(c_b, 1)
                if c == 6:
                    dve.wait_ge(c_kc, 1)
                    link(dve.tensor_copy(kc_tok, bank[6][:, 0:64]))
                    link(dve.memset(vcz, 0.0))
                    for g in range(NS_GR):
                        dve.tensor_copy(vcz[32 * g:32 * g + 32, g, :], bank[6][32 * g:32 * g + 32, 64:128])
                    rope_heads(dve, link, kc_tok.rearrange("p (h d) -> p h d", h=1), 0, 32, rcos[:, 2, 16:48],
                               rsin[:, 2, 16:48], rope_t)
                    dve.sem_inc(c_kr, 1)
                if c == 7:
                    dve.wait_ge(c_kt, 1)
                    dve.tensor_copy(kcT_[0:64, :], bank[6][0:64, 0:P]).then_inc(c_kcT, 1)
                    feature_major("nsa", 0, 8)
                if c == 8:
                    compressed_scores()
                if c == 9:
                    compressed_probabilities()
                if c == 10:
                    feature_major("nsa", 8)
                    dve.wait_ge(c_pt, 1)
                    for t in range(NT):
                        ins = dve.tensor_copy(pct[:, t * 512:(t + 1) * 512], bank[6 + t][:, :])
                    ins.then_inc(c_pe, 1)

            def nsa_rotate(c):
                b = c - 1 if c < 7 else c
                if b in (2, 3, 4, 5, 7, 8):
                    dve.wait_ge(pj_evac, PROJ0["nsa"] + b + 1)
                    at = sum(NSA_BLOCKS[:b])
                    rope_heads(dve, link, proj[:, 0, at:at + 256].rearrange("p (h d) -> p h d", h=4), 0, 32,
                               rcos[:, 0, 16:48], rsin[:, 0, 16:48], rope_t)
                    if b in (5, 8):
                        dve.sem_inc(ft_ready_d, 1)

            def compressed_scores():
                dve.wait_ge(c_s, 1)
                s4 = sc.rearrange("p (t h n) -> p t h n", t=2, n=32)
                add = const("cmp_add").rearrange("p (t n) -> p t n", t=2)
                for t in range(NT):
                    link(dve.tensor_tensor(s4[:, t], bank[6 + t][:, :].rearrange("p (h n) -> p h n", n=32),
                                           add[:, t, :].unsqueeze(1).to_broadcast([P, 16, 32]), ALU.add))
                link(dve.tensor_reduce(small[:, 1, :], sc.rearrange("p (h n) -> p h n", n=32), X_AXIS, ALU.max))
                s3 = sc.rearrange("p (h n) -> p h n", n=32)
                dve.tensor_tensor(s3, s3, small[:, 1, :].unsqueeze(2).to_broadcast([P, 32, 32]), ALU.subtract)\
                   .then_inc(c_sc, 1)

            def compressed_probabilities():
                dve.wait_ge(c_e, 1)
                p4 = pc.rearrange("p (t h n) -> p t h n", t=2, n=32)
                keep = const("cmp_01").rearrange("p (t n) -> p t n", t=2)
                for t in range(NT):
                    link(dve.tensor_tensor(p4[:, t], p4[:, t], keep[:, t, :].unsqueeze(1).to_broadcast([P, 16, 32]),
                                           ALU.mult))
                dve.tensor_reduce(small[:, 2, :], pc.rearrange("p (h n) -> p h n", n=32), X_AXIS,
                                  ALU.add).then_inc(c_p, 1)
                dve.wait_ge(c_p, 1)
                link(dve.tensor_scalar(small[:, 2, :], small[:, 2, :], TINY, None, ALU.max))
                link(dve.reciprocal(small[:, 3, :], small[:, 2, :]))
                dve.wait_ge(c_gate, 1)
                for t in range(NT):
                    coef = small[:, 1, t * 16:(t + 1) * 16].rearrange("p (j g) -> p j g", j=4)
                    inv = small[:, 3, t * 16:(t + 1) * 16].rearrange("p (j g) -> p j g", j=4)
                    gt = gate[:, t, :].rearrange("p (g j b) -> p j g b", g=4, b=3)[:, :, :, 0]
                    link(dve.tensor_tensor(coef, inv, gt, ALU.mult))
                pc3 = pc.rearrange("p (h n) -> p h n", n=32)
                dve.tensor_tensor(pc3, pc3, small[:, 1, :].unsqueeze(2).to_broadcast([P, 32, 32]),
                                  ALU.mult).then_inc(c_p, 1)

            dve.wait_ge(cst_in, 16)
            dve.tensor_copy(ident_b[:, :], ident)
            dve.tensor_copy(causal_b[:, :], const("causal")).then_inc(const_ready, 1)
            norm(0, lambda: split(0))
            for u in range(1, NSPLIT):
                split(u)
            dve.wait_ge(par_in, 16 * N_PAR)
            link(dve.tensor_scalar(head_gain[:, :, 0:3, :], head_gain[:, :, 0:3, :], 0.125, None, ALU.mult))
            link(dve.tensor_copy(pos_f[:, :], pos_i[:, :]))
            fr = const("freq")
            for j in range(3):
                link(dve.tensor_scalar(ang[:, j, :], fr, pos_f[:, j:j + 1], None, ALU.mult))
            TWO_PI = 2 * np.pi
            C1 = 6.28125
            C2 = float(np.float32(np.round((TWO_PI - C1) * 2 ** 20) / 2 ** 20))
            C3 = float(np.float32(TWO_PI - C1 - C2))
            MAGIC = 1.5 * 2 ** 23

            def reduced(dst, shift):
                k = rsin[:, :, :]
                link(dve.tensor_scalar(k, ang[:, :, :], float(1 / TWO_PI), 0.25 * shift, ALU.mult, ALU.add))
                link(dve.tensor_scalar(k, k, MAGIC, MAGIC, ALU.add, ALU.subtract))
                link(dve.scalar_tensor_tensor(dst, k, -C1, ang[:, :, :], ALU.mult, ALU.add))
                link(dve.scalar_tensor_tensor(dst, k, -C2, dst, ALU.mult, ALU.add))
                link(dve.scalar_tensor_tensor(dst, k, -C3, dst, ALU.mult, ALU.add))
                if shift:
                    link(dve.tensor_scalar(dst, dst, float(np.pi / 2), None, ALU.add))
                link(dve.tensor_scalar(dst, dst, 3.1415925, -3.1415925, ALU.min, ALU.max))

            reduced(tmp48[:, :, :], 1)
            reduced(red[:, :, :], 0)
            dve.sem_inc(rope_arg, 1)
            ffn(0)
            norm(1)
            project(U["hy_in"], HY_BLOCKS, None, hybrid_step)
            st = gla_st.rearrange("p (a c v) -> p a c v", a=2, c=4)
            eb = chunks(gla_eb)
            for c in range(3):
                dve.wait_ge(g_kv, c + 1)
                if c:
                    dve.wait_ge(g_st, c)
                for a in range(2):
                    for hh in range(2):
                        r = slice(64 * hh, 64 * hh + 64)
                        kv = bank[GLA_KV_BANKS[c]][r, a * 256 + hh * P:a * 256 + (hh + 1) * P]
                        if c == 0:
                            ins = dve.tensor_copy(st[r, a, 1, :], kv)
                        else:
                            ins = dve.scalar_tensor_tensor(st[r, a, c + 1, :], st[r, a, c, :], eb[r, a, c, 63:64], kv,
                                                           ALU.mult, ALU.add)
                ins.then_inc(g_st, 1)
            dve.wait_ge(g_sr, 1)
            sr8 = gla_sr.rearrange("p (h d) -> p h d", d=P)
            link(dve.tensor_tensor(sr8, sr8, gla_row[:, :].unsqueeze(1).to_broadcast([P, 8, P]), ALU.mult))
            dve.wait_ge(g_sq, 8)
            mean_squares(16, 8, 1.0 / GLA_DV).then_inc(g_ms, 1)
            dve.wait_ge(g_rs, 1)
            for t in range(NT):
                for h in range(GLA_H):
                    src = bank[(7, 4)[h % 2]][:, (2 * t + h // 2) * P:(2 * t + h // 2 + 1) * P]
                    n = 4 * t + h
                    ins = dve.scalar_tensor_tensor(O[:, t, 512 + h * P:512 + (h + 1) * P], src, rstd[:, 16 + n:17 + n],
                                                   gla_sr[:, n * P:(n + 1) * P], ALU.mult, ALU.mult)
            ins.then_inc(mla_up, 1)
            split(U["uq"] + NSPLIT)
            dve.wait_ge(mla_q, 2)
            v = prob[:, 0:768].rearrange("p (h d) -> p h d", h=MLA_H)
            rope_heads(dve, link, v, MLA_NOPE, 16, rcos[:, 0, 0:16], rsin[:, 0, 0:16], QT[:, 2048:2560])
            dve.sem_inc(ft_ready_d, 1)
            split(U["ukv"] + NSPLIT)
            for k in range(4):
                dve.wait_ge(xth, 8 * TURN["m0"] + 2 * (k // 2) + 2)
                dve.tensor_tensor(xt_lo[:, k, :], bank[4 + k // 2][:, (k % 2) * S:(k % 2 + 1) * S],
                                  xt_hi[:, k, :].bitcast(F32), ALU.subtract).then_inc(xtl, 1)
            feature_major("mla")
            attention("mla")
            mix_out(0)
            norm(2)
            ffn(1)
            norm(3)
            ffn(2)
            norm(4)
            project(U["nsa_in"], NSA_BLOCKS, nsa_rotate, nsa_step)
            attention("nsa")
            mix_out(1)
            norm(5)
            ffn(3)
            dve.wait_ge(f_in, 16)
            frow = O[:, 0, :]
            for t in range(NT):
                if t == 1:
                    mean(6, 1)
                dve.wait_ge(rstd_done, 2 * 6 + t + 1)
                dve.scalar_tensor_tensor(X[:, t, :], X[:, t, :], rstd[:, t:t + 1], frow, ALU.mult,
                                         ALU.mult).then_inc(x_upd, 2)
            for l in range(2):
                norm(6 + 2 * l)
                project(U[f"sec_in{l}"], SEC_BLOCKS, lambda c: sec_rms(l, c))
                feature_major(f"sec{l}")
                attention(f"sec{l}")
                kind_mean(l, 1)

                def scale(place):
                    g = G_OUT + 8 * l + out_tile(2, place)
                    kind = kind_of(place)
                    dve.wait_ge(e_mr, 2 * l + (1 if kind < 2 else 2))
                    dve.scalar_tensor_tensor(o_t[:, place, :], o_t[:, place, :], gcol[:, g:g + 1],
                                             o_rs[:, kind * S:(kind + 1) * S], ALU.mult, ALU.mult).then_inc(o_scaled, 1)

                scale(0)
                for place in range(KD):
                    if place == 2:
                        kind_mean(l, 2)
                    if place + 1 < KD:
                        scale(place + 1)
                    dve.wait_ge(xth, 8 * TURN[f"m{2 + l}"] + place + 1)
                    dve.tensor_tensor(xt_lo[:, place, :], o_t[:, place, :], xt_hi[:, place, :].bitcast(F32),
                                      ALU.subtract).then_inc(xtl, 1)
                mix_out(2 + l)
                norm(7 + 2 * l)
                ffn(4 + l)

        @block.gpsimd
        def _(pool):
            own = [0]

            def link(ins):
                own[0] += 1
                ins.then_inc(pool_own, 1)
                pool.wait_ge(pool_own, own[0])

            def inv_sqrt(lo, n):
                return pool.tensor_tensor(rstd[:, lo:lo + n], ms[:, lo:lo + n], neg_half[:, lo:lo + n], ALU.pow)

            def norm(r):
                for t in range(NT):
                    pool.wait_ge(ms_done, 2 * r + t + 1)
                    inv_sqrt(t, 1).then_inc(rstd_done, 1)

            def fetch_bias(l):
                for r2 in range(2):
                    for qt in range(NT):
                        for h in range(4):
                            at = rpb2[l, h, 7 - (2 * qt + r2), 15:16]
                            src = bass.AP(tensor=at.tensor, offset=at.offset - (GRID - 1), ap=[[1, 64], [31, 4], [1, 64]])
                            pool.dma_start(na_bias[64 * r2:64 * r2 + 64, qt, h, :], src).then_inc(b_in, 16)

            def mask_bias(l):
                pool.wait_ge(b_in, 256 * (l + 1))
                v = work[:, 2048:4096].rearrange("p (n c) -> p n c", c=64)
                m = const("na_mask").unsqueeze(1).to_broadcast([P, 32, 64])
                pool.tensor_tensor(v, v, m, ALU.add).then_inc(na_ready, 1)

            link(pool.memset(neg_half[:, :], -0.5))
            norm(0)
            norm(1)
            pool.wait_ge(pj_evac, 3)
            pool.wait_ge(rope_tab, 2)
            for t in range(NT):
                v = proj[:, t, HY_KR:HY_KR + 32].rearrange("p (h d) -> p h d", h=1)
                rope_heads(pool, link, v, 0, 16, rcos[:, t, 0:16], rsin[:, t, 0:16], small[:, 2, :])
            pool.wait_ge(mla_ms, 1)
            inv_sqrt(8, 4).then_inc(mla_rs, 1)
            pool.wait_ge(g_ms, 1)
            inv_sqrt(16, 8).then_inc(g_rs, 1)
            pool.wait_ge(mla_q, 4)
            v = prob[:, 768:1536].rearrange("p (h d) -> p h d", h=MLA_H)
            rope_heads(pool, link, v, MLA_NOPE, 16, rcos[:, 1, 0:16], rsin[:, 1, 0:16], QT[:, 2560:3072])
            pool.sem_inc(ft_ready_p, 1)
            for r in (2, 3, 4):
                norm(r)
                if r == 2:
                    for m, dst in enumerate((prob[:, :], O[:, :, :].rearrange("p t d -> p (t d)"))):
                        pool.dma_start(dst, cmp_w1[m]).then_inc(c_w, 16)
            p0 = PROJ0["nsa"]
            pool.wait_ge(pj_evac, p0 + 2)
            for t in range(NT):
                src = proj[:, t, NS_VC:NS_VC + 256].rearrange("p (g d) -> p g d", g=4)
                for e in range(2):
                    ins = pool.tensor_copy(dup[:, 1, t, :, e, :], src)
            ins.then_inc(c_dup, 1)
            for b in (2, 3, 4, 5, 7, 8):
                pool.wait_ge(pj_evac, p0 + b + 1)
                at = sum(NSA_BLOCKS[:b])
                rope_heads(pool, link, proj[:, 1, at:at + 256].rearrange("p (h d) -> p h d", h=4), 0, 32,
                           rcos[:, 1, 16:48], rsin[:, 1, 16:48], rope_p)
                if b in (5, 8):
                    pool.sem_inc(ft_ready_p, 1)
            norm(5)
            pool.dma_start(O[:, 0, :], final_gain.partition_broadcast(P)).then_inc(f_in, 16)
            norm(6)
            for l in range(2):
                norm(7 + 2 * l)
                fetch_bias(l)
                for n in range(3):
                    pool.wait_ge(e_rs, 3 * l + n + 1)
                    for t in ((0, 1) if n < 2 else (1,)):
                        sec_heads(pool, link, n, t, l, QT[:, 3072:4096])
                    pool.sem_inc(ft_ready_p, 1)
                mask_bias(l)
                norm(8 + 2 * l)


def _stream(a):
    s = np.zeros((N_UNITS, P, UNIT), np.float32)

    def columns(u, w, c0, n):
        k = w.shape[0] // P
        s[u].reshape(P, k, UNIT // k)[:, :, 0:n] = w[:, c0:c0 + n].reshape(k, P, n).transpose(1, 0, 2)

    def rows(u, w, r0):
        s[u].reshape(P, 2, D)[:] = w[r0:r0 + 2 * P].reshape(2, P, D).transpose(1, 0, 2)

    def ffn(f, gate, up, down):
        u0 = U[f"ffn{f}"]
        for t in range(STEPS):
            g = u0 + max(3 * t - 1, 0)
            columns(g, gate, 256 * t, 256)
            columns(g + 1, up, 256 * t, 256)
            rows(u0 + (FFN_UNITS - 1 if t == STEPS - 1 else 3 * t + 4), down, 256 * t)

    def project(u0, w, blocks):
        for c, n in enumerate(blocks):
            columns(u0 + c, w, sum(blocks[:c]), n)

    def reorder(w, widths, order):
        at = dict(zip(widths, np.cumsum([0] + list(widths.values()))))
        return w[:, np.concatenate([at[m] + np.arange(widths[m]) for m in order])]

    for f in range(4):
        ffn(f, *(a[n][f // 2, f % 2] for n in ("ffn_w_gate", "ffn_w_up", "ffn_w_down")))
    for l in range(2):
        gu = a["w_gate_up_2"][l]
        ffn(4 + l, gu[:, :D_FF], gu[:, D_FF:], a["w_down_2"][l])
        project(U[f"sec_in{l}"], reorder(a["w_in_2"][l], SEC_W, SEC_ORDER), SEC_BLOCKS)
    project(U["hy_in"], reorder(a["hy_w_in"][0], HY_W, HY_ORDER), HY_BLOCKS)
    project(U["nsa_in"], reorder(a["nsa_w_in"][0], NS_W, NS_ORDER), NSA_BLOCKS)
    s[U["uq"]][:, 0:1536] = a["mla_w_uq"][0].reshape(2, P, 768).transpose(1, 0, 2).reshape(P, 1536)
    s[U["ukv"]][:, 0:1024] = a["mla_w_ukv"][0]
    for m, w in enumerate((a["hy_w_out"][0], a["nsa_w_out"][0], a["w_out_2"][0], a["w_out_2"][1])):
        w = np.concatenate([w[out_tile(m, k) * P:(out_tile(m, k) + 1) * P] for k in range(KD)])
        for c in range(OUT_UNITS):
            rows(U[f"mix{m}"] + c, w, 256 * c)
    return s


def _lay_out(a):
    def cols(v):
        return np.ascontiguousarray(v.reshape(-1, P).T)

    norms = [a["ffn_norm"][0, 0], a["mix_norm"][0], a["ffn_norm"][0, 1], a["ffn_norm"][1, 0], a["mix_norm"][1],
             a["ffn_norm"][1, 1], a["norm1_g_2"][0], a["norm2_g_2"][0], a["norm1_g_2"][1], a["norm2_g_2"][1]]
    gains = np.concatenate([cols(np.stack(norms)), cols(a["out_norm_g_2"]), cols(a["mla_q_norm"]),
                            cols(a["mla_kv_norm"])], 1)
    conv = np.concatenate([a["conv_w_2"], a["conv_b_2"][:, None]], 1).reshape(2, 4, D_FF // P, P).transpose(3, 0, 1, 2)
    pos = a["positions"][0]
    places = np.zeros((P, 3), pos.dtype)
    places[:, 0], places[:, 1] = pos[:P], pos[P:]
    for g in range(NS_GR):
        places[32 * g:32 * g + NCMP, 2] = pos[CMP_LEN - 1::CMP_STRIDE][:NCMP]
    rows = np.stack([a[n][0].reshape(16, P).T for n in ("nsa_pos_k", "nsa_pos_v")], 1)
    w1 = np.stack([a[n][0].reshape(16, P, P).transpose(1, 0, 2).reshape(P, 2048) for n in ("nsa_ck_w1", "nsa_cv_w1")])
    w2 = np.stack([a["nsa_ck_w2"][0], a["nsa_cv_w2"][0]])
    return {"stream": _stream(a), "consts": shape_constants(), "gains": gains, "conv": conv, "x": a["x"],
            "positions": places, "pos_rows": rows, "cmp_w1": w1, "cmp_w2": w2, "final_gain": a["final_norm"],
            "gla_gain": a["gla_out_norm"], "gla_a2": a["gla_w_a2"], "gla_ba": a["gla_b_a"],
            "q_gain2": a["q_norm_g_2"], "k_gain2": a["k_norm_g_2"], "rpb2": a["rpb_2"]}


def kernel(**inputs):
    import concourse.bacc as _bacc
    from concourse.bass_utils import run_bass_kernel_spmd as _run

    nc = _bacc.Bacc("TRN2", target_bir_lowering=False, num_devices=1)
    arrays, args = {}, []
    for name, v in _lay_out({k: np.asarray(v) for k, v in inputs.items()}).items():
        v = np.ascontiguousarray(v)
        arrays[f"in_{name}"] = v
        args.append(nc.dram_tensor(f"in_{name}", v.shape, mybir.dt.from_np(v.dtype), kind="ExternalInput").ap())
    args.append(nc.dram_tensor("out_0", (1, S, D), F32, kind="ExternalOutput").ap())
    build(nc, *args)
    r = _run(nc, [arrays], core_ids=[0])
    return r.results[0]["out_0"]
```
